# Optimizing a Trainium2 kernel written in Bass

```python
import math
import jax, jax.numpy as jnp
from jax import lax
import numpy as np

D_MODEL = 1024
BATCH = 1
SEQ = 1024
DEPTH = 1
DEC_BATCH = 8
DEC_SEQ = 8
PAST_LEN = 1024
PAGE_SIZE = 128

HEAD_DIM = 64
SSD_HEADS = 8
SSD_WIDTH = SSD_HEADS * HEAD_DIM
SSD_GROUPS = 2
SSD_HPG = SSD_HEADS // SSD_GROUPS
D_STATE = 128
CONV_WIDTH = 4
CONV_CH = SSD_WIDTH + 2 * SSD_GROUPS * D_STATE
SSD_CHUNK = 256
DT_MIN = 0.001
DT_MAX = 0.1
ATT_HEADS = 8
ATT_WIDTH = ATT_HEADS * HEAD_DIM
KV_HEADS = 2
GQA_GROUP = ATT_HEADS // KV_HEADS
KV_WIDTH = KV_HEADS * HEAD_DIM
CMP_BLOCK = 32
SEL_BLOCK = 64
TOP_N = 16
N_LOCAL_BLOCKS = 2
WINDOW = 512
QUERY_BLOCK = 128
N_BRANCH = 3
ROT_DIM = HEAD_DIM // 4
ROPE_THETA = 500000.0
MIX_WIDTH = SSD_WIDTH + ATT_WIDTH
COL_SIZES = (SSD_WIDTH, CONV_CH, SSD_HEADS, ATT_WIDTH, 2 * KV_WIDTH, 2 * KV_WIDTH, 2 * KV_WIDTH, N_BRANCH * ATT_HEADS, ATT_WIDTH)
IN_COLS = SSD_WIDTH + CONV_CH + SSD_HEADS + ATT_WIDTH + 6 * KV_WIDTH + N_BRANCH * ATT_HEADS + ATT_WIDTH
EPS = 1e-6

kernel_name = 'hybrid_ssd_nsa_adaln_step'

def rms_norm(x, g):
    xf = x.astype(jnp.float32)
    y = xf * lax.rsqrt(jnp.mean(xf * xf, axis=-1, keepdims=True) + EPS)
    return y.astype(x.dtype) * g

def rope(x, pos):
    half = ROT_DIM // 2
    inv_freq = ROPE_THETA ** (-jnp.arange(half, dtype=jnp.float32) * 2.0 / ROT_DIM)
    ang = pos.astype(jnp.float32)[:, None] * inv_freq[None, :]
    cos = jnp.cos(ang)[None, :, None, :].astype(x.dtype)
    sin = jnp.sin(ang)[None, :, None, :].astype(x.dtype)
    x1 = x[..., :half]
    x2 = x[..., half:ROT_DIM]
    return jnp.concatenate([x1 * cos - x2 * sin, x2 * cos + x1 * sin, x[..., ROT_DIM:]], axis=-1)

def masked_softmax(s, mask):
    s = jnp.where(mask, s, -jnp.inf)
    m = jnp.max(s, axis=-1, keepdims=True)
    m = jnp.where(jnp.isfinite(m), m, 0.0)
    e = jnp.exp(s - m)
    d = jnp.sum(e, axis=-1, keepdims=True)
    return e / jnp.where(d > 0, d, 1.0)

def split_cols(u):
    out, o = [], 0
    for n in COL_SIZES:
        out.append(u[..., o:o + n])
        o += n
    return out

def kv_rows(u, pos):
    B, T = u.shape[:2]
    k = rope(u[..., :KV_WIDTH].reshape(B, T, KV_HEADS, HEAD_DIM), pos)
    v = u[..., KV_WIDTH:].reshape(B, T, KV_HEADS, HEAD_DIM)
    return jnp.stack([k, v], axis=2)

def block_means(rows):
    B, L = rows.shape[:2]
    r = rows.reshape(B, L // CMP_BLOCK, CMP_BLOCK, 2, KV_HEADS, HEAD_DIM)
    return jnp.mean(r.astype(jnp.float32), axis=2).astype(rows.dtype)

def nsa_attend(q, q_pos, kv_c, kv_s, kv_w, kw_pos):
    B, Tq = q.shape[:2]
    NC, NS = kv_c.shape[1], kv_s.shape[1]
    scale = HEAD_DIM ** -0.5
    qg = q.reshape(B, Tq, KV_HEADS, GQA_GROUP, HEAD_DIM)
    sc = jnp.einsum('bqkgd,bckd->bqkgc', qg, kv_c[:, :, 0]).astype(jnp.float32) * scale
    c_end = (jnp.arange(NC) + 1) * CMP_BLOCK - 1
    mc = (c_end[None, :] <= q_pos[:, None])[None, :, None, None, :]
    pc = masked_softmax(sc, mc)
    o_c = jnp.einsum('bqkgc,bckd->bqkgd', pc.astype(q.dtype), kv_c[:, :, 1])
    imp = jnp.sum(pc, axis=3).reshape(B, Tq, KV_HEADS, NS, SEL_BLOCK // CMP_BLOCK).sum(-1)
    blk = jnp.arange(NS)[None, :]
    cur = q_pos[:, None] // SEL_BLOCK
    valid = blk <= cur
    forced = (blk == 0) | ((cur - blk >= 0) & (cur - blk < N_LOCAL_BLOCKS))
    score = jnp.where(forced[None, :, None, :], jnp.inf, imp)
    score = jnp.where(valid[None, :, None, :], score, -jnp.inf)
    n_sel = min(TOP_N, NS)
    top_v, top_i = lax.top_k(score, n_sel)
    b_idx = jnp.arange(B)[:, None, None, None]
    h_idx = jnp.arange(KV_HEADS)[None, None, :, None]
    g = kv_s[b_idx, top_i, :, :, h_idx, :]
    ss = jnp.einsum('bqkgd,bqknsd->bqkgns', qg, g[..., 0, :]).astype(jnp.float32) * scale
    tok = top_i[..., None] * SEL_BLOCK + jnp.arange(SEL_BLOCK)
    ms = (top_v > -jnp.inf)[..., None] & (tok <= q_pos[None, :, None, None, None])
    ps = masked_softmax(ss.reshape(B, Tq, KV_HEADS, GQA_GROUP, n_sel * SEL_BLOCK),
                        ms.reshape(B, Tq, KV_HEADS, 1, n_sel * SEL_BLOCK)).reshape(ss.shape)
    o_s = jnp.einsum('bqkgns,bqknsd->bqkgd', ps.astype(q.dtype), g[..., 1, :])
    sw = jnp.einsum('bqkgd,blkd->bqkgl', qg, kv_w[:, :, 0]).astype(jnp.float32) * scale
    dist = q_pos[:, None] - kw_pos[None, :]
    mw = ((dist >= 0) & (dist <= WINDOW) & (kw_pos[None, :] >= 0))[None, :, None, None, :]
    pw = masked_softmax(sw, mw)
    o_w = jnp.einsum('bqkgl,blkd->bqkgd', pw.astype(q.dtype), kv_w[:, :, 1])
    shp = (B, Tq, ATT_HEADS, HEAD_DIM)
    return jnp.stack([o_c.reshape(shp), o_s.reshape(shp), o_w.reshape(shp)], axis=2)

def nsa_prompt(q, kv_c_rows, kv_s_rows, kv_w_rows):
    B, T = q.shape[:2]
    kv_c = block_means(kv_c_rows)
    kv_s = kv_s_rows.reshape(B, T // SEL_BLOCK, SEL_BLOCK, 2, KV_HEADS, HEAD_DIM)
    kv_w_pad = jnp.pad(kv_w_rows, ((0, 0), (WINDOW, 0), (0, 0), (0, 0), (0, 0)))
    qb = min(QUERY_BLOCK, T)

    def one_block(i):
        s0 = i * qb
        q_blk = lax.dynamic_slice_in_dim(q, s0, qb, axis=1)
        q_pos = s0 + jnp.arange(qb)
        kw = lax.dynamic_slice_in_dim(kv_w_pad, s0, qb + WINDOW, axis=1)
        kw_pos = s0 - WINDOW + jnp.arange(qb + WINDOW)
        return nsa_attend(q_blk, q_pos, kv_c, kv_s, kw, kw_pos)

    o = lax.map(one_block, jnp.arange(T // qb))
    return jnp.moveaxis(o, 0, 1).reshape(B, T, N_BRANCH, ATT_HEADS, HEAD_DIM)

def nsa_sample(q, new_c, new_s, new_w, pool_c, pool_s, win_buf, page_table):
    B, Tn = q.shape[:2]
    P = page_table.shape[1] * PAGE_SIZE
    L = P + Tn
    pad = -(-L // SEL_BLOCK) * SEL_BLOCK - L
    padw = ((0, 0), (0, pad), (0, 0), (0, 0), (0, 0))
    past_c = pool_c[page_table].reshape(B, P, 2, KV_HEADS, HEAD_DIM)
    kv_c = jnp.concatenate([block_means(past_c), block_means(jnp.pad(new_c, padw))], axis=1)
    past_s = pool_s[page_table].reshape(B, P // SEL_BLOCK, SEL_BLOCK, 2, KV_HEADS, HEAD_DIM)
    new_sb = jnp.pad(new_s, padw).reshape(B, (Tn + pad) // SEL_BLOCK, SEL_BLOCK, 2, KV_HEADS, HEAD_DIM)
    kv_s = jnp.concatenate([past_s, new_sb], axis=1)
    wb = win_buf.shape[1]
    kv_w = jnp.concatenate([win_buf.astype(new_w.dtype), new_w], axis=1)
    kw_pos = P - wb + jnp.arange(wb + Tn)
    q_pos = P + jnp.arange(Tn)
    o = nsa_attend(q, q_pos, kv_c, kv_s, kv_w, kw_pos)
    new_win = kv_w[:, kv_w.shape[1] - min(WINDOW, L):]
    return o, new_win

def ssd_scan(x, dt, a, bm, cm, h0):
    f32 = jnp.float32
    B, T = x.shape[:2]
    L = min(SSD_CHUNK, T)
    Tp = -(-T // L) * L
    nc = Tp // L

    def padt(t):
        return jnp.pad(t, [(0, 0), (0, Tp - T)] + [(0, 0)] * (t.ndim - 2))

    x = padt(x.astype(f32)).reshape(B, nc, L, SSD_GROUPS, SSD_HPG, HEAD_DIM)
    dt = padt(dt).reshape(B, nc, L, SSD_GROUPS, SSD_HPG)
    bm = padt(bm.astype(f32)).reshape(B, nc, L, SSD_GROUPS, D_STATE)
    cm = padt(cm.astype(f32)).reshape(B, nc, L, SSD_GROUPS, D_STATE)
    la = jnp.cumsum(dt * a, axis=2)
    xdt = x * dt[..., None]
    causal = jnp.tril(jnp.ones((L, L), bool))[None, None, :, :, None, None]
    seg = la[:, :, :, None] - la[:, :, None, :]
    decay = jnp.where(causal, jnp.exp(jnp.where(causal, seg, 0.0)), 0.0)
    cb = jnp.einsum('bclgn,bcsgn->bclsg', cm, bm)
    y_diag = jnp.einsum('bclsg,bclsgr,bcsgrp->bclgrp', cb, decay, xdt)
    to_end = jnp.exp(la[:, :, -1:] - la)
    states = jnp.einsum('bclgn,bclgr,bclgrp->bcgrpn', bm, to_end, xdt)
    chunk_decay = jnp.exp(la[:, :, -1])

    def step(h, inp):
        s, d = inp
        return h * d[..., None, None] + s, h

    h_last, h_in = lax.scan(step, h0.astype(f32), (jnp.moveaxis(states, 1, 0), jnp.moveaxis(chunk_decay, 1, 0)))
    h_in = jnp.moveaxis(h_in, 0, 1)
    y_off = jnp.einsum('bclgn,bcgrpn,bclgr->bclgrp', cm, h_in, jnp.exp(la))
    y = (y_diag + y_off).reshape(B, Tp, SSD_GROUPS, SSD_HPG, HEAD_DIM)[:, :T]
    return y, h_last

def ssd_branch(z, xbc, dt_raw, conv_buf, h0, conv_w, conv_b, dt_bias, a_log, d_skip, norm_g):
    B, T = xbc.shape[:2]
    f32 = jnp.float32
    xpad = jnp.concatenate([conv_buf.astype(xbc.dtype), xbc], axis=1)
    new_conv = xpad[:, T:]
    conv = lax.conv_general_dilated(xpad, conv_w[:, None, :], (1,), 'VALID',
                                    dimension_numbers=('NWC', 'WIO', 'NWC'),
                                    feature_group_count=CONV_CH) + conv_b
    u = jax.nn.silu(conv)
    xs = u[..., :SSD_WIDTH].reshape(B, T, SSD_GROUPS, SSD_HPG, HEAD_DIM)
    bm = u[..., SSD_WIDTH:SSD_WIDTH + SSD_GROUPS * D_STATE].reshape(B, T, SSD_GROUPS, D_STATE)
    cm = u[..., SSD_WIDTH + SSD_GROUPS * D_STATE:].reshape(B, T, SSD_GROUPS, D_STATE)
    dt = jax.nn.softplus(dt_raw.astype(f32) + dt_bias.astype(f32)).reshape(B, T, SSD_GROUPS, SSD_HPG)
    a = -jnp.exp(a_log.astype(f32)).reshape(SSD_GROUPS, SSD_HPG)
    y, h = ssd_scan(xs, dt, a, bm, cm, h0.reshape(B, SSD_GROUPS, SSD_HPG, HEAD_DIM, D_STATE))
    y = y + d_skip.astype(f32).reshape(SSD_GROUPS, SSD_HPG)[:, :, None] * xs.astype(f32)
    y = y.reshape(B, T, SSD_WIDTH).astype(z.dtype)
    out = rms_norm(y * jax.nn.silu(z), norm_g)
    return out, new_conv, h.reshape(B, SSD_HEADS, HEAD_DIM, D_STATE).astype(h0.dtype)

def layer_inputs(x, c, pos, w_ada, b_ada, norm_g, w_in):
    B, T = x.shape[:2]
    mod = jax.nn.silu(c) @ w_ada + b_ada
    shift, scale, gate = jnp.split(mod, 3, axis=-1)
    h = rms_norm(x, norm_g) * (1.0 + scale[:, None]) + shift[:, None]
    u = h @ w_in
    z_s, xbc, dt_raw, q_raw, u_c, u_s, u_w, g_raw, z_a = split_cols(u)
    q = rope(q_raw.reshape(B, T, ATT_HEADS, HEAD_DIM), pos)
    return gate, z_s, xbc, dt_raw, q, kv_rows(u_c, pos), kv_rows(u_s, pos), kv_rows(u_w, pos), g_raw, z_a

def layer_output(x, gate, y_ssd, o_br, g_raw, z_a, att_norm_g, w_out):
    B, T = x.shape[:2]
    gates = jax.nn.sigmoid(g_raw.astype(jnp.float32)).reshape(B, T, N_BRANCH, ATT_HEADS, 1).astype(x.dtype)
    o = jnp.sum(gates * o_br, axis=2).reshape(B, T, ATT_WIDTH)
    y_att = rms_norm(o * jax.nn.silu(z_a), att_norm_g)
    mix = jnp.concatenate([y_ssd, y_att], axis=-1) @ w_out
    return x + gate[:, None] * mix

def setup_inputs(seed: int = 0) -> dict:
    key = jax.random.key(seed)
    ks = jax.random.split(key, 24)
    f32 = jnp.float32
    n_pages = PAST_LEN // PAGE_SIZE
    n_used = DEC_BATCH * n_pages
    n_pool = n_used + n_used // 4
    win_len = min(WINDOW, PAST_LEN)

    def nrm(k, shape, s=1.0):
        return s * jax.random.normal(k, shape, f32)

    x_prompt = nrm(ks[0], (BATCH, SEQ, D_MODEL))
    x_sample = nrm(ks[1], (DEC_BATCH, DEC_SEQ, D_MODEL))
    cache_cmp_kv = nrm(ks[2], (DEPTH, n_pool, PAGE_SIZE, 2, KV_HEADS, HEAD_DIM))
    cache_slc_kv = nrm(ks[3], (DEPTH, n_pool, PAGE_SIZE, 2, KV_HEADS, HEAD_DIM))
    state_win_kv = nrm(ks[4], (DEPTH, DEC_BATCH, win_len, 2, KV_HEADS, HEAD_DIM))
    state_conv = nrm(ks[5], (DEPTH, DEC_BATCH, CONV_WIDTH - 1, CONV_CH))
    state_ssm = nrm(ks[6], (DEPTH, DEC_BATCH, SSD_HEADS, HEAD_DIM, D_STATE), 0.5)
    page_table = jax.random.permutation(ks[7], n_pool)[:n_used].reshape(DEC_BATCH, n_pages).astype(jnp.int32)
    c_prompt = nrm(ks[8], (BATCH, D_MODEL))
    c_sample = nrm(ks[9], (DEC_BATCH, D_MODEL))
    w_ada = nrm(ks[10], (DEPTH, D_MODEL, 3 * D_MODEL), D_MODEL ** -0.5)
    b_ada = nrm(ks[11], (DEPTH, 3 * D_MODEL), 0.02)
    norm_g = 1.0 + nrm(ks[12], (DEPTH, D_MODEL), 0.02)
    w_in = nrm(ks[13], (DEPTH, D_MODEL, IN_COLS), D_MODEL ** -0.5)
    conv_w = nrm(ks[14], (DEPTH, CONV_WIDTH, CONV_CH), CONV_WIDTH ** -0.5)
    conv_b = nrm(ks[15], (DEPTH, CONV_CH), 0.02)
    dt0 = jnp.exp(jax.random.uniform(ks[16], (DEPTH, SSD_HEADS), f32, math.log(DT_MIN), math.log(DT_MAX)))
    dt_bias = dt0 + jnp.log(-jnp.expm1(-dt0))
    a_log = jnp.log(jax.random.uniform(ks[17], (DEPTH, SSD_HEADS), f32, 1.0, 16.0))
    d_skip = 1.0 + nrm(ks[18], (DEPTH, SSD_HEADS), 0.1)
    ssd_norm_g = 1.0 + nrm(ks[19], (DEPTH, SSD_WIDTH), 0.02)
    att_norm_g = 1.0 + nrm(ks[20], (DEPTH, ATT_WIDTH), 0.02)
    w_out = nrm(ks[21], (DEPTH, MIX_WIDTH, D_MODEL), MIX_WIDTH ** -0.5)
    final_g = 1.0 + nrm(ks[22], (D_MODEL,), 0.02)
    return {'x_prompt': x_prompt, 'x_sample': x_sample,
            'cache_cmp_kv': cache_cmp_kv, 'cache_slc_kv': cache_slc_kv,
            'state_win_kv': state_win_kv, 'state_conv': state_conv, 'state_ssm': state_ssm,
            'page_table': page_table, 'c_prompt': c_prompt, 'c_sample': c_sample,
            'w_ada': w_ada, 'b_ada': b_ada, 'norm_g': norm_g, 'w_in': w_in,
            'conv_w': conv_w, 'conv_b': conv_b, 'dt_bias': dt_bias, 'a_log': a_log, 'd_skip': d_skip,
            'ssd_norm_g': ssd_norm_g, 'att_norm_g': att_norm_g, 'w_out': w_out, 'final_g': final_g}

def reference(x_prompt, x_sample, cache_cmp_kv, cache_slc_kv, state_win_kv, state_conv, state_ssm, page_table,
              c_prompt, c_sample, w_ada, b_ada, norm_g, w_in, conv_w, conv_b, dt_bias, a_log, d_skip,
              ssd_norm_g, att_norm_g, w_out, final_g):
    n_prompt, seq = x_prompt.shape[:2]
    dec_seq = x_sample.shape[1]
    past = page_table.shape[1] * PAGE_SIZE
    pos_p = jnp.arange(seq, dtype=jnp.int32)
    pos_s = past + jnp.arange(dec_seq, dtype=jnp.int32)
    xp, xs = x_prompt, x_sample
    out_p = [[], [], [], [], []]
    out_s = [[], [], [], [], []]
    for l in range(DEPTH):
        ssd_w = (conv_w[l], conv_b[l], dt_bias[l], a_log[l], d_skip[l], ssd_norm_g[l])
        gate, z_s, xbc, dt_raw, q, kv_c, kv_s, kv_w, g_raw, z_a = layer_inputs(
            xp, c_prompt, pos_p, w_ada[l], b_ada[l], norm_g[l], w_in[l])
        conv0 = jnp.zeros((n_prompt, CONV_WIDTH - 1, CONV_CH), xp.dtype)
        h0 = jnp.zeros((n_prompt, SSD_HEADS, HEAD_DIM, D_STATE), xp.dtype)
        y_ssd, conv_new, ssm_new = ssd_branch(z_s, xbc, dt_raw, conv0, h0, *ssd_w)
        o = nsa_prompt(q, kv_c, kv_s, kv_w)
        xp = layer_output(xp, gate, y_ssd, o, g_raw, z_a, att_norm_g[l], w_out[l])
        for lst, v in zip(out_p, (kv_c, kv_s, kv_w[:, seq - min(WINDOW, seq):], conv_new, ssm_new)):
            lst.append(v)
        gate, z_s, xbc, dt_raw, q, kv_c, kv_s, kv_w, g_raw, z_a = layer_inputs(
            xs, c_sample, pos_s, w_ada[l], b_ada[l], norm_g[l], w_in[l])
        y_ssd, conv_new, ssm_new = ssd_branch(z_s, xbc, dt_raw, state_conv[l], state_ssm[l], *ssd_w)
        o, win_new = nsa_sample(q, kv_c, kv_s, kv_w, cache_cmp_kv[l], cache_slc_kv[l], state_win_kv[l], page_table)
        xs = layer_output(xs, gate, y_ssd, o, g_raw, z_a, att_norm_g[l], w_out[l])
        for lst, v in zip(out_s, (kv_c, kv_s, win_new, conv_new, ssm_new)):
            lst.append(v)
    y_prompt = rms_norm(xp, final_g)
    y_sample = rms_norm(xs, final_g)
    sp = [jnp.stack(v) for v in out_p]
    sd = [jnp.stack(v) for v in out_s]
    return (y_prompt, y_sample, sp[0], sp[1], sp[2], sp[3], sp[4], sd[0], sd[1], sd[2], sd[3], sd[4])


_drawn_inputs = setup_inputs


def setup_inputs(seed=0):
    import zlib

    import numpy as np

    out = dict(_drawn_inputs(seed))
    spreads = {}
    factors = {'conv_b': 2.766, 'd_skip': 3.548, 'ssd_norm_g': 7.682, 'att_norm_g': 8.0, 'final_g': 2.788}
    for name, (base, spread) in spreads.items():
        noise = np.random.default_rng([zlib.crc32(name.encode()), seed]).standard_normal(out[name].shape)
        drawn = base * np.exp(spread * noise) if base else spread * noise
        out[name] = __import__('jax').numpy.asarray(drawn.astype(out[name].dtype))
    for name, factor in factors.items():
        out[name] = (out[name] * factor).astype(out[name].dtype)
    return out
```

```python
import numpy as np
import concourse.bass as bass
from concourse import mybir
from contextlib import ExitStack

F32 = mybir.dt.float32
F32R = mybir.dt.float32r
BF16 = mybir.dt.bfloat16
I32 = mybir.dt.int32
U32 = mybir.dt.uint32
ALU = mybir.AluOpType
ACT = mybir.ActivationFunctionType
AX = mybir.AxisListType

DM = 1024
SEQ = 1024
NB, NT = 8, 8
SR = NB * NT
PAST, PAGE = 1024, 128
NPG = PAST // PAGE
NPOOL = 80
HD = 64
SH, SG = 8, 2
SW = SH * HD
DS = 128
CW = 4
CCH = SW + 2 * SG * DS
AH, KVH = 8, 2
GQ = AH // KVH
KVW = KVH * HD
CB, SB = 32, 64
WIN = 512
ROT = HD // 4
HR = ROT // 2
THETA = 500000.0
NBR = 3
EPS = 1e-6
NEG = -1.0e30
P = 128
KT8 = DM // P
TT = SEQ // P
NCB = SEQ // CB
TOK = SEQ + SR

C_ZS = 0
C_X = C_ZS + SW
C_DT = C_X + CCH
C_Q = C_DT + SH
C_KC = C_Q + AH * HD
C_KS = C_KC + 2 * KVW
C_KW = C_KS + 2 * KVW
C_G = C_KW + 2 * KVW
C_ZA = C_G + NBR * AH


def constants():
    f = np.float32
    p = np.arange(P)
    parts = {}
    parts["ident"] = np.eye(P, dtype=f)
    parts["tri"] = (p[:, None] <= p[None, :]).astype(f)
    parts["low"] = (p[:, None] > p[None, :]).astype(f)
    parts["caus"] = np.where(p[None, :] > p[:, None], f(NEG), f(0))
    parts["edge"] = np.where(p[None, :] < p[:, None], f(NEG), f(0))
    q = (np.arange(TT)[None, :, None] * P + p[:, None, None])
    cend = (np.arange(NCB) + 1) * CB - 1
    cm = (cend[None, None, :] <= q).astype(f)
    parts["cm"] = cm.reshape(P, TT * NCB)
    parts["blk"] = (p[:, None] // CB == np.arange(P // CB)[None, :]).astype(f) / f(CB)
    s = np.arange(P)
    same = (s[:, None] // NT == s[None, :] // NT) & (s[:, None] < SR) & (s[None, :] < SR)
    parts["tris"] = (same & (s[:, None] <= s[None, :])).astype(f)[:, :SR]
    parts["lows"] = (same & (s[:, None] > s[None, :])).astype(f)[:, :SR]
    parts["ind"] = ((s[:, None] // NT == np.arange(NB)[None, :]) & (s[:, None] < SR)).astype(f)
    b2, hh, tt = s // 64, (s // NT) % AH, s % NT
    tok = np.arange(SR)
    pairs = np.arange(NB // 2)
    own = (tok[None, None, :] // NT == 2 * pairs[None, :, None] + b2[:, None, None]) \
        & (tok[None, None, :] % NT <= tt[:, None, None])
    parts["nneg"] = np.where(own, f(0), f(NEG)).reshape(P, NB // 2 * SR)
    parts["wneg"] = np.where(np.arange(NT)[None, :] >= tt[:, None], f(0), f(NEG))
    c4 = np.arange(P)
    ownc = c4[None, None, :] // NCB == 2 * np.arange(2)[None, :, None] + b2[:, None, None]
    parts["sneg"] = np.where(ownc, f(0), f(NEG)).reshape(P, 2 * P)
    parts["gsum"] = ((b2[:, None] == b2[None, :]) & (tt[:, None] == tt[None, :])
                     & (hh[:, None] // GQ == hh[None, :] // GQ)).astype(f)
    parts["idx"] = np.broadcast_to(np.arange(1, PAST // SB + 1, dtype=f), (P, PAST // SB))
    dup = [p[:, None] == HD * k + p[None, :] % HD for k in range(KVH)]
    parts["dup"] = np.concatenate(dup, axis=1).astype(f)
    parts["ones"] = np.ones((P, P), f)
    inv = f(THETA) ** (-np.arange(HR, dtype=f) * f(2.0) / f(ROT))
    pos = np.zeros((P, TT + 1), f)
    pos[:, :TT] = (np.arange(TT)[None, :] * P + p[:, None])
    pos[:SR, TT] = PAST + tok % NT
    ang = (pos[:, :, None] * inv.astype(f)[None, None, :]).astype(f)
    parts["cos"] = np.cos(ang).astype(f).reshape(P, -1)
    parts["sin"] = np.sin(ang).astype(f).reshape(P, -1)
    parts["pcol"] = np.stack([p, p % (PAGE // CB)], axis=1).astype(f)
    at, out = 0, {}
    for k, v in parts.items():
        out[k] = (at, v.shape[1])
        at += v.shape[1]
    return out, np.ascontiguousarray(np.concatenate(list(parts.values()), axis=1).astype(f))


def build_layer(nc, A, O, where, ncols, gate_dram, out_dram):
    ctx = ExitStack()
    with ctx:
        base = {}

        def sb(name, cols, dt=F32):
            base[name] = nc.sbuf_base
            return ctx.enter_context(nc.sbuf_tensor(name, [P, cols], dt))

        def sem(name):
            return ctx.enter_context(nc.semaphore(name))

        consts = sb("consts", ncols)
        hT = sb("hT", KT8 * TOK)
        W = sb("W", 2 * KT8 * 512)
        U = sb("U", 8 * TOK)
        Y = sb("Y", 9 * 512)
        Q = sb("Q", 9 * 512)
        Vs = sb("Vs", 9 * KVW)
        Vw = sb("Vw", 9 * KVW)
        KTs = sb("KTs", SEQ)
        KTw = sb("KTw", SEQ)
        T = sb("T", 6144)
        small = sb("small", 1400)
        masks = sb("masks", 3 * P, BF16)
        cmpm = sb("cmpm", 2 * 2 * KVW)
        KcTs = sb("KcTs", 2 * P)
        KnT = sb("KnT", 2 * SR)
        KcT = sb("KcT", 5 * NCB)
        Vbd = sb("Vbd", KVH * GQ * HD)
        hst = sb("hst", SW)
        idx = sb("idx", 2 + NB * NPG, I32)
        pgt = sb("pgt", 2 + NB * NPG, I32)
        PS = ctx.enter_context(nc.psum_tensor("PS", [P, 8 * 512], F32))

        def const(name):
            a, n = where[name]
            return consts[:, a:a + n]

        ident = const("ident")
        cosT = const("cos").rearrange("p (i f) -> p i f", f=HR)
        sinT = const("sin").rearrange("p (i f) -> p i f", f=HR)
        take = [0]

        def sm(n):
            a = take[0]
            take[0] += n
            assert take[0] <= 1400
            return small[:, a:a + n]

        s1T = sm(8 * 9).rearrange("p (c r) -> p c r", r=9)
        shT = sm(8 * 9).rearrange("p (c r) -> p c r", r=9)
        vecT = sm(56)
        normT, mixgT = vecT[:, 0:8], vecT[:, 8:16]
        convw = vecT[:, 16:56].rearrange("p (k c) -> p k c", k=5)
        cT = sm(8 * 9)
        ss = sm(9)
        rms = sm(9)
        graw = sm(9 * 24).rearrange("p (i g) -> p i g", g=24)
        gtmp = sm(9 * 24).rearrange("p (i g) -> p i g", g=24)
        dtr = sm(9 * 8).rearrange("p (i g) -> p i g", g=8)
        dtv = sm(9 * 8).rearrange("p (i g) -> p i g", g=8)
        dte = sm(9 * 8).rearrange("p (i g) -> p i g", g=8)
        dtA = sm(9 * 8).rearrange("p (i g) -> p i g", g=8)
        abc = sm(8)
        dbias = sm(8)
        dskip = sm(8)
        st = sm(300)
        hT3 = hT[:, :].rearrange("p (k t) -> p k t", k=KT8)
        Wk = [W[:, n * 4096:(n + 1) * 4096].rearrange("p (k c) -> p k c", k=KT8) for n in range(2)]
        U3 = U[:, :].rearrange("p (c t) -> p c t", c=8)
        Q3 = Q[:, :].rearrange("p (i c) -> p i c", i=9)
        Y3 = Y[:, :].rearrange("p (i c) -> p i c", i=9)
        kvc3 = Y[:, 0:9 * 256].rearrange("p (i c) -> p i c", i=9)
        Vs3 = Vs[:, :].rearrange("p (i c) -> p i c", i=9)
        Vw3 = Vw[:, :].rearrange("p (i c) -> p i c", i=9)
        Ks3 = T[:, 0:1152].rearrange("p (i c) -> p i c", i=9)
        Kw3 = T[:, 1152:2304].rearrange("p (i c) -> p i c", i=9)
        identb, causb, edgeb = (masks[:, n * P:(n + 1) * P] for n in range(3))
        cmpm3 = cmpm[:, :].rearrange("p (h c) -> p h c", h=2)

        def bank(n, a=0, b=512):
            return PS[:, n * 512 + a:n * 512 + b]

        def rows(i):
            return P if i < TT else SR

        s_A = sem('A')
        s_B = sem('B')
        s_Bblk = sem('Bblk')
        s_Btok = sem('Btok')
        s_CmT = sem('CmT')
        s_KT = sem('KT')
        s_KTev = sem('KTev')
        s_KTev_act = sem('KTev_act')
        s_MT = sem('MT')
        s_QS = sem('QS')
        s_QSt = sem('QSt')
        s_S = sem('S')
        s_V = sem('V')
        s_Vc = sem('Vc')
        s_act_chain = sem('act_chain')
        s_bias_in = sem('bias_in')
        s_blocksum = sem('blocksum')
        s_cT = sem('cT')
        s_cTp = sem('cTp')
        s_c_in = sem('c_in')
        s_cmasked = sem('cmasked')
        s_cmp_in = sem('cmp_in')
        s_cmz = sem('cmz')
        s_consts_in = sem('consts_in')
        s_conv = sem('conv')
        s_conv_stored = sem('conv_stored')
        s_copied = sem('copied')
        s_csil = sem('csil')
        s_csum = sem('csum')
        s_dec = sem('dec')
        s_doubled = sem('doubled')
        s_dsum = sem('dsum')
        s_dt = sem('dt')
        s_dtabs = sem('dtabs')
        s_dtexp = sem('dtexp')
        s_dtrep = sem('dtrep')
        s_dve_chain = sem('dve_chain')
        s_edec = sem('edec')
        s_empty_act = sem('empty_act')
        s_empty_dve = sem('empty_dve')
        s_eps = sem('eps')
        s_ex = sem('ex')
        s_exp = sem('exp')
        s_fill = sem('fill')
        s_final = sem('final')
        s_froot = sem('froot')
        s_gate_bias_in = sem('gate_bias_in')
        s_gate_out = sem('gate_out')
        s_gate_s_in = sem('gate_s_in')
        s_gated = sem('gated')
        s_gates_in = sem('gates_in')
        s_gs = sem('gs')
        s_hT_act = sem('hT_act')
        s_hT_dve = sem('hT_dve')
        s_hT_smp = sem('hT_smp')
        s_hTs_act = sem('hTs_act')
        s_hTs_dve = sem('hTs_dve')
        s_heads_in = sem('heads_in')
        s_hout = sem('hout')
        s_hstT = sem('hstT')
        s_hstored = sem('hstored')
        s_idx = sem('idx')
        s_kv_evac = sem('kv_evac')
        s_kv_evac_act = sem('kv_evac_act')
        s_kv_stored = sem('kv_stored')
        s_leading = sem('leading')
        s_max = sem('max')
        s_mod = sem('mod')
        s_modT = sem('modT')
        s_modTp = sem('modTp')
        s_mod_ok = sem('mod_ok')
        s_natT = sem('natT')
        s_nat_in = sem('nat_in')
        s_nst = sem('nst')
        s_nstate = sem('nstate')
        s_orow = sem('orow')
        s_ostored = sem('ostored')
        s_out = sem('out')
        s_pages = sem('pages')
        s_pages_in = sem('pages_in')
        s_pcn = sem('pcn')
        s_pool_chain = sem('pool_chain')
        s_proj = sem('proj')
        s_qlead = sem('qlead')
        s_rest = sem('rest')
        s_rms = sem('rms')
        s_root = sem('root')
        s_rope = sem('rope')
        s_sO = sem('sO')
        s_sS = sem('sS')
        s_scaled = sem('scaled')
        s_sconv_in = sem('sconv_in')
        s_segl = sem('segl')
        s_sexp = sem('sexp')
        s_silu = sem('silu')
        s_skip = sem('skip')
        s_small_T = sem('small_T')
        s_smax = sem('smax')
        s_smp_gated = sem('smp_gated')
        s_smp_in = sem('smp_in')
        s_squared = sem('squared')
        s_squares = sem('squares')
        s_sread = sem('sread')
        s_states_stored = sem('states_stored')
        s_stored = sem('stored')
        s_summed = sem('summed')
        s_tail = sem('tail')
        s_tailT = sem('tailT')
        s_taps = sem('taps')
        s_turned = sem('turned')
        s_turned_act = sem('turned_act')
        s_turned_dve = sem('turned_dve')
        s_u = sem('u')
        s_vec_in = sem('vec_in')
        s_wo_in = sem('wo_in')
        s_wo_scaled = sem('wo_scaled')
        s_xT = sem('xT')
        s_xev_act = sem('xev_act')
        s_xev_dve = sem('xev_dve')
        s_xn = sem('xn')
        s_xproj = sem('xproj')
        s_xsT = sem('xsT')
        s_xtok = sem('xtok')
        s_xw = sem('xw')
        s_y = sem('y')
        s_yroot = sem('yroot')
        s_ysq = sem('ysq')
        s_z = sem('z')
        s_zmul = sem('zmul')
        wload = [sem("wload0"), sem("wload1")]
        xin = [sem(f"xin{n}") for n in range(9)]
        xagain = [sem("xagain0"), sem("xagain1")]
        ystored = [sem("ystored0"), sem("ystored1")]
        ada = [[(0, 512, A["w_ada"][0][:, n * 512:(n + 1) * 512])] for n in range(6)]
        GROUPS = ada[0:4]
        w_in = A["w_in"][0]
        GROUPS += [[(0, 512, w_in[:, C_KC:C_KC + 512])],
                   [(0, 280, w_in[:, C_KW:C_KW + 280]), (280, 288, w_in[:, C_DT:C_DT + SH])],
                   [(0, 512, w_in[:, C_Q:C_Q + 512])],
                   [(0, 512, w_in[:, C_X:C_X + 512])],
                   [(0, 512, w_in[:, C_X + 512:C_X + 1024])]]
        GROUPS += ada[4:6]
        GROUPS += [[(0, 512, w_in[:, C_ZS:C_ZS + 512])],
                   [(0, 512, w_in[:, C_ZA:C_ZA + 512])]]
        G_KV, G_KW, G_Q, G_X, G_GATE, G_Z = 4, 5, 6, 7, 9, 11
        gate_rows = Y[0:9, 3328:4352]

        def arrived(eng, g):
            eng.wait_ge(wload[g % 2], 16 * sum(len(GROUPS[n]) for n in range(g % 2, g + 1, 2)))

        stores = {}

        def store(eng, dst, src, signal=s_stored, **kw):
            stores[signal.name] = (signal, stores.get(signal.name, (signal, 0))[1] + 16)
            eng.dma_start(dst, src, **kw).then_inc(signal, 16)

        def unit_parts(u):
            g, i, b = u // 9, u % 9, u % 4
            r = rows(i)
            dsts = {0: [(kvc3[0:r, i, :], 0, 256), (Ks3[0:r, i, :], 256, 384), (Vs3[0:r, i, :], 384, 512)],
                    1: [(Kw3[0:r, i, :], 0, 128), (Vw3[0:r, i, :], 128, 256), (graw[0:r, i, :], 256, 280),
                        (dtr[0:r, i, :], 280, 288)],
                    2: []}[g]
            parts = [(d, bank(b, x, y)[0:r]) for d, x, y in dsts]
            if g == 2:
                parts = [(Q3[0:r, i, :].rearrange("p (g k d) -> p k g d", g=GQ, k=KVH),
                          bank(b)[0:r].rearrange("p (k g d) -> p k g d", g=GQ, k=KVH))]
            return parts

        raw = [T[:, 3328 + 1115 * n:3328 + 1115 * (n + 1)] for n in range(2)]
        raw_s = [r[:, SEQ + 3:].rearrange("p (b t) -> p b t", t=NT + 3) for r in raw]
        tail = T[:, 5558:5774].rearrange("p (c t) -> p c t", c=8)
        scT = T[:, 5774:5966].rearrange("p (c b t) -> p c b t", c=8, t=3)
        taps = T[:, 5120:6144]
        sconv = Y[0:24, 2304:3328]

        segl = T[:, 0:1024].rearrange("p (h s) -> p h s", h=SH)
        decf = [T[:, 1024:2048], W[:, 4096:5120]]
        dec = [d.rearrange("p (h l) -> p h l", h=SH) for d in decf]
        xtok, xdt, xw, sk = ([T[:, a:a + 512], W[:, a + 3072:a + 3584]] for a in (2048, 2560, 3072, 3584))
        Btok, CBm = ([T[:, a:a + 256], W[:, a + 3072:a + 3328]] for a in (4096, 4352))
        yo = T[:, 4608:5120]
        segls = T[0:SR, 0:512].rearrange("p (h s) -> p h s", h=SH)
        decs = T[0:SR, 512:1024].rearrange("p (h l) -> p h l", h=SH)
        CmT = [T[:, 1024 + 512 * g:1600 + 512 * g] for g in range(SG)]
        Bblk = T[0:SR, 0:2048].rearrange("p (g b n) -> p g b n", g=SG, b=NB)
        kvrep = xtok[0][0:SR]
        nat = W[:, 0:4096].rearrange("p (b c n) -> p b c n", b=NB, c=4)
        hTs = W[:, 4096:8192].rearrange("p (b c) -> p b c", b=NB)
        ex = [st[:, 8 + 24 * n:32 + 24 * n] for n in range(2)]
        edec = st[:, 64:96].rearrange("p (c b) -> p c b", c=4)

        pgs = U[:, 0:4096].rearrange("p (b j c) -> p b j c", b=2, j=NPG)
        pgw = U[:, 4096:6144].rearrange("p (b j c) -> p b j c", b=2, j=WIN // P)
        KTpair = U[:, 6144:8192].rearrange("p (b c) -> p b c", b=2)
        KTwpair = T[:, 0:1024].rearrange("p (b c) -> p b c", b=2)
        PP = T[:, 1024:2816]
        PPs, PPw, PPc = PP[:, 0:1088], PP[:, 1088:1664], PP[:, 1664:1792]
        PTs = T[:, 2816:4864].rearrange("p (n r) -> p n r", r=P)
        QS = T[:, 4864:5376].rearrange("p (b h t) -> p b h t", b=NB, h=AH)
        orow = T[:, 5376:5568].rearrange("p (n d) -> p n d", n=NBR)
        smax, snmax, ssum = st[:, 100:103], st[:, 103:106], st[:, 106:109]
        imp, least, cand, last, drop = (st[:, 110:126], st[:, 126:127], st[:, 128:142], st[:, 142:143], st[:, 144:160])

        Pb = [T[:, n * 1024:(n + 1) * 1024] for n in range(4)]
        def rounded(name, over, col, cols=1024):
            return nc.alloc_sbuf_tensor_at(name, [P, cols], F32R, offset=(base[over] + 31) // 32 * 32 + 4 * col)[:, :]

        QH = [rounded(f"QH{n}", "T", 4096 + 1024 * n).rearrange("p (h t) -> p h t", h=AH) for n in range(2)]
        QL = [rounded(f"QL{n}", over, 0).rearrange("p (h t) -> p h t", h=AH) for n, over in enumerate(("KTs", "KTw"))]
        K2 = {(k, kv): rounded(f"K2{k}{kv}", over, col) for k, kv, over, col in
              (("s", 0, "hT", 5632), ("s", 1, "hT", 6656), ("w", 0, "hT", 7680), ("w", 1, "W", 0))}
        Kc2 = rounded("Kc2", "KcT", NCB, 2 * NCB)
        K2_PARTS = [(K2[k, kv][:, h * 512:(h + 1) * 512], kv, K[:, h * 512:(h + 1) * 512])
                    for h in range(2) for k, K in (("s", KTs), ("w", KTw)) for kv in range(KVH)]
        PT = [W[:, 2048 + n * 512:2560 + n * 512] for n in range(4)]
        OT = hT[:, 5120:5632]
        spare = U[:, 8192:8704]
        zt = [T[:, 5568:6080], spare]
        za = W[:, 4096:8192].rearrange("p (i c) -> p i c", i=TT)
        Z_AHEAD = [range(4 * p, 4 * p + 3) for p in range(NB // 2)] + [range(16, 18)]
        Z_AMID = [4 * p + 3 for p in range(NB // 2)]
        sneg_m = [st[:, 100 + 8 * n:108 + 8 * n] for n in range(2)]
        dsum = [st[:, 164 + 24 * n:188 + 24 * n].rearrange("p (n h) -> p n h", n=NBR) for n in range(2)]
        wgt = st[:, 212:220]
        cmax, cbias = st[:, 220:228], st[:, 228:260]

        UNITS, BUNDLES = [], []
        for i in range(TT):
            BUNDLES.append([len(UNITS)])
            UNITS.append((i, "c", 0, AH))
            for k, n in (("s", i + 1), ("w", min(i, WIN // P) + 1)):
                nh = {1: 8, 2: 4, 3: 2, 4: 2}.get(n, 1)
                for h in range(0, AH, max(nh, 2)):
                    BUNDLES.append([len(UNITS) + m for m in range(max(nh, 2) // nh)])
                    UNITS += [(i, k, h + m, nh) for m in range(max(nh, 2) // nh)]

        def keys(u):
            i, k, _, nh = UNITS[u]
            if k == "c":
                return 0, 2, 2 * P
            a = 0 if k == "s" else max(0, i - WIN // P)
            return a, i + 1 - a, 1024 // nh

        def blocks(bundle):
            us = BUNDLES[bundle]
            _, k, h0, nh = UNITS[us[0]]
            _, n, step = keys(us[0])
            if k == "c":
                return [(None, 0, 0, [(us[0], 0), (us[0], P)])]
            heads = range(h0, h0 + nh * len(us))
            out = []
            for kv in sorted({h // GQ for h in heads}):
                mine = [h for h in heads if h // GQ == kv]
                out += [(kv, t, mine[0], [(us[(h - h0) // nh], (h - h0) % nh * step + t * P) for h in mine]) for t in range(n)]
            return out

        TGROUPS, OF_BUNDLE = [], []
        for m in range(len(BUNDLES)):
            bl, first = blocks(m), len(TGROUPS)
            per = 4 // len(bl[0][3])
            TGROUPS += [(m, bl[x:x + per]) for x in range(0, len(bl), per)]
            OF_BUNDLE.append(range(first, len(TGROUPS)))

        def ends_branch(g):
            m = TGROUPS[g][0]
            u = BUNDLES[m][-1]
            return g == OF_BUNDLE[m][-1] and UNITS[u][2] + UNITS[u][3] == AH

        CGROUPS = [g for g, (m, _) in enumerate(TGROUPS) if UNITS[BUNDLES[m][0]][1] == "c"]

        def last_turn(u):
            return FILLS["T", OF_BUNDLE[next(m for m, us in enumerate(BUNDLES) if u in us)][-1]][0] + 1

        STEPS, CORE = [("QT", 0), ("S", 0)], [[] for _ in range(TT)]
        late = []

        def values(g):
            i, k = UNITS[BUNDLES[TGROUPS[g][0]][0]][0:2]
            at = [("V", g)]
            if ends_branch(g):
                at += [("SUM", i)] if k == "c" else [("COPY", 2 * i + (k == "w"))]
                late.extend([] if k == "c" else [("BACK", 2 * i + (k == "w"))])
            return at

        for m, us in enumerate(BUNDLES):
            i = UNITS[us[0]][0]
            ahead = BUNDLES[m + 1] if m + 1 < len(BUNDLES) else []
            ahead = [[("S", ahead[0])] if ahead else [], [("S", u) for u in ahead[1:]]]
            if UNITS[us[0]][1] == "w" and UNITS[us[0]][2] == 4 * (i > 0) and i < TT - 1:
                CORE[i].append(("QT", i + 1))
            CORE[i] += ahead[0]
            gs = OF_BUNDLE[m]
            for x, g in enumerate(gs):
                if x == (len(gs) + 1) // 2:
                    CORE[i] += ahead[1]
                CORE[i].append(("T", g))
                CORE[i] += late
                late.clear()
                if g >= 2:
                    CORE[i] += values(g - 2)
            if len(gs) < 2:
                CORE[i] += ahead[1]
        for g in (len(TGROUPS) - 2, len(TGROUPS) - 1):
            CORE[TT - 1] += values(g)
        CORE[TT - 1] += late

        def weave(core, fill):
            out, done = [], 0
            for n, step in enumerate(core):
                out.append(step)
                while done < (n + 1) * len(fill) // len(core):
                    if fill[done] and fill[done][0] == "GATE" and fill[done][1] >= 0 and ("BACK", 2 * fill[done][1] + 1) not in out:
                        break
                    out.append(fill[done])
                    done += 1
            return out

        for i in range(TT):
            fill = [("RES", i - 2), ("SQUARE", i - 2), ("GATE", i - 1), None, ("SCALE", i - 1), ("FINAL", i - 2),
                    ("TURN", i - 1)] + 4 * [("OUT", i - 1)] + [None, ("RES", i - 1)] + 2 * [("OUT", i - 1)]
            steps = CORE[i][:1] + 2 * [("OUT", i - 2)] + weave(CORE[i][1:], fill)
            STEPS += [s for s in steps if s and (s[0] in ("S", "T", "V", "QT", "SUM", "COPY", "BACK") or s[1] >= 0)]
        a, b, c = TT - 2, TT - 1, TT
        STEPS += 2 * [("OUT", a)] + [("RES", a), ("SQUARE", a), ("GATE", b), ("GATE", c), ("SCALE", b), ("FINAL", a), ("TURN", b),
                  ("SCALE", c)] + 4 * [("OUT", b)] + [("TURN", c), ("RES", b)] + 4 * [("OUT", b)] + [("RES", b), ("SQUARE", b), ("ROOT", b)]
        STEPS += 4 * [("OUT", c)] + [("FINAL", b), ("RES", c)] + 4 * [("OUT", c)] + [("RES", c), ("SQUARE", c), ("ROOT", c), ("FINAL", c)]
        AGAIN, times = [], {}
        for step in STEPS:
            AGAIN.append(times.get(step, 0))
            times[step] = AGAIN[-1] + 1

        FILLS, OWNER, EMPTIED = {}, [], []
        for what, u in STEPS:
            for _ in range({"QT": 2, "T": 1, "BACK": 1, "TURN": 2}.get(what, 0)):
                FILLS.setdefault((what, u), []).append(len(OWNER))
                OWNER.append("dve" if what in ("BACK", "QT") or (what != "TURN" and len(OWNER) % 2) or (what == "TURN" and len(FILLS[what, u]) > 1)
                             else "act")
                EMPTIED.append(OWNER.count(OWNER[-1]))

        def turn_parts(what, u, n):
            b = bank(4 + FILLS[what, u][n] % 2)
            if what == "TURN":
                return [(mixT(u, n), b[:, 0:4 * rows(u)])]
            cols = P * sum(len(bl[3]) for bl in TGROUPS[u][1])
            return [(PT[u % 4][:, 0:cols], b[:, 0:cols])]

        xre = [hT[:, n * 1024:1024 + n * 1024] for n in range(2)]
        res = [hT[:, 2048 + n * 1024:3072 + n * 1024] for n in range(2)]
        gate_p, fin_g = hT[:, 4096:5120], W[:, DM:2 * DM]
        gate_s = [M[0:SR, 0, :] for M in (Y3, Q3)]

        def mixT(u, n):
            return (Y3, Q3)[n][:, u, 0:4 * rows(u)]

        ssq, fss, eps2 = st[:, 260:278], st[:, 280:289], st[:, 289:290]
        wo = U[:, 0:8192].rearrange("p (k c) -> p k c", k=8)
        smp = U[0:SR, 0:1536].rearrange("p (h n d) -> p h n d", h=AH, n=NBR)

        def heads(ap, r=P):
            return ap[0:r].rearrange("p (h d) -> p h d", d=HD)

        def over_d(ap, r=P):
            return ap[0:r].unsqueeze(2).broadcast_to([r, SH, HD])

        chains = {"dve": 0, "act": 0, "pool": 0}

        def after(eng, key, chain, ins):
            chains[key] += 1
            ins.then_inc(chain, 1)
            eng.wait_ge(chain, chains[key])

        block = ctx.enter_context(nc.Block())

        @block.gpsimd
        def _(pool):
            pool.dma_start(abc, A["a_log"][0].partition_broadcast(P)).then_inc(s_heads_in, 16)
            pool.dma_start(dbias, A["dt_bias"][0].partition_broadcast(P)).then_inc(s_heads_in, 16)
            pool.dma_start(dskip, A["d_skip"][0].partition_broadcast(P)).then_inc(s_heads_in, 16)
            ptab = A["page_table"]
            for h in range(2):
                src = ptab[4 * h:4 * h + 4, :].rearrange("b j -> (b j)").unsqueeze(1)
                pool.dma_start(pgt[:, h:h + 1], src.unsqueeze(1).broadcast_to([4 * NPG, P // CB, 1]),
                               allow_slow_non_contiguous=True).then_inc(s_pages_in, 16)
            pool.dma_start(pgt[:, 2:], ptab.rearrange("b j -> (b j)").partition_broadcast(P)).then_inc(s_pages_in, 16)

            for h in range(2):
                if h == 0:
                    pool.wait_ge(s_xT, 16)
                pool.wait_ge(s_idx, 2)
                if h == 1:
                    pool.wait_ge(s_blocksum, 6)
                pool.indirect_dma_start(U[:, 0:8192], None, A["cache_cmp_kv"][0].rearrange("n (j t) a h d -> (n j) (t a h d)", t=CB),
                                        bass.IndirectOffsetOnAxis(ap=idx[:, h:h + 1].bitcast(U32), axis=0)).then_inc(s_cmp_in, 16)
                pool.wait_ge(s_cmp_in, 16 * (h + 1))
                w = CB * 2 * KVW // 2
                step = 0
                while w >= 2 * KVW:
                    dst = U[:, 0:w] if w > 2 * KVW else cmpm3[:, h, :]
                    nc.gpsimd.tensor_tensor(dst, U[:, 0:w], U[:, w:2 * w], ALU.add).then_inc(s_blocksum, 1)
                    step += 1
                    pool.wait_ge(s_blocksum, 6 * h + step)
                    w //= 2
                nc.gpsimd.tensor_scalar(cmpm3[:, h, :], cmpm3[:, h, :], 1.0 / CB, None, ALU.mult).then_inc(s_blocksum, 1)
            for n, (name, K3, V3) in enumerate((("cmp", kvc3[:, :, 0:128], kvc3[:, :, 128:256]), ("slc", Ks3, Vs3), ("win", Kw3, Vw3))):
                pool.wait_ge(s_rope, n + 1)
                pool.wait_ge(s_kv_evac, (4, 4, 9)[n])
                pool.wait_ge(s_kv_evac_act, (5, 5, 9)[n])
                i0 = TT - WIN // P if name == "win" else 0
                for a, X3 in ((0, K3), (1, V3)):
                    dst = O[f"new_{name}_prompt"][0, 0].rearrange("(i p) a h d -> p i a (h d)", p=P)[:, :, a, :]
                    store(pool, dst, X3[:, i0:TT, :], s_kv_stored)
                    if name == "win":
                        store(pool, O["new_win_sample"][0][:, WIN - NT:, a].rearrange("b t h d -> b t (h d)"), X3[0:SR, TT, :], s_kv_stored)
                    else:
                        store(pool, O[f"new_{name}_sample"][0].rearrange("b t a h d -> (b t) a (h d)")[:, a, :], X3[0:SR, TT, :], s_kv_stored)
            store(pool, O["new_win_sample"][0][:, 0:WIN - NT].rearrange("b t a h d -> b (t a h d)"),
                  A["state_win_kv"][0][:, NT:].rearrange("b t a h d -> b (t a h d)"))
            for ct in range(8):
                pool.wait_ge(s_xev_act, ct + 1)
                pool.wait_ge(s_xev_dve, ct + 1)
                nc.gpsimd.tensor_copy(tail[:, ct, 0:3], raw[ct % 2][:, SEQ:SEQ + 3]).then_inc(s_tail, 1)
                nc.gpsimd.tensor_copy(tail[:, ct, 3:27].rearrange("p (b t) -> p b t", t=3), raw_s[ct % 2][:, :, NT:]).then_inc(s_tail, 1)
            pool.wait_ge(s_taps, 2)
            store(pool, O["new_conv_prompt"][0, 0], taps[0:3, :], s_conv_stored)
            store(pool, O["new_conv_sample"][0].rearrange("b t c -> (b t) c"), taps[3:27, :], s_conv_stored)
            pool.wait_ge(s_mod_ok, 6)
            pool.dma_start(nat, A["state_ssm"][0].rearrange("b (c h) d n -> (h d) b c n", c=4)).then_inc(s_nat_in, 16)
            pool.wait_ge(s_conv, 8)
            pool.wait_ge(s_rope, 4)
            pool.wait_ge(s_dt, 1)
            pool.wait_ge(s_kv_stored, 16 * 12)
            for i in range(TT + 1):
                r = rows(i)
                lo, seg = (const("low"), segl) if i < TT else (const("lows"), segls)
                k = r
                if i:
                    pool.wait_ge(s_A, i)
                nc.gpsimd.tensor_tensor(seg, lo[0:r].unsqueeze(1).broadcast_to([r, SH, r]),
                                        dtA[0:r, i, :].unsqueeze(2).broadcast_to([r, SH, r]), ALU.mult).then_inc(s_segl, 1)
                if i >= 2:
                    pool.wait_ge(s_B, i - 1)
                    pool.wait_ge(s_y, i - 1)
                pool.wait_ge(s_xtok, i + 1)
                n = i % 2
                nc.gpsimd.tensor_tensor(heads(xdt[n], r), heads(xtok[n], r), over_d(dtv[:, i, :], r), ALU.mult).then_inc(s_pool_chain, 1)
                nc.gpsimd.tensor_tensor(heads(sk[n], r), heads(xtok[n], r), over_d(dskip, r), ALU.mult).then_inc(s_skip, 1)
                pool.wait_ge(s_pool_chain, i + 1)
                pool.wait_ge(s_ex, i + 1)
                nc.gpsimd.tensor_tensor(heads(xw[n], r), heads(xdt[n], r), over_d(ex[i % 2][:, 0:8], r), ALU.mult).then_inc(s_xw, 1)
            pool.wait_ge(s_skip, TT + 1)
            pool.wait_ge(s_xw, TT + 1)
            nc.gpsimd.tensor_copy(heads(kvrep, SR), over_d(dtA[:, TT, :], SR)).then_inc(s_dtrep, 1)
            pool.wait_ge(s_hout, 1)
            store(pool, O["new_ssm_prompt"][0, 0].rearrange("(c h) d n -> (h d) c n", c=4),
                  yo.rearrange("p (c n) -> p c n", c=4), s_hstored)
            pool.wait_ge(s_nstate, 8)
            for b in range(2):
                store(pool, O["new_ssm_sample"][0].rearrange("b (c h) d n -> (h d) b c n", c=4)[:, 4 * b:4 * b + 4],
                      nat[:, 4 * b:4 * b + 4], s_states_stored)
            cache_rows = A["cache_slc_kv"][0].rearrange("n t a h d -> (n t) (a h d)")
            pool.wait_ge(s_B, TT + 1)
            pool.wait_ge(s_CmT, 2)
            for p in range(NB // 2):
                if p:
                    pool.wait_ge(s_sO, p)
                for b in range(2):
                    for j in range(NPG):
                        c = 2 + (2 * p + b) * NPG + j
                        pool.indirect_dma_start(pgs[:, b, j, :], None, cache_rows,
                                                bass.IndirectOffsetOnAxis(ap=idx[:, c:c + 1].bitcast(U32), axis=0)).then_inc(s_pages, 16)
                    pool.dma_start(pgw[:, b], A["state_win_kv"][0][2 * p + b].rearrange("(j t) a h d -> t j (a h d)", t=P)).then_inc(s_pages, 16)
            pool.wait_ge(s_wo_in, 16)
            for k in range(KT8):
                nc.gpsimd.tensor_scalar(wo[:, k, :], wo[:, k, :], mixgT[:, k:k + 1], None, ALU.mult).then_inc(s_wo_scaled, 1)

        @block.scalar
        def _(act):
            def alink(ins):
                after(act, "act", s_act_chain, ins)

            act.wait_ge(s_c_in, 32)
            act.activation(Y[0:9, 2048:3072], Y[0:9, 1024:2048], ACT.Silu).then_inc(s_csil, 1)
            for i in range(TT + 1):
                act.wait_ge(xin[i], 16)
                x = U[:, i * DM:(i + 1) * DM] if i < TT else Y[0:SR, 0:DM]
                if i:
                    act.wait_ge(s_squares, i)
                act.activation(Y[0:rows(i), 3072:4096], x, ACT.Square, accum_out=ss[0:rows(i), i:i + 1]).then_inc(s_squares, 1)
            act.wait_ge(s_squares, TT + 1)
            act.wait_ge(s_eps, 1)
            act.activation(rms[:, 0:TT], ss[:, 0:TT], ACT.Sqrt, scale=1.0 / DM, bias=st[:, 0:1]).then_inc(s_rms, 1)
            act.activation(rms[0:SR, TT:], ss[0:SR, TT:], ACT.Sqrt, scale=1.0 / DM, bias=st[0:SR, 0:1]).then_inc(s_rms, 1)
            act.wait_ge(s_modT, 2)
            for n in range(0, 16, 2):
                ct, half = n % 8, n // 8
                act.wait_ge(s_xT, n + 1)
                act.activation(hT3[:, ct, half * 512:half * 512 + 512], bank(2 + n % 4), ACT.Identity,
                               scale=s1T[:, ct, 0:1], bias=shT[:, ct, 0:1]).then_inc(s_hT_act, 1)
            act.wait_ge(s_modTp, 1)
            for u in range(0, 27, 2):
                act.wait_ge(s_proj, u + 1)
                parts = unit_parts(u)
                for n, (d, s) in enumerate(parts):
                    ins = act.activation(d, s, ACT.Copy)
                ins.then_inc(s_kv_evac_act, 1)
                if u == 22:
                    act.wait_ge(s_dtabs, 1)
                    act.activation(dte, dte, ACT.Exp, scale=-1.0).then_inc(s_dtexp, 1)
                    act.wait_ge(s_dtexp, 1)
                    act.activation(dte, dte, ACT.Ln, bias=1.0).then_inc(s_dtexp, 1)
                    act.activation(gtmp, graw, ACT.Exp, scale=-1.0).then_inc(s_dtexp, 1)
                    act.wait_ge(s_heads_in, 48)
                    act.activation(abc, abc, ACT.Exp).then_inc(s_dtexp, 1)
            for n, (b, d) in enumerate(((4, KTs[:, 0:512]), (6, KTw[:, 0:512]))):
                act.wait_ge(s_KT, 2 * n + 1)
                act.activation(d, bank(b), ACT.Copy).then_inc(s_KTev_act, 1)
            for ct in range(9):
                if ct < 8:
                    act.wait_ge(s_xproj, ct + 1)
                    if ct >= 2:
                        act.wait_ge(s_conv, ct - 1)
                        act.wait_ge(s_tail, 2 * (ct - 1))
                    act.activation(raw[ct % 2][:, 3:515], bank(2 * (ct % 2)), ACT.Copy).then_inc(s_xev_act, 1)
                if ct >= 1:
                    act.wait_ge(s_conv, ct)
                    act.activation(U3[:, ct - 1, :], U3[:, ct - 1, :], ACT.Silu).then_inc(s_u, 1)
            for i in range(TT + 1):
                r = rows(i)
                act.wait_ge(s_A, i + 1)
                if i == 0:
                    act.wait_ge(s_kv_stored, 16 * 12)
                    act.wait_ge(s_conv, 8)
                    act.wait_ge(s_mod_ok, 6)
                if i >= 2:
                    act.wait_ge(s_xw, i - 1)
                    act.wait_ge(s_skip, i - 1)
                    act.wait_ge(s_y, i - 1)
                act.activation(xtok[i % 2][0:r], bank(0)[0:r], ACT.Copy).then_inc(s_xtok, 1)
                n = 24 if i < TT else 16
                act.activation(ex[i % 2][0:r, 0:n], bank(4, 0, n)[0:r], ACT.Exp).then_inc(s_ex, 1)
                if i >= 2:
                    act.wait_ge(s_B, i - 1)
                if i < TT:
                    act.activation(decf[i % 2], PS[:, 1024:2048], ACT.Exp).then_inc(s_dec, 1)
                else:
                    act.activation(T[0:SR, 512:1024], bank(2)[0:SR], ACT.Exp).then_inc(s_dec, 1)
            for n in range(0, 8, 2):
                act.wait_ge(s_natT, n + 1)
                act.activation(hTs[:, n, :], bank(n), ACT.Copy).then_inc(s_hTs_act, 1)
            act.wait_ge(s_dsum, 1)
            act.activation(st[:, 64:96], bank(4, 0, 32), ACT.Exp).then_inc(s_edec, 1)
            act.wait_ge(s_nst, 8)
            act.wait_ge(s_conv_stored, 32)
            act.wait_ge(s_hstored, 16)
            def z_silu(u):
                s, i = u // 9, u % 9
                r = rows(i)
                act.wait_ge(s_z, u + 1)
                if s == 0 and i >= 2:
                    act.wait_ge(s_ysq, u - 1)
                if u == 17:
                    act.wait_ge(s_ysq, 9)
                d = zt[u % 2][0:r] if s == 0 else za[:, i, :] if i < TT else spare[0:r]
                act.activation(d, bank(7)[0:r], ACT.Silu).then_inc(s_silu, 1)
                if s == 0:
                    act.wait_ge(s_zmul, u + 1)
                    act.activation(d, Y3[0:r, i, :], ACT.Square, accum_out=ssq[0:r, 2 * i:2 * i + 1]).then_inc(s_ysq, 1)

            for p in range(NB // 2):
                for u in Z_AHEAD[p]:
                    z_silu(u)
                for n in (0, 2, 4):
                    act.wait_ge(s_turned, 10 * p + n + 1)
                    if p:
                        act.wait_ge(s_sS, p)
                    d = KTpair[:, n // 2, 0:512] if n < 4 else KTwpair[:, 0, :]
                    act.activation(d, bank(4), ACT.Copy).then_inc(s_turned_act, 1)
                for n, X in ((0, PPc), (2, PPw), (1, PPs)):
                    act.wait_ge(s_smax, 3 * p + (0, 2, 1).index(n) + 1)
                    act.activation(X, X, ACT.Exp, bias=snmax[:, n:n + 1], accum_out=ssum[:, n:n + 1]).then_inc(s_sexp, 1)
                    if n == 2:
                        z_silu(Z_AMID[p])
                        act.wait_ge(s_turned, 10 * p + 7)
                        if p:
                            act.wait_ge(s_sO, p)
                        act.activation(PTs[:, 8:12, :].rearrange("p n r -> p (n r)"), bank(4), ACT.Copy).then_inc(s_turned_act, 1)
                act.wait_ge(s_turned, 10 * p + 9)
                act.activation(PTs[:, 0:4, :].rearrange("p n r -> p (n r)"), bank(4), ACT.Copy).then_inc(s_turned_act, 1)
            for u in Z_AHEAD[NB // 2]:
                z_silu(u)
            act.wait_ge(s_ysq, 9)
            q = ssq.rearrange("p (i s) -> p i s", s=2)[:, :, 0:1]
            for a, b, r in ((0, TT, P), (TT, TT + 1, SR)):
                act.activation(q[0:r, a:b], q[0:r, a:b], ACT.Sqrt, scale=1.0 / SW, bias=eps2[0:r]).then_inc(s_yroot, 1)
            act.wait_ge(s_sO, 4)
            act.wait_ge(s_orow, 4)
            act.wait_ge(s_ostored, 64)
            for n, (d, _, _) in enumerate(K2_PARTS + [(Kc2, 0, 0)]):
                act.wait_ge(s_doubled, n + 1)
                act.activation(d, bank(n % 8, 0, d.shape[1]), ACT.Copy).then_inc(s_leading, 1)
            for (what, u), again in zip(STEPS, AGAIN):
                r = rows(u) if u <= TT else None
                if what == "GATE":
                    if u < TT:
                        act.wait_ge(s_zmul, 10 + u)
                    q = ssq[0:r, 2 * u + 1:2 * u + 2]
                    alink(act.activation(za[0:r, min(u, TT - 1), :], Q3[0:r, u, :], ACT.Square, accum_out=q))
                    act.activation(q, q, ACT.Sqrt, scale=1.0 / SW, bias=eps2[0:r]).then_inc(s_root, 1)
                if what == "ROOT" or (what == "GATE" and 1 <= u < TT):
                    v = u if what == "ROOT" else u - 1
                    act.wait_ge(s_squared, v + 1)
                    f = fss[0:rows(v), v:v + 1]
                    act.activation(f, f, ACT.Sqrt, scale=1.0 / DM, bias=eps2[0:rows(v)]).then_inc(s_froot, 1)
                if what == "SQUARE":
                    act.wait_ge(s_summed, 2 * u + 2)
                    f = fss[0:r, u:u + 1]
                    act.activation(xre[u % 2][0:r], res[u % 2][0:r], ACT.Square, accum_out=f).then_inc(s_squared, 1)
                if what == "S":
                    i, k, h, nh = UNITS[u]
                    a, n, step = keys(u)
                    S = PS[:, u % 2 * 1024:u % 2 * 1024 + 1024]
                    act.wait_ge(s_max, u + 1)
                    if k == "c":
                        act.activation(Pb[u % 4][:, 0:step], Pb[u % 4][:, 0:step], ACT.Exp).then_inc(s_exp, 1)
                    else:
                        if u >= 4:
                            act.wait_ge(s_fill, last_turn(u - 4))
                        for m in range(nh):
                            ins = act.activation(Pb[u % 4][:, m * step:m * step + n * P], S[:, m * step:m * step + n * P], ACT.Exp,
                                                 bias=sneg_m[u % 2][:, m:m + 1], accum_out=dsum[i % 2][:, " sw".index(k), h + m:h + m + 1])
                        ins.then_inc(s_exp, 1)
                if what == "COPY":
                    i, k = u // 2, "sw"[u % 2]
                    act.wait_ge(s_V, [g for g in range(len(TGROUPS)) if ends_branch(g) and g not in CGROUPS][u] + 1)
                    if u:
                        act.wait_ge(s_fill, FILLS["BACK", u - 1][0] + 1)
                    act.activation(OT, bank(6), ACT.Copy).then_inc(s_copied, 1)
                for n, F in enumerate(FILLS.get((what, u), [])):
                    if what == "QT":
                        act.wait_ge(s_fill, F + 1)
                        act.activation(QH[u % 2][:, GQ * n:GQ * n + GQ, :], bank(4 + F % 2).rearrange("p (h t) -> p h t", h=GQ), ACT.Copy,
                                       scale=HD ** -0.5).then_inc(s_qlead, 1)
                    if OWNER[F] == "act":
                        act.wait_ge(s_fill, F + 1)
                        if what == "T" and u >= 4:
                            act.wait_ge(s_V, u - 3)
                        for d, s in turn_parts(what, u, n):
                            ins = act.activation(d, s, ACT.Copy)
                        ins.then_inc(s_empty_act, 1)

        @block.vector
        def _(dve):
            def link(ins):
                after(dve, "dve", s_dve_chain, ins)

            nc.vector.memset(st[:, 0:1], EPS).then_inc(s_eps, 1)
            dve.wait_ge(s_cTp, 1)
            link(nc.vector.tensor_copy(vecT, bank(7, 72, 128)))
            nc.vector.tensor_copy(cT, bank(7, 0, 72)).then_inc(s_cT, 1)
            dve.wait_ge(s_rms, 2)
            link(nc.vector.reciprocal(rms[:, 0:TT], rms[:, 0:TT]))
            link(nc.vector.reciprocal(rms[0:SR, TT:], rms[0:SR, TT:]))
            for i in range(TT + 1):
                x = U[:, i * DM:(i + 1) * DM] if i < TT else Y[0:SR, 0:DM]
                nc.vector.tensor_scalar(x, x, rms[0:rows(i), i:i + 1], None, ALU.mult).then_inc(s_xn, 1)
            dve.wait_ge(s_bias_in, 16)

            def mod_bias(g):
                dve.wait_ge(s_mod, g + 1)
                cols, bias = T[0:9, g * 512:(g + 1) * 512], T[0:9, 3072 + g * 512:3584 + g * 512]
                if g >= 4:
                    cols = bias = gate_rows[:, (g - 4) * 512:(g - 3) * 512]
                nc.vector.tensor_tensor(cols, bank(g % 2)[0:9, :], bias,
                                        ALU.add).then_inc(s_mod_ok, 1)

            for g in range(4):
                mod_bias(g)
            dve.wait_ge(s_modTp, 1)
            nc.vector.tensor_copy(shT, bank(6, 0, 72).rearrange("p (c r) -> p c r", r=9)).then_inc(s_modT, 1)
            nc.vector.scalar_tensor_tensor(s1T, bank(6, 72, 144).rearrange("p (c r) -> p c r", r=9), 1.0,
                                           normT.unsqueeze(2).broadcast_to([P, 8, 9]), ALU.add, ALU.mult).then_inc(s_modT, 1)
            dve.wait_ge(s_modT, 2)
            for n in range(1, 16, 2):
                ct, half = n % 8, n // 8
                dve.wait_ge(s_xT, n + 1)
                nc.vector.tensor_scalar(hT3[:, ct, half * 512:half * 512 + 512], bank(2 + n % 4),
                                        s1T[:, ct, 0:1], shT[:, ct, 0:1], ALU.mult, ALU.add).then_inc(s_hT_dve, 1)
            dve.wait_ge(s_xsT, 1)
            hs = hT3[:, :, SEQ:].rearrange("p k (b t) -> p k b t", t=NT)
            link(nc.vector.tensor_tensor(hs, bank(7).rearrange("p (k b t) -> p k b t", k=8, t=NT),
                                         s1T[:, :, 1:9].unsqueeze(3).broadcast_to([P, 8, NB, NT]), ALU.mult))
            nc.vector.tensor_tensor(hs, hs, shT[:, :, 1:9].unsqueeze(3).broadcast_to([P, 8, NB, NT]),
                                    ALU.add).then_inc(s_hT_smp, 1)
            dve.wait_ge(s_pages_in, 48)
            pcol = const("pcol")
            nc.vector.scalar_tensor_tensor(idx[:, 0:2], pgt[:, 0:2], float(PAGE // CB), pcol[:, 1:2].broadcast_to([P, 2]),
                                           ALU.mult, ALU.add).then_inc(s_idx, 1)
            nc.vector.scalar_tensor_tensor(idx[:, 2:], pgt[:, 2:], float(PAGE), pcol[:, 0:1].broadcast_to([P, NB * NPG]),
                                           ALU.mult, ALU.add).then_inc(s_idx, 1)
            for ap in (graw, dtr):
                nc.vector.memset(ap, 0.0)
            nc.vector.memset(Vbd[:, :], 0.0)
            nc.vector.memset(hst[:, :], 0.0)
            nc.vector.tensor_copy(identb, ident)
            nc.vector.tensor_copy(causb, const("caus"))
            link(nc.vector.tensor_copy(edgeb, const("edge")))

            def rope(X, i0, i1, r, heads):
                X4 = X[0:r, i0:i1, :].rearrange("p i (h d) -> p i h d", d=HD)
                x1, x2 = X4[:, :, :, 0:HR], X4[:, :, :, HR:ROT]
                shp = [r, i1 - i0, heads, HR]
                n = (i1 - i0) * heads * HR
                cos, sin = (t[0:r, i0:i1, :].unsqueeze(2).broadcast_to(shp) for t in (cosT, sinT))
                tmp = [T[0:r, 2304 + 256 * k:2304 + 256 * k + n].rearrange("p (i h d) -> p i h d", h=heads, d=HR) for k in range(4)]
                nc.vector.tensor_tensor(tmp[0], x1, cos, ALU.mult)
                nc.vector.tensor_tensor(tmp[1], x2, sin, ALU.mult)
                nc.vector.tensor_tensor(tmp[2], x2, cos, ALU.mult)
                link(nc.vector.tensor_tensor(tmp[3], x1, sin, ALU.mult))
                nc.vector.tensor_tensor(x1, tmp[0], tmp[1], ALU.subtract)
                return nc.vector.tensor_tensor(x2, tmp[2], tmp[3], ALU.add)

            roped = [0]

            def rope_all(X, heads):
                for i0 in range(0, TT, 4):
                    link(rope(X, i0, i0 + 4, P, heads))
                rope(X, TT, TT + 1, SR, heads).then_inc(s_rope, 1)
                roped[0] += 1
                dve.wait_ge(s_rope, roped[0])

            dve.wait_ge(s_modTp, 1)
            for u in range(1, 27, 2):
                dve.wait_ge(s_proj, u + 1)
                for d, s in unit_parts(u):
                    ins = nc.vector.tensor_copy(d, s)
                ins.then_inc(s_kv_evac, 1)
                if u == 11:
                    dve.wait_ge(s_kv_evac_act, 5)
                    dve.wait_ge(s_kv_evac, 6)
                    rope_all(kvc3[:, :, 0:128], KVH)
                    rope_all(Ks3, KVH)
                if u == 19:
                    dve.wait_ge(s_kv_evac_act, 9)
                    dve.wait_ge(s_kv_evac, 10)
                    rope_all(Kw3, KVH)
                    dve.wait_ge(s_heads_in, 48)
                    link(nc.vector.tensor_tensor(dtv, dtr, dbias.unsqueeze(1).broadcast_to([P, 9, SH]), ALU.add))
                    nc.vector.scalar_tensor_tensor(dte, dtv, -1.0, dtv, ALU.mult, ALU.max).then_inc(s_dtabs, 1)
                if u == 25:
                    dve.wait_ge(s_dtexp, 4)
                    link(nc.vector.scalar_tensor_tensor(dtv, dtv, 0.0, dte, ALU.max, ALU.add))
                    link(nc.vector.tensor_tensor(dtA, dtv, abc.unsqueeze(1).broadcast_to([P, 9, SH]), ALU.mult))
                    link(nc.vector.tensor_scalar(dtA, dtA, -1.0, None, ALU.mult))
                    link(nc.vector.tensor_scalar(gtmp, gtmp, 1.0, None, ALU.add))
                    nc.vector.reciprocal(gtmp, gtmp).then_inc(s_dt, 1)
            for n, (b, d) in enumerate(((5, KTs[:, 512:]), (7, KTw[:, 512:]))):
                dve.wait_ge(s_KT, 2 * n + 2)
                nc.vector.tensor_copy(d, bank(b)).then_inc(s_KTev, 1)
            dve.wait_ge(s_small_T, 1)
            nc.vector.tensor_copy(KnT[:, :], bank(4, 0, 128)).then_inc(s_KTev, 1)
            nc.vector.tensor_copy(KcT[:, 0:NCB], bank(4, 128, 160))
            nc.vector.tensor_copy(KcT[:, NCB:].rearrange("p (h c) -> p h c", h=GQ),
                                  bank(4, 160, 192).unsqueeze(1).broadcast_to([P, GQ, NCB])).then_inc(s_KTev, 1)
            nc.vector.tensor_copy(KcTs[:, :], bank(5, 0, 256)).then_inc(s_KTev, 1)
            nc.vector.tensor_copy(scT, bank(5, 256, 448).rearrange("p (c b t) -> p c b t", c=8, t=3)).then_inc(s_KTev, 1)
            dve.wait_ge(s_Vc, 1)
            Vbd4 = Vbd[:, :].rearrange("p (k h d) -> p k h d", k=KVH, h=GQ)
            for h in range(GQ):
                q = slice(32 * h, 32 * h + 32)
                ins = nc.vector.tensor_copy(Vbd4[q, :, h, :], bank(6, 0, 128)[q].rearrange("p (k d) -> p k d", k=KVH))
            ins.then_inc(s_KTev, 1)
            dve.wait_ge(s_kv_evac_act, 14)
            dve.wait_ge(s_kv_evac, 13)
            rope_all(Q3, AH)
            dve.wait_ge(s_blocksum, 12)
            for n in range(2):
                nc.vector.memset(raw[n][:, 0:3], 0.0)
            for ct in range(8):
                r, rs = raw[ct % 2], raw_s[ct % 2]
                dve.wait_ge(s_xproj, ct + 1)
                if ct >= 2:
                    dve.wait_ge(s_tail, 2 * (ct - 1))
                nc.vector.tensor_copy(r[:, 515:SEQ + 3], bank(2 * (ct % 2) + 1))
                nc.vector.tensor_copy(rs[:, :, 0:3], scT[:, ct])
                nc.vector.tensor_copy(rs[:, :, 3:], bank(4 + ct % 2, 0, SR).rearrange("p (b t) -> p b t", t=NT)).then_inc(s_xev_dve, 1)
                dve.wait_ge(s_xev_act, ct + 1)
                dve.wait_ge(s_xev_dve, ct + 1)
                o, os_ = U3[:, ct, 0:SEQ], U3[:, ct, SEQ:].rearrange("p (b t) -> p b t", t=NT)
                nc.vector.tensor_scalar(o, r[:, 0:SEQ], convw[:, 0, ct:ct + 1], convw[:, 4, ct:ct + 1], ALU.mult, ALU.add)
                link(nc.vector.tensor_scalar(os_, rs[:, :, 0:NT], convw[:, 0, ct:ct + 1], convw[:, 4, ct:ct + 1], ALU.mult, ALU.add))
                for k in range(1, CW):
                    w = convw[:, k, ct:ct + 1]
                    nc.vector.scalar_tensor_tensor(o, r[:, k:k + SEQ], w, o, ALU.mult, ALU.add)
                    ins = nc.vector.scalar_tensor_tensor(os_, rs[:, :, k:k + NT], w, os_, ALU.mult, ALU.add)
                    if k < CW - 1:
                        link(ins)
                ins.then_inc(s_conv, 1)
            dve.wait_ge(s_gate_bias_in, 16)
            for g in range(4, 6):
                mod_bias(g)
            dve.wait_ge(s_tailT, 1)
            dve.wait_ge(s_conv, 8)
            for h in range(2):
                nc.vector.tensor_copy(taps[0:27, h * 512:(h + 1) * 512], bank(6 + h)[0:27]).then_inc(s_taps, 1)
            def ssd_masks(i):
                r = rows(i)
                tri, D, n = (const("tri"), dec[i % 2], P) if i < TT else (const("tris"), decs, SR)
                dve.wait_ge(s_A, i + 1)
                if i == 0:
                    dve.wait_ge(s_gate_out, 16)
                    dve.wait_ge(s_kv_stored, 16 * 12)
                    dve.wait_ge(s_tail, 16)
                if i >= 2:
                    dve.wait_ge(s_B, i - 1)
                nc.vector.tensor_copy(Btok[i % 2][0:r], bank(1, 0, 256)[0:r]).then_inc(s_Btok, 1)
                cb3 = CBm[i % 2][0:r, 0:2 * n].rearrange("p (g l) -> p g l", g=SG)
                link(nc.vector.tensor_tensor(cb3, bank(1, 256, 256 + 2 * n)[0:r].rearrange("p (g l) -> p g l", g=SG),
                                             tri[0:r].unsqueeze(1).broadcast_to([r, SG, n]), ALU.mult))
                dve.wait_ge(s_dec, i + 1)
                for g in range(SG):
                    ins = nc.vector.tensor_tensor(D[:, 4 * g:4 * g + 4], D[:, 4 * g:4 * g + 4],
                                                  cb3[:, g].unsqueeze(1).broadcast_to([r, 4, n]), ALU.mult)
                ins.then_inc(s_MT, 1)

            ssd_masks(0)
            for i in range(TT + 1):
                r, e = rows(i), ex[i % 2]
                if i < TT:
                    ssd_masks(i + 1)
                if i == TT:
                    nc.vector.memset(T[:, 1024:2048], 0.0).then_inc(s_cmz, 1)
                    dve.wait_ge(s_cmz, 1)
                    for g in range(SG):
                        nc.vector.tensor_copy(CmT[g].rearrange("p (b c) -> p b c", c=NT * (NB + 1))[:, :, 0:NT],
                                              U3[:, 6 + g, SEQ:].rearrange("p (b t) -> p b t", t=NT)).then_inc(s_CmT, 1)
                    for n in range(1, 8, 2):
                        dve.wait_ge(s_natT, n + 1)
                        nc.vector.tensor_copy(hTs[:, n, :], bank(n)).then_inc(s_hTs_dve, 1)
                dve.wait_ge(s_B, i + 1)
                dve.wait_ge(s_skip, i + 1)
                y = heads(Y3[0:r, i, :], r)
                if i:
                    nc.vector.tensor_tensor(heads(yo, r), heads(bank(6), r), over_d(e[:, 8:16], r), ALU.mult)
                link(nc.vector.tensor_tensor(y, heads(bank(5), r), heads(sk[i % 2], r), ALU.add))
                if i:
                    ins = nc.vector.tensor_tensor(y, y, heads(yo, r), ALU.add)
                if i < TT:
                    link(nc.vector.tensor_tensor(heads(hst), heads(hst), over_d(e[:, 16:24]), ALU.mult))
                    ins = nc.vector.tensor_tensor(hst[:, :], hst[:, :], bank(7), ALU.add)
                ins.then_inc(s_y, 1)
                dve.wait_ge(s_y, i + 1)
            dve.wait_ge(s_hstT, 1)
            nc.vector.tensor_copy(yo, bank(0)).then_inc(s_hout, 1)
            for g in range(SG):
                nc.vector.tensor_tensor(Bblk[:, g], Btok[0][0:SR, g * P:(g + 1) * P].unsqueeze(1).broadcast_to([SR, NB, P]),
                                        const("ind")[0:SR].unsqueeze(2).broadcast_to([SR, NB, P]), ALU.mult).then_inc(s_Bblk, 1)
            dve.wait_ge(s_edec, 1)
            for m in range(8):
                c, h = m // 2, m % 2
                dve.wait_ge(s_nst, m + 1)
                part = nat[:, 4 * h:4 * h + 4, c, :]
                link(nc.vector.tensor_tensor(part, part, edec[:, c, 4 * h:4 * h + 4].unsqueeze(2).broadcast_to([P, 4, P]), ALU.mult))
                nc.vector.tensor_tensor(part, part, bank(m).rearrange("p (b n) -> p b n", b=4), ALU.add).then_inc(s_nstate, 1)
            dve.wait_ge(s_nst, 8)
            dve.wait_ge(s_conv_stored, 32)
            dve.wait_ge(s_hstored, 16)
            nc.vector.memset(eps2, EPS)
            link(nc.vector.memset(QS, 0.0))
            dve.wait_ge(s_QSt, 1)
            for k in range(KVH):
                q = slice(64 * k, 64 * k + 64)
                nc.vector.tensor_scalar(QS[q, :, GQ * k:GQ * k + GQ, :], bank(7, 0, 256)[q].rearrange("p (g b t) -> p b g t", g=GQ, t=NT),
                                        HD ** -0.5, None, ALU.mult).then_inc(s_QS, 1)
            nneg = const("nneg").rearrange("p (n c) -> p n c", n=NB // 2)
            sneg = const("sneg").rearrange("p (n c) -> p n c", n=2)
            link(nc.vector.memset(drop, 0.0))

            def row_max(n, X):
                link(nc.vector.reduce_max(smax[:, n:n + 1], X, AX.X))
                nc.vector.tensor_scalar(snmax[:, n:n + 1], smax[:, n:n + 1], -1.0, None, ALU.mult).then_inc(s_smax, 1)

            def z_mul(u):
                if u < 9:
                    y = Y3[0:rows(u), u, :]
                    dve.wait_ge(s_silu, u + 1)
                    nc.vector.tensor_tensor(y, y, zt[u % 2][0:rows(u)], ALU.mult).then_inc(s_zmul, 1)

            for p in range(NB // 2):
                for u in Z_AHEAD[p]:
                    z_mul(u)
                for n in (1, 3, 5):
                    dve.wait_ge(s_turned, 10 * p + n + 1)
                    if p:
                        dve.wait_ge(s_sS, p)
                    d = KTpair[:, n // 2, 512:] if n < 4 else KTwpair[:, 1, :]
                    nc.vector.tensor_copy(d, bank(5)).then_inc(s_turned_dve, 1)
                dve.wait_ge(s_sS, p + 1)
                if p:
                    dve.wait_ge(s_turned, 10 * p)
                link(nc.vector.tensor_tensor(PPc, bank(3, 128, 256), sneg[:, p % 2, :], ALU.add))
                row_max(0, PPc)
                nc.vector.tensor_copy(PPw[:, NT:512], bank(2, NT, 512))
                nc.vector.tensor_tensor(PPw[:, 0:NT], bank(2, 0, NT), const("wneg"), ALU.add)
                link(nc.vector.tensor_tensor(PPw[:, 512:], bank(3, 64, 128), nneg[:, p, :], ALU.add))
                row_max(2, PPw)
                dve.wait_ge(s_sexp, 3 * p + 1)
                link(nc.vector.reciprocal(ssum[:, 0:1], ssum[:, 0:1]))
                nc.vector.tensor_scalar(PPc, PPc, ssum[:, 0:1], None, ALU.mult).then_inc(s_pcn, 1)
                dve.wait_ge(s_gs, p + 1)
                link(nc.vector.tensor_reduce(imp, bank(3, 256, 384).rearrange("p (s k two) -> p k s two", s=4, two=2), AX.XY, ALU.add))
                link(nc.vector.tensor_reduce(least, imp[:, 1:15], AX.X, ALU.min))
                link(nc.vector.scalar_tensor_tensor(cand, imp[:, 1:15], least, const("idx")[:, 1:15], ALU.is_equal, ALU.mult))
                link(nc.vector.reduce_max(last, cand, AX.X))
                link(nc.vector.tensor_scalar(drop[:, 1:15], const("idx")[:, 1:15], last, NEG, ALU.is_equal, ALU.mult))
                dve.wait_ge(s_turned, 10 * p + 8)
                nc.vector.tensor_copy(PTs[:, 12, :], bank(5, 0, P))
                nc.vector.tensor_copy(PTs[0:SR, 14, :], bank(5, P, 2 * P)[0:SR]).then_inc(s_turned_dve, 1)
                nc.vector.tensor_tensor(PPs[:, 0:PAST].rearrange("p (k s) -> p k s", s=SB), PS[:, 0:PAST].rearrange("p (k s) -> p k s", s=SB),
                                        drop.unsqueeze(2).broadcast_to([P, PAST // SB, SB]), ALU.add)
                nc.vector.tensor_tensor(PPs[:, PAST:], bank(3, 0, 64), nneg[:, p, :], ALU.add).then_inc(s_sread, 1)
                dve.wait_ge(s_sread, p + 1)
                row_max(1, PPs)
                z_mul(Z_AMID[p])
                dve.wait_ge(s_turned, 10 * p + 10)
                nc.vector.tensor_copy(PTs[0:SR, 13, :], bank(3, 384, 512)[0:SR])
                nc.vector.tensor_copy(PTs[:, 4:8].rearrange("p n r -> p (n r)"), bank(5)).then_inc(s_turned_dve, 1)
                dve.wait_ge(s_sexp, 3 * p + 3)
                nc.vector.memset(ssum[:, 0:1], 1.0)
                link(nc.vector.reciprocal(ssum[:, 1:3], ssum[:, 1:3]))
                dve.wait_ge(s_sO, p + 1)
                if p:
                    dve.wait_ge(s_ostored, 16 * p)
                for n in range(4):
                    q, k = slice(32 * n, 32 * n + 32), n % 2
                    ins = nc.vector.tensor_tensor(orow[q], bank(6, 0, 384)[q].rearrange("p (n k d) -> p n k d", n=NBR, k=KVH)[:, :, k, :],
                                                  ssum[q].unsqueeze(2).broadcast_to([32, NBR, HD]), ALU.mult)
                ins.then_inc(s_orow, 1)
                dve.wait_ge(s_orow, p + 1)
            dve.wait_ge(s_smp_in, 16 * NB)
            link(nc.vector.tensor_tensor(smp, smp, gtmp[0:SR, TT, :].rearrange("p (n h) -> p h n", n=NBR).unsqueeze(3).broadcast_to([SR, AH, NBR, HD]),
                                         ALU.mult))
            osm = heads(Q3[0:SR, TT, :], SR)
            link(nc.vector.tensor_tensor(osm, smp[:, :, 0, :], smp[:, :, 1, :], ALU.add))
            link(nc.vector.tensor_tensor(osm, osm, smp[:, :, 2, :], ALU.add))
            dve.wait_ge(s_silu, 18)
            nc.vector.tensor_tensor(Q3[0:SR, TT, :], Q3[0:SR, TT, :], spare[0:SR], ALU.mult).then_inc(s_smp_gated, 2)
            for n, (d, _, _) in enumerate(K2_PARTS + [(Kc2, 0, 0)]):
                dve.wait_ge(s_leading, n + 1)
                low = d[64:128]
                nc.vector.tensor_tensor(low, bank(n % 8, 0, d.shape[1])[64:128], low.bitcast(F32), ALU.subtract).then_inc(s_rest, 1)
            dve.wait_ge(s_smp_gated, 2)
            cm = const("cm").rearrange("p (i c) -> p i c", i=TT)
            for (what, u), again in zip(STEPS, AGAIN):
                r = rows(u) if u <= TT else None
                if what == "GATE" and u < TT:
                    nc.vector.tensor_tensor(Q3[:, u, :], Q3[:, u, :], za[:, u, :], ALU.mult).then_inc(s_zmul, 1)
                if what == "RES":
                    dve.wait_ge(s_out, 2 * u + again + 1)
                    if u + again == 0:
                        dve.wait_ge(s_gates_in, 32)
                    if u >= 2 and again == 0:
                        dve.wait_ge(ystored[u % 2], 16 * (u // 2))
                    if again == 0:
                        dve.wait_ge(xagain[u % 2], 16 * (u // 2 + 1))
                    c = slice(512 * again, 512 * again + 512)
                    x = res[u % 2][0:r, c]
                    if u == TT:
                        dve.wait_ge(s_gate_s_in, 32)
                    nc.vector.tensor_tensor(x, bank(7)[0:r], gate_p[:, c] if u < TT else gate_s[again], ALU.mult).then_inc(s_gated, 1)
                    dve.wait_ge(s_gated, 2 * u + again + 1)
                    nc.vector.tensor_tensor(x, x, xre[u % 2][0:r, c], ALU.add).then_inc(s_summed, 1)
                if what == "SCALE":
                    dve.wait_ge(s_root, u + 1)
                    if u == 0:
                        dve.wait_ge(s_yroot, 2)
                    q = ssq[0:r, 2 * u:2 * u + 2]
                    link(nc.vector.reciprocal(q, q))
                    for s, M in enumerate((Y3, Q3)):
                        nc.vector.tensor_scalar(M[0:r, u, :], M[0:r, u, :], q[:, s:s + 1], None, ALU.mult).then_inc(s_scaled, 1)
                if what == "FINAL":
                    dve.wait_ge(s_froot, u + 1)
                    x = res[u % 2][0:r]
                    link(nc.vector.reciprocal(fss[0:r, u:u + 1], fss[0:r, u:u + 1]))
                    nc.vector.scalar_tensor_tensor(x, x, fss[0:r, u:u + 1], fin_g[0:r], ALU.mult, ALU.mult).then_inc(s_final, 1)
                if what == "S":
                    i, k, h, nh = UNITS[u]
                    a, n, step = keys(u)
                    S = PS[:, u % 2 * 1024:u % 2 * 1024 + 1024]
                    dve.wait_ge(s_S, u + 1)
                    if k == "c":
                        C, S = Pb[u % 4][:, 0:step].rearrange("p (h c) -> p h c", h=AH), S[:, 0:step].rearrange("p (h c) -> p h c", h=AH)
                        if u >= 4:
                            dve.wait_ge(s_fill, last_turn(u - 4))
                        link(nc.vector.tensor_scalar(cbias, cm[:, i, :], -1.0, -NEG, ALU.add, ALU.mult))
                        link(nc.vector.tensor_tensor(C, S, cbias.unsqueeze(1).broadcast_to([P, AH, NCB]), ALU.add))
                        link(nc.vector.tensor_reduce(cmax, C, AX.X, ALU.max))
                        nc.vector.tensor_tensor(C, C, cmax.unsqueeze(2).broadcast_to([P, AH, NCB]), ALU.subtract).then_inc(s_max, 1)
                    else:
                        if u >= 2:
                            dve.wait_ge(s_exp, u - 1)
                        nc.vector.tensor_reduce(sneg_m[u % 2][:, 0:nh], S.rearrange("p (h s) -> p h s", h=nh)[:, :, 0:n * P], AX.X, ALU.max,
                                                negate=True).then_inc(s_max, 1)
                if what == "T" and u in CGROUPS:
                    c = BUNDLES[TGROUPS[u][0]][0]
                    i = UNITS[c][0]
                    C = Pb[c % 4][:, 0:256].rearrange("p (h c) -> p h c", h=AH)
                    dve.wait_ge(s_exp, c + 1)
                    link(nc.vector.tensor_tensor(C, C, cm[:, i, :].unsqueeze(1).broadcast_to([P, AH, NCB]), ALU.mult))
                    nc.vector.tensor_reduce(dsum[i % 2][:, 0, :], C, AX.X, ALU.add).then_inc(s_cmasked, 1)
                for n, F in enumerate(FILLS.get((what, u), [])):
                    if what == "QT":
                        dve.wait_ge(s_qlead, 2 * u + n + 1)
                        h = slice(GQ * n, GQ * n + GQ)
                        nc.vector.scalar_tensor_tensor(QL[u % 2][:, h, :], bank(4 + F % 2).rearrange("p (h t) -> p h t", h=GQ), HD ** -0.5,
                                                       QH[u % 2][:, h, :].bitcast(F32), ALU.mult, ALU.subtract).then_inc(s_empty_dve, 1)
                    elif OWNER[F] == "dve" and what != "BACK":
                        dve.wait_ge(s_fill, F + 1)
                        if what == "T" and u >= 4:
                            dve.wait_ge(s_V, u - 3)
                        for d, s in turn_parts(what, u, n):
                            ins = nc.vector.tensor_copy(d, s)
                        ins.then_inc(s_empty_dve, 1)
                if what in ("SUM", "BACK"):
                    i, n = (u, 0) if what == "SUM" else (u // 2, 1 + u % 2)
                    d = dsum[i % 2][:, n, :]
                    link(nc.vector.tensor_scalar(wgt, d, 1e-30, None, ALU.max))
                    link(nc.vector.reciprocal(wgt, wgt))
                    link(nc.vector.tensor_tensor(wgt, wgt, gtmp[:, i, n * AH:(n + 1) * AH], ALU.mult))
                    o = Q3[:, i, :]
                    if what == "SUM":
                        dve.wait_ge(s_V, CGROUPS[i] + 1)
                        nc.vector.tensor_tensor(heads(o), heads(bank(6)), over_d(wgt), ALU.mult).then_inc(s_csum, 1)
                        dve.wait_ge(s_csum, i + 1)
                    else:
                        F = FILLS[what, u][0]
                        dve.wait_ge(s_fill, F + 1)
                        back = bank(4 + F % 2).rearrange("p (g k d) -> p k g d", g=GQ, k=KVH)
                        w = wgt.rearrange("p (k g) -> p k g", k=KVH).unsqueeze(3).broadcast_to([P, KVH, GQ, HD])
                        nc.vector.tensor_tensor(spare.rearrange("p (k g d) -> p k g d", k=KVH, g=GQ), back, w, ALU.mult).then_inc(s_empty_dve, 1)
                        dve.wait_ge(s_empty_dve, EMPTIED[F])
                        link(nc.vector.tensor_tensor(o, o, spare, ALU.add))

        @block.tensor
        def _(pe):
            pe.wait_ge(s_csil, 1)
            pe.wait_ge(s_consts_in, 16)
            pe.wait_ge(s_vec_in, 5 * 16)
            nc.tensor.transpose(bank(7, 72, 128), Y[0:56, 4096:4224], ident[0:56, 0:56])
            for c in range(KT8):
                ins = nc.tensor.transpose(bank(7, c * 9, c * 9 + 9), Y[0:9, 2048 + c * P:2048 + (c + 1) * P], ident[0:9, 0:9])
            ins.then_inc(s_cTp, 1)
            pe.wait_ge(s_cT, 1)

            def mod_group(g):
                at = g if g < 4 else G_GATE + g - 4
                arrived(pe, at)
                if g >= 2:
                    pe.wait_ge(s_mod_ok, g - 1)
                for k in range(KT8):
                    ins = nc.tensor.matmul(bank(g % 2)[0:9, :], cT[:, k * 9:k * 9 + 9], Wk[at % 2][:, k, :],
                                           start=(k == 0), stop=(k == KT8 - 1))
                    if k == KT8 - 1:
                        ins.then_inc(s_mod, 1)

            for g in range(4):
                mod_group(g)
            pe.wait_ge(s_mod_ok, 4)
            for c in range(16):
                ins = nc.tensor.transpose(bank(6, c * 9, c * 9 + 9), T[0:9, c * P:(c + 1) * P], ident[0:9, 0:9])
            ins.then_inc(s_modTp, 1)
            pe.wait_ge(s_xn, TT + 1)
            for n in range(16):
                ct, half = n % 8, n // 8
                if n >= 4:
                    pe.wait_ge((s_hT_act, s_hT_dve)[n % 2], (n - 4) // 2 + 1)
                for j in range(4):
                    i = 4 * half + j
                    ins = nc.tensor.transpose(bank(2 + n % 4, j * P, j * P + P), U[:, i * DM + ct * P:i * DM + ct * P + P], ident)
                ins.then_inc(s_xT, 1)
            for ct in range(8):
                ins = nc.tensor.transpose(bank(7, ct * SR, ct * SR + SR), Y[0:SR, ct * P:(ct + 1) * P], ident[0:SR, 0:SR])
            ins.then_inc(s_xsT, 1)

            pe.wait_ge(s_hT_act, 8)
            pe.wait_ge(s_hT_dve, 8)
            pe.wait_ge(s_hT_smp, 1)
            pe.wait_ge(s_mod_ok, 4)
            UCOLS = (512, 288, 512)
            for u in range(27):
                g, i = u // 9, u % 9
                if i == 0:
                    arrived(pe, G_KV + g)
                if u >= 4:
                    pe.wait_ge((s_kv_evac_act, s_kv_evac)[u % 2], (u - 4) // 2 + 1)
                for k in range(KT8):
                    ins = nc.tensor.matmul(bank(u % 4, 0, UCOLS[g])[0:rows(i)], hT3[:, k, i * P:i * P + rows(i)],
                                           Wk[(G_KV + g) % 2][:, k, 0:UCOLS[g]], start=(k == 0), stop=(k == KT8 - 1))
                ins.then_inc(s_proj, 1)
            pe.wait_ge(s_rope, 3)
            for n, K3 in enumerate((Ks3, Kw3)):
                for i in range(TT):
                    ins = nc.tensor.transpose(bank(4 + 2 * n + i // 4, i % 4 * P, i % 4 * P + P), K3[:, i, :], ident)
                    if i % 4 == 3:
                        ins.then_inc(s_KT, 1)
            pe.wait_ge(s_KTev_act, 2)
            pe.wait_ge(s_KTev, 2)
            pe.wait_ge(s_kv_evac, 13)
            for n, K3 in enumerate((Ks3, Kw3)):
                nc.tensor.transpose(bank(4, n * SR, (n + 1) * SR), K3[0:SR, TT, :], ident[0:SR, 0:SR])
            for i in range(TT):
                for a in range(2):
                    nc.tensor.matmul(bank(4, 128 + a * 32 + 4 * i, 132 + a * 32 + 4 * i), kvc3[:, i, a * P:(a + 1) * P], const("blk"),
                                     start=True, stop=True)
            pe.wait_ge(s_blocksum, 12)
            for h in range(2):
                nc.tensor.transpose(bank(5, h * P, (h + 1) * P), cmpm3[:, h, 0:P], ident)
            pe.wait_ge(s_sconv_in, 16)
            for ct in range(8):
                ins = nc.tensor.transpose(bank(5, 256 + ct * 24, 280 + ct * 24), sconv[:, ct * P:(ct + 1) * P], ident[0:24, 0:24])
            ins.then_inc(s_small_T, 1)
            pe.wait_ge(s_KTev, 6)
            nc.tensor.matmul(bank(6, 0, P), KcT[:, NCB:], ident, start=True, stop=True).then_inc(s_Vc, 1)
            pe.wait_ge(s_kv_evac_act, 14)
            for ct in range(8):
                if ct % 4 == 0:
                    arrived(pe, G_X + ct // 4)
                if ct >= 2:
                    pe.wait_ge(s_xev_act, ct - 1)
                    pe.wait_ge(s_xev_dve, ct - 1)
                w = Wk[(G_X + ct // 4) % 2]
                for b, a, n in ((2 * (ct % 2), 0, 512), (2 * (ct % 2) + 1, 512, 512), (4 + ct % 2, SEQ, SR)):
                    for k in range(KT8):
                        ins = nc.tensor.matmul(bank(b, 0, n), w[:, k, ct % 4 * P:ct % 4 * P + P], hT3[:, k, a:a + n],
                                               start=(k == 0), stop=(k == KT8 - 1))
                ins.then_inc(s_xproj, 1)
            pe.wait_ge(s_xev_act, 7)
            pe.wait_ge(s_xev_dve, 7)
            for g in range(4, 6):
                mod_group(g)
            pe.wait_ge(s_tail, 16)
            pe.wait_ge(s_KTev, 7)
            for ct in range(8):
                ins = nc.tensor.transpose(bank(6 + ct // 4, ct % 4 * P, ct % 4 * P + P)[0:27], tail[:, ct, :], ident)
            ins.then_inc(s_tailT, 1)

            def ssd_A(i):
                r = rows(i)
                t = slice(i * P, i * P + r)
                if i == 0:
                    pe.wait_ge(s_u, 8)
                    pe.wait_ge(s_mod_ok, 6)
                    pe.wait_ge(s_taps, 2)
                    pe.wait_ge(s_KTev, 7)
                    pe.wait_ge(s_dt, 1)
                else:
                    pe.wait_ge(s_xtok, i)
                    pe.wait_ge(s_MT, i)
                    pe.wait_ge(s_ex, i)
                    pe.wait_ge(s_dec, i)
                for c in range(6):
                    nc.tensor.transpose(bank(c // 4, c % 4 * P, c % 4 * P + P)[0:r], U3[:, c, t], ident)
                for g in range(SG):
                    nc.tensor.matmul(bank(1, 256 + g * r, 256 + (g + 1) * r)[0:r], U3[:, 4 + g, t], U3[:, 6 + g, t],
                                     start=True, stop=True)
                lo, tr = (const("low"), const("tri")) if i < TT else (const("lows"), const("tris"))
                for n, m in enumerate((lo, tr, const("ones"))[0:3 if i < TT else 2]):
                    nc.tensor.matmul(bank(4, 8 * n, 8 * n + 8)[0:r], m[0:r], dtA[0:r, i, :], start=True, stop=True)
                pe.wait_ge(s_segl, i + 1)
                for h in range(SH):
                    s = segl[:, h, :] if i < TT else segls[:, h, :]
                    o = bank(2 + h // 4, h % 4 * P, h % 4 * P + P) if i < TT else bank(2, h * SR, (h + 1) * SR)[0:SR]
                    ins = nc.tensor.matmul(o, s, tr[0:r], start=True, stop=True)
                ins.then_inc(s_A, 1)

            def ssd_B(i):
                r = rows(i)
                if i:
                    pe.wait_ge(s_y, i)
                if 0 < i < TT:
                    for g in range(SG):
                        nc.tensor.matmul(bank(6, g * 256, (g + 1) * 256), U3[:, 6 + g, i * P:(i + 1) * P],
                                         hst[:, g * 256:(g + 1) * 256], start=True, stop=True)
                if i == TT:
                    pe.wait_ge(s_hTs_act, 4)
                    pe.wait_ge(s_hTs_dve, 4)
                    pe.wait_ge(s_CmT, 2)
                    for g in range(SG):
                        for b in range(NB):
                            nc.tensor.matmul(bank(6, g * 256, (g + 1) * 256)[0:SR], CmT[g][:, b * SR:(b + 1) * SR],
                                             hTs[:, b, g * 256:(g + 1) * 256], start=(b == 0), stop=(b == NB - 1))
                pe.wait_ge(s_MT, i + 1)
                pe.wait_ge(s_xw, i + 1)
                n = i % 2
                D = dec[n] if i < TT else decs
                for h in range(SH):
                    ins = nc.tensor.matmul(bank(5, h * HD, (h + 1) * HD)[0:r], D[:, h, :], xdt[n][0:r, h * HD:(h + 1) * HD],
                                           start=True, stop=True)
                pe.wait_ge(s_Btok, i + 1)
                if i < TT:
                    for g in range(SG):
                        ins = nc.tensor.matmul(bank(7, g * 256, (g + 1) * 256), Btok[n][:, g * P:(g + 1) * P],
                                               xw[n][:, g * 256:(g + 1) * 256], start=True, stop=True)
                ins.then_inc(s_B, 1)

            ssd_A(0)
            for i in range(TT):
                ssd_A(i + 1)
                ssd_B(i)
            pe.wait_ge(s_nat_in, 16)
            pe.wait_ge(s_xtok, 9)
            pe.wait_ge(s_ex, 9)
            pe.wait_ge(s_dec, 9)
            pe.wait_ge(s_MT, 9)
            pe.wait_ge(s_y, 8)
            for b in range(NB):
                for c in range(4):
                    ins = nc.tensor.transpose(bank(b, c * P, (c + 1) * P), nat[:, b, c, :], ident)
                ins.then_inc(s_natT, 1)
            ssd_B(TT)
            for c in range(4):
                ins = nc.tensor.transpose(bank(0, c * P, (c + 1) * P), hst[:, c * P:(c + 1) * P], ident)
            ins.then_inc(s_hstT, 1)
            pe.wait_ge(s_dtrep, 1)
            for c in range(4):
                ins = nc.tensor.matmul(bank(4, c * 8, c * 8 + 8), kvrep[:, c * P:(c + 1) * P], const("ind")[0:SR], start=True, stop=True)
            ins.then_inc(s_dsum, 1)
            pe.wait_ge(s_Bblk, 2)
            pe.wait_ge(s_hout, 1)
            pe.wait_ge(s_y, 9)
            pe.wait_ge(s_edec, 1)
            for m in range(8):
                c, h = m // 2, m % 2
                nc.tensor.matmul(bank(m), xw[0][0:SR, c * P:(c + 1) * P],
                                 Bblk[:, c // 2, 4 * h:4 * h + 4, :].rearrange("p b n -> p (b n)"), start=True, stop=True).then_inc(s_nst, 1)

            pe.wait_ge(s_rope, 4)
            pe.wait_ge(s_nstate, 8)
            for g in range(GQ):
                ins = nc.tensor.transpose(bank(7, g * SR, (g + 1) * SR), Q3[0:SR, TT, g * P:(g + 1) * P], ident[0:SR, 0:SR])
            ins.then_inc(s_QSt, 1)

            def turn(G, parts):
                if G >= 2:
                    pe.wait_ge((s_turned_act, s_turned_dve)[G % 2], (G - 2) // 2 + 1)
                for a, src in parts:
                    n = src.shape[1]
                    ins = nc.tensor.transpose(bank(4 + G % 2, a, a + P)[0:n], src, ident)
                ins.then_inc(s_turned, 1)

            def z_unit(u):
                s, i = u // 9, u % 9
                if i == 0:
                    arrived(pe, G_Z + s)
                if u:
                    pe.wait_ge(s_silu, u)
                for k in range(KT8):
                    ins = nc.tensor.matmul(bank(7)[0:rows(i)], hT3[:, k, i * P:i * P + rows(i)], Wk[(G_Z + s) % 2][:, k, :],
                                           start=(k == 0), stop=(k == KT8 - 1))
                ins.then_inc(s_z, 1)

            pe.wait_ge(s_QS, 2)
            for p in range(NB // 2):
                for u in Z_AHEAD[p]:
                    z_unit(u)
                pe.wait_ge(s_pages, 288 * (p + 1))
                for n in range(6):
                    src = pgs[:, n // 2, 4 * (n % 2):4 * (n % 2) + 4] if n < 4 else pgw[:, n - 4]
                    turn(10 * p + n, [(j * P, src[:, j, 0:P]) for j in range(4)])
                pe.wait_ge(s_turned_act, 5 * p + 3)
                pe.wait_ge(s_turned_dve, 5 * p + 3)
                if p:
                    pe.wait_ge(s_sread, p)
                for b in range(2):
                    q = slice(64 * b, 64 * b + 64)
                    lhsT = QS[:, 2 * p + b].rearrange("p h t -> p (h t)")
                    for o, rhs in ((bank(3, 128, 256), KcTs[:, p // 2 * P:(p // 2 + 1) * P]), (bank(3, 0, 64), KnT[:, 0:SR]),
                                   (bank(3, 64, 128), KnT[:, SR:]), (bank(2), KTwpair[:, b, :]),
                                   (bank(0), KTpair[:, b, 0:512]), (bank(1), KTpair[:, b, 512:])):
                        ins = nc.tensor.matmul(o[q], lhsT, rhs, start=True, stop=True)
                ins.then_inc(s_sS, 1)
                z_unit(Z_AMID[p])
                pe.wait_ge(s_pcn, p + 1)
                nc.tensor.matmul(bank(3, 256, 384), const("gsum"), PPc, start=True, stop=True).then_inc(s_gs, 1)
                pe.wait_ge(s_sexp, 3 * p + 2)
                turn(10 * p + 6, [(j * P, PPw[:, j * P:(j + 1) * P]) for j in range(4)])
                turn(10 * p + 7, [(0, PPc), (P, PPw[:, 512:])])
                pe.wait_ge(s_turned_act, 5 * p + 4)
                pe.wait_ge(s_turned_dve, 5 * p + 4)
                if p:
                    pe.wait_ge(s_orow, p)
                nc.tensor.matmul(bank(6, 0, P), PTs[:, 12, :], cmpm3[:, p // 2, P:], start=True, stop=True)
                for o, t0, vals, nt, tn, Vn in ((bank(6, 2 * P, 3 * P), 8, pgw, WIN // P, 14, Vw3), (bank(6, P, 2 * P), 0, pgs, NPG, 13, Vs3)):
                    if t0 == 0:
                        pe.wait_ge(s_sexp, 3 * p + 3)
                        for n in range(2):
                            if n == 1:
                                nc.tensor.transpose(bank(3, 384, 512)[0:SR], PPs[:, PAST:], ident)
                            turn(10 * p + 8 + n, [(j * P, PPs[:, (4 * n + j) * P:(4 * n + j + 1) * P]) for j in range(4)])
                        pe.wait_ge(s_turned_act, 5 * p + 5)
                        pe.wait_ge(s_turned_dve, 5 * p + 5)
                    for b in range(2):
                        q = slice(64 * b, 64 * b + 64)
                        for t in range(nt):
                            nc.tensor.matmul(o[q], PTs[:, t0 + t, q], vals[:, b, t, P:], start=(t == 0), stop=False)
                        ins = nc.tensor.matmul(o[q], PTs[0:SR, tn, q], Vn[0:SR, TT, :], start=False, stop=True)
                ins.then_inc(s_sO, 1)
            for u in Z_AHEAD[NB // 2]:
                z_unit(u)

            pe.wait_ge(s_orow, 4)
            pe.wait_ge(s_silu, 18)
            for n, (_, kv, K) in enumerate(K2_PARTS):
                nc.tensor.matmul(bank(n), const("dup")[:, kv * P:(kv + 1) * P], K, start=True, stop=True).then_inc(s_doubled, 1)
            pe.wait_ge(s_rest, 1)
            for kv in range(KVH):
                ins = nc.tensor.matmul(bank(0, kv * NCB, (kv + 1) * NCB), const("dup")[:, kv * P:(kv + 1) * P], KcT[:, 0:NCB], start=True, stop=True)
            ins.then_inc(s_doubled, 1)
            pe.wait_ge(s_rest, len(K2_PARTS) + 1)

            def emptied(F):
                if F >= 0:
                    pe.wait_ge({"act": s_empty_act, "dve": s_empty_dve}[OWNER[F]], EMPTIED[F])

            for (what, u), again in zip(STEPS, AGAIN):
                if what in ("GATE", "SCALE", "RES", "SQUARE", "ROOT", "FINAL", "SUM", "COPY"):
                    continue
                if what == "TURN":
                    r = rows(u)
                    pe.wait_ge(s_scaled, 2 * u + 2)
                    for n, F in enumerate(FILLS[what, u]):
                        emptied(F - 2)
                        for c in range(4):
                            ins = nc.tensor.transpose(bank(4 + F % 2, c * r, (c + 1) * r), (Y3, Q3)[n][0:r, u, c * P:(c + 1) * P],
                                                      ident[0:r, 0:r])
                        ins.then_inc(s_fill, 1)
                    continue
                if what == "OUT":
                    r = rows(u)
                    half, n = again // 4, again % 4
                    if again == 0:
                        pe.wait_ge(s_wo_scaled, KT8) if u == 0 else None
                        for F in FILLS["TURN", u]:
                            emptied(F)
                    if n == 0 and u + half:
                        pe.wait_ge(s_gated, 2 * u + half)
                    for k in range(2 * n, 2 * n + 2):
                        ins = nc.tensor.matmul(bank(7)[0:r], mixT(u, k // 4)[:, k % 4 * r:(k % 4 + 1) * r], wo[:, k, half * 512:(half + 1) * 512],
                                               start=(k == 0), stop=(k == KT8 - 1))
                    if n == 3:
                        ins.then_inc(s_out, 1)
                    continue
                if what == "QT":
                    for kv, F in enumerate(FILLS[what, u]):
                        emptied(F - 2)
                        for g in range(GQ):
                            q, to = Q3[:, u, g * P + kv * HD:g * P + (kv + 1) * HD], bank(4 + F % 2, g * P, (g + 1) * P)
                            nc.tensor.transpose(to[0:64], q, ident)
                            ins = nc.tensor.matmul(to[64:128], q, ident, start=True, stop=True)
                        ins.then_inc(s_fill, 1)
                elif what == "S":
                    i, k, h, nh = UNITS[u]
                    a, n, step = keys(u)
                    if k == "c":
                        emptied(FILLS["QT", i][1])
                    if u >= 2:
                        pe.wait_ge(s_exp, u - 1)
                    base = u % 2 * 1024
                    if k == "c":
                        for hh in range(AH):
                            for n, q in enumerate((QH, QL)):
                                ins = nc.tensor.matmul(PS[:, base + hh * NCB:base + (hh + 1) * NCB], q[i % 2][:, hh, :],
                                                       Kc2[:, hh // GQ * NCB:(hh // GQ + 1) * NCB], start=(n == 0), stop=(n == 1))
                    else:
                        for hh in range(h, h + nh):
                            K = K2[k, hh // GQ]
                            for t in range(0, n, 4):
                                m = min(4, n - t)
                                edge = k == "w" and t == 0 and i >= WIN // P
                                last = t + m == n
                                for x, q in enumerate((QH, QL)):
                                    ins = nc.tensor.matmul(PS[:, base + t * P:base + (t + m) * P], q[i % 2][:, hh, :],
                                                           K[:, (a + t) * P:(a + t + m) * P], start=(x == 0), stop=x == 1 and not (edge or last))
                                if edge:
                                    ins = nc.tensor.matmul(PS[:, base:base + P], identb, edgeb, start=False, stop=not last)
                                if last:
                                    ins = nc.tensor.matmul(PS[:, base + (n - 1) * P:base + n * P], identb, causb, start=False, stop=True)
                            base += step
                    ins.then_inc(s_S, 1)
                elif what == "T":
                    F = FILLS[what, u][0]
                    m, bl = TGROUPS[u]
                    pe.wait_ge(s_exp, BUNDLES[m][-1] + 1)
                    if u in CGROUPS:
                        pe.wait_ge(s_cmasked, CGROUPS.index(u) + 1)
                    emptied(F - 2)
                    for n, (unit, c) in enumerate(x for b in bl for x in b[3]):
                        ins = nc.tensor.transpose(bank(4 + F % 2, n * P, (n + 1) * P), Pb[unit % 4][:, c:c + P], ident)
                    ins.then_inc(s_fill, 1)
                elif what == "V":
                    m, bl = TGROUPS[u]
                    i, k = UNITS[BUNDLES[m][0]][0:2]
                    a, n, _ = keys(BUNDLES[m][0])
                    emptied(FILLS["T", u][0])
                    if k == "c" and i:
                        pe.wait_ge(s_copied, 2 * i)
                    if k == "s" and u - 1 in CGROUPS:
                        pe.wait_ge(s_csum, i + 1)
                    if k == "w" and ends_branch(u - 1):
                        pe.wait_ge(s_copied, 2 * i + 1)
                    if k == "c":
                        for kk in range(KVH):
                            ins = nc.tensor.matmul(bank(6, kk * 256, (kk + 1) * 256), PT[u % 4][:, kk * P:(kk + 1) * P],
                                                   Vbd[:, kk * 256:(kk + 1) * 256], start=True, stop=True)
                    else:
                        V3, at = Vs3 if k == "s" else Vw3, 0
                        for kv, t, h0, where_h in bl:
                            w, c = len(where_h) * P, h0 % GQ * P
                            ins = nc.tensor.matmul(bank(6, c, c + w)[64 * kv:64 * kv + 64], V3[:, a + t, kv * HD:(kv + 1) * HD],
                                                   PT[u % 4][:, at:at + w], start=(t == 0), stop=(t == n - 1))
                            at += w
                    ins.then_inc(s_V, 1)
                elif what == "BACK":
                    F = FILLS[what, u][0]
                    pe.wait_ge(s_copied, u + 1)
                    emptied(F - 2)
                    for g in range(GQ):
                        ins = nc.tensor.transpose(bank(4 + F % 2, g * P, (g + 1) * P), OT[:, g * P:(g + 1) * P], ident)
                    ins.then_inc(s_fill, 1)


        @block.sync
        def _(sp):
            sp.dma_start(Y[0:1, 1024:2048], A["c_prompt"]).then_inc(s_c_in, 16)
            sp.dma_start(Y[1:9, 1024:2048], A["c_sample"]).then_inc(s_c_in, 16)
            vec = Y[:, 4096:4224]
            for r, n, src in ((0, 8, A["norm_g"]), (8, 4, A["ssd_norm_g"]), (12, 4, A["att_norm_g"]),
                              (16, 32, A["conv_w"].rearrange("l k c -> l (k c)")), (48, 8, A["conv_b"])):
                sp.dma_start(vec[r:r + n, :], src[0].rearrange("(c p) -> c p", p=P)).then_inc(s_vec_in, 16)
            sp.dma_start(consts[:, :], A["table"]).then_inc(s_consts_in, 16)
            for i in range(TT):
                sp.dma_start(U[:, i * DM:(i + 1) * DM], A["x_prompt"][0][i * P:(i + 1) * P, :]).then_inc(xin[i], 16)
            sp.dma_start(Y[0:SR, 0:DM], A["x_sample"].rearrange("b t c -> (b t) c")).then_inc(xin[TT], 16)
            sp.dma_start(T[0:9, 3072:5120], A["b_ada"][0, 0:2 * DM].partition_broadcast(9)).then_inc(s_bias_in, 16)
            USED = {g: (s_mod, g + 1) for g in range(4)} | {G_GATE: (s_mod, 5), G_GATE + 1: (s_mod, 6)}
            USED |= {g: (s_proj, 9 * (g - G_KV + 1)) for g in (G_KV, G_KW, G_Q)}
            USED |= {g: (s_xproj, 4 * (g - G_X + 1)) for g in (G_X, G_X + 1)}
            for g in range(len(GROUPS)):
                if g >= 2:
                    sp.wait_ge(*USED[g - 2])
                if g == G_Z:
                    sp.wait_ge(s_nst, 8)
                if g == G_Z + 1:
                    sp.wait_ge(s_states_stored, 32)
                for a, b, src in GROUPS[g]:
                    sp.dma_start(Wk[g % 2][:, :, a:b], src.rearrange("(k p) c -> p k c", p=P)).then_inc(wload[g % 2], 16)
                if g == G_KW:
                    sp.wait_ge(s_hT_smp, 1)
                    sp.dma_start(gate_rows, A["b_ada"][0, 2 * DM:].partition_broadcast(9)).then_inc(s_gate_bias_in, 16)
                    sp.dma_start(sconv, A["state_conv"][0].rearrange("b t c -> (b t) c")).then_inc(s_sconv_in, 16)
                if g == G_GATE + 1:
                    sp.wait_ge(s_mod_ok, 6)
                    sp.dma_start(gate_dram, gate_rows).then_inc(s_gate_out, 16)
            for p in range(NB // 2):
                sp.wait_ge(s_orow, p + 1)
                sp.dma_start(out_dram[2 * p:2 * p + 2].rearrange("b r c -> (b r) c"), orow.rearrange("p n d -> p (n d)")).then_inc(s_ostored, 16)
            sp.wait_ge(s_ostored, 64)
            sp.wait_ge(s_sO, 4)
            for b in range(NB):
                sp.dma_start(smp[b * NT:(b + 1) * NT], out_dram[b].rearrange("(h t) (n d) -> t h n d", t=NT, n=NBR)).then_inc(s_smp_in, 16)
            sp.wait_ge(s_smp_gated, 2)
            sp.wait_ge(s_silu, 18)
            sp.wait_ge(s_gate_out, 16)
            x_rows = [A["x_prompt"][0][i * P:(i + 1) * P, :] for i in range(TT)] + [A["x_sample"].rearrange("b t c -> (b t) c")]
            y_rows = [O["y_prompt"][0][i * P:(i + 1) * P, :] for i in range(TT)] + [O["y_sample"].rearrange("b t c -> (b t) c")]
            for i in range(2):
                sp.dma_start(xre[i], x_rows[i]).then_inc(xagain[i], 16)
            sp.dma_start(wo, A["w_out"][0].rearrange("(k p) c -> p k c", p=P)).then_inc(s_wo_in, 16)
            sp.dma_start(gate_p, gate_dram[0].partition_broadcast(P)).then_inc(s_gates_in, 16)
            sp.dma_start(fin_g, A["final_g"].partition_broadcast(P)).then_inc(s_gates_in, 16)
            for i in range(TT + 1):
                sp.wait_ge(s_squared, i + 1)
                if i + 2 <= TT:
                    sp.dma_start(xre[i % 2][0:rows(i + 2)], x_rows[i + 2]).then_inc(xagain[i % 2], 16)
                sp.wait_ge(s_final, i + 1)
                store(sp, y_rows[i], res[i % 2][0:rows(i)], ystored[i % 2])
                if i == 0:
                    for c in range(2):
                        sp.dma_start(gate_s[c], gate_dram[1:9, c * 512:(c + 1) * 512].unsqueeze(1).broadcast_to([NB, NT, 512])).then_inc(s_gate_s_in, 16)
            for signal, count in stores.values():
                sp.wait_ge(signal, count)


_IN = ['x_prompt', 'x_sample', 'cache_cmp_kv', 'cache_slc_kv', 'state_win_kv', 'state_conv', 'state_ssm',
       'page_table', 'c_prompt', 'c_sample', 'w_ada', 'b_ada', 'norm_g', 'w_in', 'conv_w', 'conv_b',
       'dt_bias', 'a_log', 'd_skip', 'ssd_norm_g', 'att_norm_g', 'w_out', 'final_g']
_OUT = [("y_prompt", (1, SEQ, DM)), ("y_sample", (NB, NT, DM)),
        ("new_cmp_prompt", (1, 1, SEQ, 2, KVH, HD)), ("new_slc_prompt", (1, 1, SEQ, 2, KVH, HD)),
        ("new_win_prompt", (1, 1, WIN, 2, KVH, HD)), ("new_conv_prompt", (1, 1, CW - 1, CCH)),
        ("new_ssm_prompt", (1, 1, SH, HD, DS)),
        ("new_cmp_sample", (1, NB, NT, 2, KVH, HD)), ("new_slc_sample", (1, NB, NT, 2, KVH, HD)),
        ("new_win_sample", (1, NB, WIN, 2, KVH, HD)), ("new_conv_sample", (1, NB, CW - 1, CCH)),
        ("new_ssm_sample", (1, NB, SH, HD, DS))]


def kernel(**inputs):
    import concourse.bacc as bacc
    from concourse.bass_utils import run_bass_kernel_spmd

    nc = bacc.Bacc("TRN2", target_bir_lowering=False, num_devices=1)
    where, table = constants()
    arrays = {"in_" + n: np.ascontiguousarray(inputs[n]) for n in _IN}
    arrays["in_table"] = table
    A = {n[3:]: nc.dram_tensor(n, a.shape, mybir.dt.from_np(a.dtype), kind="ExternalInput").ap()
         for n, a in arrays.items()}
    O = {n: nc.dram_tensor("out_" + n, shape, F32, kind="ExternalOutput").ap() for n, shape in _OUT}
    gate_dram = nc.dram_tensor("gate_rows", (9, DM), F32).ap()
    out_dram = nc.dram_tensor("sample_heads", (NB, AH * NT, NBR * HD), F32).ap()
    build_layer(nc, A, O, where, table.shape[1], gate_dram, out_dram)
    r = run_bass_kernel_spmd(nc, [arrays], core_ids=[0])
    return tuple(r.results[0]["out_" + n] for n, _ in _OUT)
```

```python
import numpy as np
import concourse.bass as bass
from concourse import mybir
from contextlib import ExitStack

F32 = mybir.dt.float32
F32R = mybir.dt.float32r
BF16 = mybir.dt.bfloat16
I32 = mybir.dt.int32
U32 = mybir.dt.uint32
ALU = mybir.AluOpType
ACT = mybir.ActivationFunctionType
AX = mybir.AxisListType

DM = 1024
SEQ = 1024
NB, NT = 8, 8
SR = NB * NT
PAST, PAGE = 1024, 128
NPG = PAST // PAGE
NPOOL = 80
HD = 64
SH, SG = 8, 2
SW = SH * HD
DS = 128
CW = 4
CCH = SW + 2 * SG * DS
AH, KVH = 8, 2
GQ = AH // KVH
KVW = KVH * HD
CB, SB = 32, 64
WIN = 512
ROT = HD // 4
HR = ROT // 2
THETA = 500000.0
NBR = 3
EPS = 1e-6
NEG = -1.0e30
P = 128
KT8 = DM // P
TT = SEQ // P
NCB = SEQ // CB
TOK = SEQ + SR

C_ZS = 0
C_X = C_ZS + SW
C_DT = C_X + CCH
C_Q = C_DT + SH
C_KC = C_Q + AH * HD
C_KS = C_KC + 2 * KVW
C_KW = C_KS + 2 * KVW
C_G = C_KW + 2 * KVW
C_ZA = C_G + NBR * AH


def constants():
    f = np.float32
    p = np.arange(P)
    parts = {}
    parts["ident"] = np.eye(P, dtype=f)
    parts["tri"] = (p[:, None] <= p[None, :]).astype(f)
    parts["low"] = (p[:, None] > p[None, :]).astype(f)
    parts["caus"] = np.where(p[None, :] > p[:, None], f(NEG), f(0))
    parts["edge"] = np.where(p[None, :] < p[:, None], f(NEG), f(0))
    q = (np.arange(TT)[None, :, None] * P + p[:, None, None])
    cend = (np.arange(NCB) + 1) * CB - 1
    cm = (cend[None, None, :] <= q).astype(f)
    parts["cm"] = cm.reshape(P, TT * NCB)
    parts["blk"] = (p[:, None] // CB == np.arange(P // CB)[None, :]).astype(f) / f(CB)
    s = np.arange(P)
    same = (s[:, None] // NT == s[None, :] // NT) & (s[:, None] < SR) & (s[None, :] < SR)
    parts["tris"] = (same & (s[:, None] <= s[None, :])).astype(f)[:, :SR]
    parts["lows"] = (same & (s[:, None] > s[None, :])).astype(f)[:, :SR]
    parts["ind"] = ((s[:, None] // NT == np.arange(NB)[None, :]) & (s[:, None] < SR)).astype(f)
    b2, hh, tt = s // 64, (s // NT) % AH, s % NT
    tok = np.arange(SR)
    pairs = np.arange(NB // 2)
    own = (tok[None, None, :] // NT == 2 * pairs[None, :, None] + b2[:, None, None]) \
        & (tok[None, None, :] % NT <= tt[:, None, None])
    parts["nneg"] = np.where(own, f(0), f(NEG)).reshape(P, NB // 2 * SR)
    parts["wneg"] = np.where(np.arange(NT)[None, :] >= tt[:, None], f(0), f(NEG))
    c4 = np.arange(P)
    ownc = c4[None, None, :] // NCB == 2 * np.arange(2)[None, :, None] + b2[:, None, None]
    parts["sneg"] = np.where(ownc, f(0), f(NEG)).reshape(P, 2 * P)
    parts["gsum"] = ((b2[:, None] == b2[None, :]) & (tt[:, None] == tt[None, :])
                     & (hh[:, None] // GQ == hh[None, :] // GQ)).astype(f)
    parts["idx"] = np.broadcast_to(np.arange(1, PAST // SB + 1, dtype=f), (P, PAST // SB))
    dup = [p[:, None] == HD * k + p[None, :] % HD for k in range(KVH)]
    parts["dup"] = np.concatenate(dup, axis=1).astype(f)
    parts["ones"] = np.ones((P, P), f)
    inv = f(THETA) ** (-np.arange(HR, dtype=f) * f(2.0) / f(ROT))
    pos = np.zeros((P, TT + 1), f)
    pos[:, :TT] = (np.arange(TT)[None, :] * P + p[:, None])
    pos[:SR, TT] = PAST + tok % NT
    ang = (pos[:, :, None] * inv.astype(f)[None, None, :]).astype(f)
    parts["cos"] = np.cos(ang).astype(f).reshape(P, -1)
    parts["sin"] = np.sin(ang).astype(f).reshape(P, -1)
    parts["pcol"] = np.stack([p, p % (PAGE // CB)], axis=1).astype(f)
    at, out = 0, {}
    for k, v in parts.items():
        out[k] = (at, v.shape[1])
        at += v.shape[1]
    return out, np.ascontiguousarray(np.concatenate(list(parts.values()), axis=1).astype(f))


def build_layer(nc, A, O, where, ncols, gate_dram, out_dram):
    ctx = ExitStack()
    with ctx:
        base = {}

        def sb(name, cols, dt=F32):
            base[name] = nc.sbuf_base
            return ctx.enter_context(nc.sbuf_tensor(name, [P, cols], dt))

        def sem(name):
            return ctx.enter_context(nc.semaphore(name))

        consts = sb("consts", ncols)
        hT = sb("hT", KT8 * TOK)
        W = sb("W", 2 * KT8 * 512)
        U = sb("U", 8 * TOK)
        Y = sb("Y", 9 * 512)
        Q = sb("Q", 9 * 512)
        Vs = sb("Vs", 9 * KVW)
        Vw = sb("Vw", 9 * KVW)
        KTs = sb("KTs", SEQ)
        KTw = sb("KTw", SEQ)
        T = sb("T", 6144)
        small = sb("small", 1400)
        masks = sb("masks", 3 * P, BF16)
        cmpm = sb("cmpm", 2 * 2 * KVW)
        KcTs = sb("KcTs", 2 * P)
        KnT = sb("KnT", 2 * SR)
        KcT = sb("KcT", 5 * NCB)
        Vbd = sb("Vbd", KVH * GQ * HD)
        hst = sb("hst", SW)
        idx = sb("idx", 2 + NB * NPG, I32)
        pgt = sb("pgt", 2 + NB * NPG, I32)
        PS = ctx.enter_context(nc.psum_tensor("PS", [P, 8 * 512], F32))

        def const(name):
            a, n = where[name]
            return consts[:, a:a + n]

        ident = const("ident")
        cosT = const("cos").rearrange("p (i f) -> p i f", f=HR)
        sinT = const("sin").rearrange("p (i f) -> p i f", f=HR)
        take = [0]

        def sm(n):
            a = take[0]
            take[0] += n
            assert take[0] <= 1400
            return small[:, a:a + n]

        s1T = sm(8 * 9).rearrange("p (c r) -> p c r", r=9)
        shT = sm(8 * 9).rearrange("p (c r) -> p c r", r=9)
        vecT = sm(56)
        normT, mixgT = vecT[:, 0:8], vecT[:, 8:16]
        convw = vecT[:, 16:56].rearrange("p (k c) -> p k c", k=5)
        cT = sm(8 * 9)
        ss = sm(9)
        rms = sm(9)
        graw = sm(9 * 24).rearrange("p (i g) -> p i g", g=24)
        gtmp = sm(9 * 24).rearrange("p (i g) -> p i g", g=24)
        dtr = sm(9 * 8).rearrange("p (i g) -> p i g", g=8)
        dtv = sm(9 * 8).rearrange("p (i g) -> p i g", g=8)
        dte = sm(9 * 8).rearrange("p (i g) -> p i g", g=8)
        dtA = sm(9 * 8).rearrange("p (i g) -> p i g", g=8)
        abc = sm(8)
        dbias = sm(8)
        dskip = sm(8)
        st = sm(300)
        hT3 = hT[:, :].rearrange("p (k t) -> p k t", k=KT8)
        Wk = [W[:, n * 4096:(n + 1) * 4096].rearrange("p (k c) -> p k c", k=KT8) for n in range(2)]
        U3 = U[:, :].rearrange("p (c t) -> p c t", c=8)
        Q3 = Q[:, :].rearrange("p (i c) -> p i c", i=9)
        Y3 = Y[:, :].rearrange("p (i c) -> p i c", i=9)
        kvc3 = Y[:, 0:9 * 256].rearrange("p (i c) -> p i c", i=9)
        Vs3 = Vs[:, :].rearrange("p (i c) -> p i c", i=9)
        Vw3 = Vw[:, :].rearrange("p (i c) -> p i c", i=9)
        Ks3 = T[:, 0:1152].rearrange("p (i c) -> p i c", i=9)
        Kw3 = T[:, 1152:2304].rearrange("p (i c) -> p i c", i=9)
        identb, causb, edgeb = (masks[:, n * P:(n + 1) * P] for n in range(3))
        cmpm3 = cmpm[:, :].rearrange("p (h c) -> p h c", h=2)

        def bank(n, a=0, b=512):
            return PS[:, n * 512 + a:n * 512 + b]

        def rows(i):
            return P if i < TT else SR

        s_Bblk = sem('Bblk')
        s_Btok = sem('Btok')
        s_CmT = sem('CmT')
        s_act_chain = sem('act_chain')
        s_below = sem('below')
        s_bias_in = sem('bias_in')
        s_blocksum = sem('blocksum')
        s_cT = sem('cT')
        s_cTp = sem('cTp')
        s_c_in = sem('c_in')
        s_chunk_done = sem('chunk_done')
        s_chunk_ready = sem('chunk_ready')
        s_cm_zeroed = sem('cm_zeroed')
        s_cmasked = sem('cmasked')
        s_cmp_in = sem('cmp_in')
        s_cmp_values = sem('cmp_values')
        s_consts_in = sem('consts_in')
        s_conv = sem('conv')
        s_conv_silu = sem('conv_silu')
        s_conv_stored = sem('conv_stored')
        s_copied = sem('copied')
        s_csil = sem('csil')
        s_csum = sem('csum')
        s_dec = sem('dec')
        s_decay_cb = sem('decay_cb')
        s_doubled = sem('doubled')
        s_dsum = sem('dsum')
        s_dt = sem('dt')
        s_dtabs = sem('dtabs')
        s_dtexp = sem('dtexp')
        s_dtrep = sem('dtrep')
        s_dve_chain = sem('dve_chain')
        s_edec = sem('edec')
        s_empty_act = sem('empty_act')
        s_empty_dve = sem('empty_dve')
        s_eps = sem('eps')
        s_exp = sem('exp')
        s_fill = sem('fill')
        s_final = sem('final')
        s_froot = sem('froot')
        s_gate_bias_in = sem('gate_bias_in')
        s_gate_out = sem('gate_out')
        s_gate_s_in = sem('gate_s_in')
        s_gated = sem('gated')
        s_gates_in = sem('gates_in')
        s_group_sum = sem('group_sum')
        s_hT_act = sem('hT_act')
        s_hT_dve = sem('hT_dve')
        s_hT_smp = sem('hT_smp')
        s_hTs_act = sem('hTs_act')
        s_hTs_dve = sem('hTs_dve')
        s_heads_in = sem('heads_in')
        s_hout = sem('hout')
        s_hstT = sem('hstT')
        s_hstored = sem('hstored')
        s_idx = sem('idx')
        s_keys_out = sem('keys_out')
        s_keys_out_act = sem('keys_out_act')
        s_keys_turned = sem('keys_turned')
        s_kv_evac = sem('kv_evac')
        s_kv_evac_act = sem('kv_evac_act')
        s_kv_stored = sem('kv_stored')
        s_leading = sem('leading')
        s_max = sem('max')
        s_mod = sem('mod')
        s_modT = sem('modT')
        s_modTp = sem('modTp')
        s_mod_ok = sem('mod_ok')
        s_natT = sem('natT')
        s_nat_in = sem('nat_in')
        s_orow = sem('orow')
        s_ostored = sem('ostored')
        s_out = sem('out')
        s_pages = sem('pages')
        s_pages_in = sem('pages_in')
        s_pc_norm = sem('pc_norm')
        s_pool_chain = sem('pool_chain')
        s_proj = sem('proj')
        s_qlead = sem('qlead')
        s_rest = sem('rest')
        s_rms = sem('rms')
        s_root = sem('root')
        s_rope = sem('rope')
        s_scaled = sem('scaled')
        s_sconv_in = sem('sconv_in')
        s_scores = sem('scores')
        s_segl = sem('segl')
        s_silu = sem('silu')
        s_skip = sem('skip')
        s_small_T = sem('small_T')
        s_smp_cscores = sem('smp_cscores')
        s_smp_exp = sem('smp_exp')
        s_smp_gated = sem('smp_gated')
        s_smp_in = sem('smp_in')
        s_smp_max = sem('smp_max')
        s_smp_q = sem('smp_q')
        s_smp_q_turned = sem('smp_q_turned')
        s_smp_read = sem('smp_read')
        s_smp_scores = sem('smp_scores')
        s_smp_sum = sem('smp_sum')
        s_squared = sem('squared')
        s_squares = sem('squares')
        s_ssd_y = sem('ssd_y')
        s_state_added = sem('state_added')
        s_state_new = sem('state_new')
        s_states_stored = sem('states_stored')
        s_stored = sem('stored')
        s_summed = sem('summed')
        s_sums_exp = sem('sums_exp')
        s_tail = sem('tail')
        s_tailT = sem('tailT')
        s_taps = sem('taps')
        s_turned = sem('turned')
        s_turned_act = sem('turned_act')
        s_turned_dve = sem('turned_dve')
        s_values = sem('values')
        s_vec_in = sem('vec_in')
        s_wo_first_in = sem('wo_first_in')
        s_wo_in = sem('wo_in')
        s_wo_scaled = sem('wo_scaled')
        s_xT = sem('xT')
        s_xev_act = sem('xev_act')
        s_xev_dve = sem('xev_dve')
        s_xn = sem('xn')
        s_xproj = sem('xproj')
        s_xsT = sem('xsT')
        s_xtok = sem('xtok')
        s_xw = sem('xw')
        s_yroot = sem('yroot')
        s_ysq = sem('ysq')
        s_z_out = sem('z_out')
        s_zmul = sem('zmul')
        wload = [sem("wload0"), sem("wload1")]
        xin = [sem(f"xin{n}") for n in range(9)]
        xagain = [sem("xagain0"), sem("xagain1")]
        ystored = [sem("ystored0"), sem("ystored1")]
        ada = [[(0, 512, A["w_ada"][0][:, n * 512:(n + 1) * 512])] for n in range(6)]
        GROUPS = ada[0:4]
        w_in = A["w_in"][0]
        GROUPS += [[(0, 512, w_in[:, C_KC:C_KC + 512])],
                   [(0, 280, w_in[:, C_KW:C_KW + 280]), (280, 288, w_in[:, C_DT:C_DT + SH])],
                   [(0, 512, w_in[:, C_Q:C_Q + 512])],
                   [(0, 512, w_in[:, C_X:C_X + 512])],
                   [(0, 512, w_in[:, C_X + 512:C_X + 1024])]]
        GROUPS += ada[4:6]
        GROUPS += [[(0, 512, w_in[:, C_ZS:C_ZS + 512])],
                   [(0, 512, w_in[:, C_ZA:C_ZA + 512])]]
        G_KV, G_KW, G_Q, G_X, G_GATE, G_Z = 4, 5, 6, 7, 9, 11
        gate_rows = Y[0:9, 3328:4352]

        def arrived(eng, g):
            eng.wait_ge(wload[g % 2], 16 * sum(len(GROUPS[n]) for n in range(g % 2, g + 1, 2)))

        stores = {}

        def store(eng, dst, src, signal=s_stored, **kw):
            stores[signal.name] = (signal, stores.get(signal.name, (signal, 0))[1] + 16)
            eng.dma_start(dst, src, **kw).then_inc(signal, 16)

        def unit_parts(u):
            g, i, b = u // 9, u % 9, u % 4
            r = rows(i)
            dsts = {0: [(kvc3[0:r, i, :], 0, 256), (Ks3[0:r, i, :], 256, 384), (Vs3[0:r, i, :], 384, 512)],
                    1: [(Kw3[0:r, i, :], 0, 128), (Vw3[0:r, i, :], 128, 256), (graw[0:r, i, :], 256, 280),
                        (dtr[0:r, i, :], 280, 288)],
                    2: []}[g]
            parts = [(d, bank(b, x, y)[0:r]) for d, x, y in dsts]
            if g == 2:
                parts = [(Q3[0:r, i, :].rearrange("p (g k d) -> p k g d", g=GQ, k=KVH),
                          bank(b)[0:r].rearrange("p (k g d) -> p k g d", g=GQ, k=KVH))]
            return parts

        raw = [T[:, 3328 + 1115 * n:3328 + 1115 * (n + 1)] for n in range(2)]
        raw_s = [r[:, SEQ + 3:].rearrange("p (b t) -> p b t", t=NT + 3) for r in raw]
        tail = T[:, 5558:5774].rearrange("p (c t) -> p c t", c=8)
        scT = T[:, 5774:5966].rearrange("p (c b t) -> p c b t", c=8, t=3)
        taps = T[:, 5120:6144]
        sconv = Y[0:24, 2304:3328]

        segl = T[:, 0:1024].rearrange("p (h s) -> p h s", h=SH)
        decf = [T[:, 1024:2048], W[:, 4096:5120]]
        dec = [d.rearrange("p (h l) -> p h l", h=SH) for d in decf]
        xtok, xdt, xw, sk = ([T[:, a:a + 512], W[:, a + 3072:a + 3584]] for a in (2048, 2560, 3072, 3584))
        Btok, CBm = ([T[:, a:a + 256], W[:, a + 3072:a + 3328]] for a in (4096, 4352))
        yo = T[:, 4608:5120]
        segls = T[0:SR, 0:512].rearrange("p (h s) -> p h s", h=SH)
        decs = T[0:SR, 512:1024].rearrange("p (h l) -> p h l", h=SH)
        CmT = [T[:, 1024 + 512 * g:1600 + 512 * g] for g in range(SG)]
        Bblk = T[:, 0:2048].rearrange("p (g b n) -> p g b n", g=SG, b=NB)
        kvrep = xtok[0][0:SR]
        nat = W[:, 0:4096].rearrange("p (b c n) -> p b c n", b=NB, c=4)
        hTs = W[:, 4096:8192].rearrange("p (b c) -> p b c", b=NB)
        ex = [st[:, 8 + 24 * n:32 + 24 * n] for n in range(2)]
        edec = st[:, 64:96].rearrange("p (c b) -> p c b", c=4)

        pgs = U[:, 0:4096].rearrange("p (b j c) -> p b j c", b=2, j=NPG)
        pgw = U[:, 4096:6144].rearrange("p (b j c) -> p b j c", b=2, j=WIN // P)
        KTpair = U[:, 6144:8192].rearrange("p (b c) -> p b c", b=2)
        KTwpair = T[:, 0:1024].rearrange("p (b c) -> p b c", b=2)
        PP = T[:, 1024:2816]
        PPs, PPw, PPc = PP[:, 0:1088], PP[:, 1088:1664], PP[:, 1664:1792]
        PTs = T[:, 2816:4864].rearrange("p (n r) -> p n r", r=P)
        QS = T[:, 4864:5376].rearrange("p (b h t) -> p b h t", b=NB, h=AH)
        orow = T[:, 5376:5568].rearrange("p (n d) -> p n d", n=NBR)
        smax, snmax, ssum = st[:, 100:103], st[:, 103:106], st[:, 106:109]
        imp, least, cand, last, drop = (st[:, 110:126], st[:, 126:127], st[:, 128:142], st[:, 142:143], st[:, 144:160])

        Pb = [T[:, n * 1024:(n + 1) * 1024] for n in range(4)]
        def rounded(name, over, col, cols=1024):
            return nc.alloc_sbuf_tensor_at(name, [P, cols], F32R, offset=(base[over] + 31) // 32 * 32 + 4 * col)[:, :]

        QH = [rounded(f"QH{n}", "T", 4096 + 1024 * n).rearrange("p (h t) -> p h t", h=AH) for n in range(2)]
        QL = [rounded(f"QL{n}", over, 0).rearrange("p (h t) -> p h t", h=AH) for n, over in enumerate(("KTs", "KTw"))]
        K2 = {(k, kv): rounded(f"K2{k}{kv}", over, col) for k, kv, over, col in
              (("s", 0, "hT", 5632), ("s", 1, "hT", 6656), ("w", 0, "hT", 7680), ("w", 1, "W", 0))}
        Kc2 = rounded("Kc2", "KcT", NCB, 2 * NCB)
        K2_PARTS = [(K2[k, kv][:, h * 512:(h + 1) * 512], kv, K[:, h * 512:(h + 1) * 512])
                    for h in range(2) for k, K in (("s", KTs), ("w", KTw)) for kv in range(KVH)]
        PT = [W[:, 2048 + n * 512:2560 + n * 512] for n in range(4)]
        OT = hT[:, 5120:5632]
        spare = U[:, 8192:8704]
        zt = [T[:, 5568:6080], spare]
        za = W[:, 4096:8192].rearrange("p (i c) -> p i c", i=TT)
        Z_AHEAD = [range(4 * p, 4 * p + 3) for p in range(NB // 2)] + [range(16, 18)]
        Z_AMID = [4 * p + 3 for p in range(NB // 2)]

        def z_bank(u):
            return 2 if u % 4 == 1 else 7

        sneg_m = [st[:, 100 + 8 * n:108 + 8 * n] for n in range(2)]
        dsum = [st[:, 164 + 24 * n:188 + 24 * n].rearrange("p (n h) -> p n h", n=NBR) for n in range(2)]
        wgt = st[:, 212:220]
        cmax, cbias = st[:, 220:228], st[:, 228:260]

        UNITS, BUNDLES = [], []
        for i in range(TT):
            BUNDLES.append([len(UNITS)])
            UNITS.append((i, "c", 0, AH))
            for k, n in (("s", i + 1), ("w", min(i, WIN // P) + 1)):
                nh = {1: 8, 2: 4, 3: 2, 4: 2}.get(n, 1)
                for h in range(0, AH, max(nh, 2)):
                    BUNDLES.append([len(UNITS) + m for m in range(max(nh, 2) // nh)])
                    UNITS += [(i, k, h + m, nh) for m in range(max(nh, 2) // nh)]

        def keys(u):
            i, k, _, nh = UNITS[u]
            if k == "c":
                return 0, 2, 2 * P
            a = 0 if k == "s" else max(0, i - WIN // P)
            return a, i + 1 - a, 1024 // nh

        def blocks(bundle):
            us = BUNDLES[bundle]
            _, k, h0, nh = UNITS[us[0]]
            _, n, step = keys(us[0])
            if k == "c":
                return [(None, 0, 0, [(us[0], 0), (us[0], P)])]
            heads = range(h0, h0 + nh * len(us))
            out = []
            for kv in sorted({h // GQ for h in heads}):
                mine = [h for h in heads if h // GQ == kv]
                out += [(kv, t, mine[0], [(us[(h - h0) // nh], (h - h0) % nh * step + t * P) for h in mine]) for t in range(n)]
            return out

        TGROUPS, OF_BUNDLE = [], []
        for m in range(len(BUNDLES)):
            bl, first = blocks(m), len(TGROUPS)
            per = 4 // len(bl[0][3])
            TGROUPS += [(m, bl[x:x + per]) for x in range(0, len(bl), per)]
            OF_BUNDLE.append(range(first, len(TGROUPS)))

        def ends_branch(g):
            m = TGROUPS[g][0]
            u = BUNDLES[m][-1]
            return g == OF_BUNDLE[m][-1] and UNITS[u][2] + UNITS[u][3] == AH

        CGROUPS = [g for g, (m, _) in enumerate(TGROUPS) if UNITS[BUNDLES[m][0]][1] == "c"]

        def last_turn(u):
            return FILLS["T", OF_BUNDLE[next(m for m, us in enumerate(BUNDLES) if u in us)][-1]][0] + 1

        STEPS, CORE = [("QT", 0), ("S", 0)], [[] for _ in range(TT)]
        late = []

        def values(g):
            i, k = UNITS[BUNDLES[TGROUPS[g][0]][0]][0:2]
            at = [("V", g)]
            if ends_branch(g):
                at += [("SUM", i)] if k == "c" else [("COPY", 2 * i + (k == "w"))]
                late.extend([] if k == "c" else [("BACK", 2 * i + (k == "w"))])
            return at

        for m, us in enumerate(BUNDLES):
            i = UNITS[us[0]][0]
            ahead = BUNDLES[m + 1] if m + 1 < len(BUNDLES) else []
            ahead = [[("S", ahead[0])] if ahead else [], [("S", u) for u in ahead[1:]]]
            if UNITS[us[0]][1] == "w" and UNITS[us[0]][2] == 4 * (i > 0) and i < TT - 1:
                CORE[i].append(("QT", i + 1))
            CORE[i] += ahead[0]
            gs = OF_BUNDLE[m]
            for x, g in enumerate(gs):
                if x == (len(gs) + 1) // 2:
                    CORE[i] += ahead[1]
                CORE[i].append(("T", g))
                CORE[i] += late
                late.clear()
                if g >= 3:
                    CORE[i] += values(g - 3)
            if len(gs) < 2:
                CORE[i] += ahead[1]
        for g in range(len(TGROUPS) - 3, len(TGROUPS)):
            CORE[TT - 1] += values(g)
        CORE[TT - 1] += late

        MIX = [TT] + list(range(TT))
        OUTPUT = ("GATE", "SCALE", "TURN", "OUT", "RES", "SQUARE", "ROOT", "FINAL")

        def weave(core, fill):
            out, done = [], 0
            for n, step in enumerate(core):
                out.append(step)
                while done < (n + 1) * len(fill) // len(core):
                    what, m = (fill[done] or [("", 0)])[0]
                    if what == "GATE" and m > 0 and ("BACK", 2 * m - 1) not in out:
                        break
                    out += fill[done]
                    done += 1
            return out

        def out(m, n):
            return n * [("OUT", m)]

        for i in range(TT):
            before = [out(i - 1, 1), out(i - 1, 1)] if i > 1 else []
            fill = [[("GATE", i)] + out(i - 1, 2), [("RES", i - 1), ("SQUARE", i - 1)], [], [("SCALE", i)], [("FINAL", i - 2)] * (i > 1),
                    [("TURN", i)]] + 4 * [out(i, 1)] + [[], [("RES", i)]]
            if i == 0:
                fill = [[], [("GATE", 0)], [("SCALE", 0)], [("TURN", 0)]]
            if i == 1:
                fill = 4 * [out(0, 1)] + [[("RES", 0)]] + 2 * [out(0, 1)] + fill
            STEPS += CORE[i][:1] + sum(before, []) + weave(CORE[i][1:], fill)
        a, b = TT - 1, TT
        STEPS += out(a, 2) + [("GATE", b)] + out(a, 2) + [("RES", a), ("SQUARE", a), ("SCALE", b), ("FINAL", a - 1), ("TURN", b)]
        STEPS += out(b, 4) + [("ROOT", a), ("FINAL", a), ("RES", b)] + out(b, 4) + [("RES", b), ("SQUARE", b), ("ROOT", b), ("FINAL", b)]
        AGAIN, times = [], {}
        for step in STEPS:
            AGAIN.append(times.get(step, 0))
            times[step] = AGAIN[-1] + 1

        FILLS, OWNER, EMPTIED = {}, [], []
        for what, u in STEPS:
            for _ in range({"QT": 2, "T": 1, "BACK": 1, "TURN": 2}.get(what, 0)):
                FILLS.setdefault((what, u), []).append(len(OWNER))
                OWNER.append("dve" if what in ("BACK", "QT") or (what != "TURN" and len(OWNER) % 2) or (what == "TURN" and len(FILLS[what, u]) > 1)
                             else "act")
                EMPTIED.append(OWNER.count(OWNER[-1]))

        def turn_parts(what, u, n):
            b = bank(4 + FILLS[what, u][n] % 2)
            if what == "TURN":
                return [(mixT(MIX[u], n), b[:, 0:4 * rows(MIX[u])])]
            cols = P * sum(len(bl[3]) for bl in TGROUPS[u][1])
            return [(PT[u % 4][:, 0:cols], b[:, 0:cols])]

        xre = [hT[:, n * 1024:1024 + n * 1024] for n in range(2)]
        res = [hT[:, 2048 + n * 1024:3072 + n * 1024] for n in range(2)]
        gate_p, fin_g = hT[:, 4096:5120], W[:, DM:2 * DM]
        gate_s = [hst[0:SR, :], cmpm[0:SR, :]]

        def mixT(u, n):
            return (Y3, Q3)[n][:, u, 0:4 * rows(u)]

        ssq, fss, eps2 = st[:, 260:278], st[:, 280:289], st[:, 289:290]
        wo = U[:, 0:8192].rearrange("p (k c) -> p k c", k=8)
        smp = U[0:SR, 0:1536].rearrange("p (h n d) -> p h n d", h=AH, n=NBR)

        def heads(ap, r=P):
            return ap[0:r].rearrange("p (h d) -> p h d", d=HD)

        def over_d(ap, r=P):
            return ap[0:r].unsqueeze(2).broadcast_to([r, SH, HD])

        chains = {"dve": 0, "act": 0, "pool": 0}

        def after(eng, key, chain, ins):
            chains[key] += 1
            ins.then_inc(chain, 1)
            eng.wait_ge(chain, chains[key])

        block = ctx.enter_context(nc.Block())

        @block.gpsimd
        def _(pool):
            pool.dma_start(abc, A["a_log"][0].partition_broadcast(P)).then_inc(s_heads_in, 16)
            pool.dma_start(dbias, A["dt_bias"][0].partition_broadcast(P)).then_inc(s_heads_in, 16)
            pool.dma_start(dskip, A["d_skip"][0].partition_broadcast(P)).then_inc(s_heads_in, 16)
            ptab = A["page_table"]
            for h in range(2):
                src = ptab[4 * h:4 * h + 4, :].rearrange("b j -> (b j)").unsqueeze(1)
                pool.dma_start(pgt[:, h:h + 1], src.unsqueeze(1).broadcast_to([4 * NPG, P // CB, 1]),
                               allow_slow_non_contiguous=True).then_inc(s_pages_in, 16)
            pool.dma_start(pgt[:, 2:], ptab.rearrange("b j -> (b j)").partition_broadcast(P)).then_inc(s_pages_in, 16)

            for h in range(2):
                if h == 0:
                    pool.wait_ge(s_xT, 16)
                pool.wait_ge(s_idx, 2)
                if h == 1:
                    pool.wait_ge(s_blocksum, 6)
                pool.indirect_dma_start(U[:, 0:8192], None, A["cache_cmp_kv"][0].rearrange("n (j t) a h d -> (n j) (t a h d)", t=CB),
                                        bass.IndirectOffsetOnAxis(ap=idx[:, h:h + 1].bitcast(U32), axis=0)).then_inc(s_cmp_in, 16)
                pool.wait_ge(s_cmp_in, 16 * (h + 1))
                w = CB * 2 * KVW // 2
                step = 0
                while w >= 2 * KVW:
                    dst = U[:, 0:w] if w > 2 * KVW else cmpm3[:, h, :]
                    nc.gpsimd.tensor_tensor(dst, U[:, 0:w], U[:, w:2 * w], ALU.add).then_inc(s_blocksum, 1)
                    step += 1
                    pool.wait_ge(s_blocksum, 6 * h + step)
                    w //= 2
                nc.gpsimd.tensor_scalar(cmpm3[:, h, :], cmpm3[:, h, :], 1.0 / CB, None, ALU.mult).then_inc(s_blocksum, 1)
            for n, (name, K3, V3) in enumerate((("cmp", kvc3[:, :, 0:128], kvc3[:, :, 128:256]), ("slc", Ks3, Vs3), ("win", Kw3, Vw3))):
                pool.wait_ge(s_rope, n + 1)
                pool.wait_ge(s_kv_evac, (4, 4, 9)[n])
                pool.wait_ge(s_kv_evac_act, (5, 5, 9)[n])
                i0 = TT - WIN // P if name == "win" else 0
                for a, X3 in ((0, K3), (1, V3)):
                    dst = O[f"new_{name}_prompt"][0, 0].rearrange("(i p) a h d -> p i a (h d)", p=P)[:, :, a, :]
                    store(pool, dst, X3[:, i0:TT, :], s_kv_stored)
                    if name == "win":
                        store(pool, O["new_win_sample"][0][:, WIN - NT:, a].rearrange("b t h d -> b t (h d)"), X3[0:SR, TT, :], s_kv_stored)
                    else:
                        store(pool, O[f"new_{name}_sample"][0].rearrange("b t a h d -> (b t) a (h d)")[:, a, :], X3[0:SR, TT, :], s_kv_stored)
            store(pool, O["new_win_sample"][0][:, 0:WIN - NT].rearrange("b t a h d -> b (t a h d)"),
                  A["state_win_kv"][0][:, NT:].rearrange("b t a h d -> b (t a h d)"))
            for ct in range(8):
                pool.wait_ge(s_xev_act, ct + 1)
                pool.wait_ge(s_xev_dve, ct + 1)
                nc.gpsimd.tensor_copy(tail[:, ct, 0:3], raw[ct % 2][:, SEQ:SEQ + 3]).then_inc(s_tail, 1)
                nc.gpsimd.tensor_copy(tail[:, ct, 3:27].rearrange("p (b t) -> p b t", t=3), raw_s[ct % 2][:, :, NT:]).then_inc(s_tail, 1)
            pool.wait_ge(s_conv, 8)
            pool.wait_ge(s_rope, 4)
            pool.wait_ge(s_dt, 1)
            pool.wait_ge(s_kv_stored, 16 * 12)
            for i in range(TT + 1):
                r = rows(i)
                lo, seg = (const("low"), segl) if i < TT else (const("lows"), segls)
                k = r
                if i:
                    pool.wait_ge(s_chunk_ready, i)
                nc.gpsimd.tensor_tensor(seg, lo[0:r].unsqueeze(1).broadcast_to([r, SH, r]),
                                        dtA[0:r, i, :].unsqueeze(2).broadcast_to([r, SH, r]), ALU.mult).then_inc(s_segl, 1)
                if i == 0:
                    pool.wait_ge(s_taps, 2)
                    store(pool, O["new_conv_prompt"][0, 0], taps[0:3, :], s_conv_stored)
                    store(pool, O["new_conv_sample"][0].rearrange("b t c -> (b t) c"), taps[3:27, :], s_conv_stored)
                    pool.wait_ge(s_mod_ok, 6)
                    pool.dma_start(nat, A["state_ssm"][0].rearrange("b (c h) d n -> (h d) b c n", c=4)).then_inc(s_nat_in, 16)
                if i >= 2:
                    pool.wait_ge(s_chunk_done, i - 1)
                    pool.wait_ge(s_ssd_y, i - 1)
                pool.wait_ge(s_xtok, i + 1)
                n = i % 2
                nc.gpsimd.tensor_tensor(heads(xdt[n], r), heads(xtok[n], r), over_d(dtv[:, i, :], r), ALU.mult).then_inc(s_pool_chain, 1)
                nc.gpsimd.tensor_tensor(heads(sk[n], r), heads(xtok[n], r), over_d(dskip, r), ALU.mult).then_inc(s_skip, 1)
                pool.wait_ge(s_pool_chain, i + 1)
                pool.wait_ge(s_sums_exp, i + 1)
                nc.gpsimd.tensor_tensor(heads(xw[n], r), heads(xdt[n], r), over_d(ex[i % 2][:, 0:8], r), ALU.mult).then_inc(s_xw, 1)
            pool.wait_ge(s_skip, TT + 1)
            pool.wait_ge(s_xw, TT + 1)
            nc.gpsimd.tensor_copy(heads(kvrep, SR), over_d(dtA[:, TT, :], SR)).then_inc(s_dtrep, 1)
            pool.wait_ge(s_hout, 1)
            store(pool, O["new_ssm_prompt"][0, 0].rearrange("(c h) d n -> (h d) c n", c=4),
                  yo.rearrange("p (c n) -> p c n", c=4), s_hstored)
            cache_rows = A["cache_slc_kv"][0].rearrange("n t a h d -> (n t) (a h d)")

            def load_pages(p):
                for b in range(2):
                    for j in range(NPG):
                        c = 2 + (2 * p + b) * NPG + j
                        pool.indirect_dma_start(pgs[:, b, j, :], None, cache_rows,
                                                bass.IndirectOffsetOnAxis(ap=idx[:, c:c + 1].bitcast(U32), axis=0)).then_inc(s_pages, 16)
                    pool.dma_start(pgw[:, b], A["state_win_kv"][0][2 * p + b].rearrange("(j t) a h d -> t j (a h d)", t=P)).then_inc(s_pages, 16)

            pool.wait_ge(s_chunk_done, TT + 1)
            pool.wait_ge(s_CmT, 2)
            nc.gpsimd.memset(T[SR:, 0:2048], 0.0).then_inc(s_below, 1)
            nc.gpsimd.memset(xw[0][SR:], 0.0).then_inc(s_below, 1)
            load_pages(0)
            pool.wait_ge(s_state_added, 8)
            for b in range(2):
                store(pool, O["new_ssm_sample"][0].rearrange("b (c h) d n -> (h d) b c n", c=4)[:, 4 * b:4 * b + 4],
                      nat[:, 4 * b:4 * b + 4], s_states_stored)
            for p in range(1, NB // 2):
                pool.wait_ge(s_smp_sum, p)
                load_pages(p)
            for k in (2, 3, 4, 5, 6, 7, 0, 1):
                if k in (2, 0):
                    pool.wait_ge(s_wo_in if k == 2 else s_wo_first_in, 16)
                nc.gpsimd.tensor_scalar(wo[:, k, :], wo[:, k, :], mixgT[:, k:k + 1], None, ALU.mult).then_inc(s_wo_scaled, 1)

        @block.scalar
        def _(act):
            def alink(ins):
                after(act, "act", s_act_chain, ins)

            act.wait_ge(s_c_in, 32)
            act.activation(Y[0:9, 2048:3072], Y[0:9, 1024:2048], ACT.Silu).then_inc(s_csil, 1)
            for i in range(TT + 1):
                act.wait_ge(xin[i], 16)
                x = U[:, i * DM:(i + 1) * DM] if i < TT else Y[0:SR, 0:DM]
                if i:
                    act.wait_ge(s_squares, i)
                act.activation(Y[0:rows(i), 3072:4096], x, ACT.Square, accum_out=ss[0:rows(i), i:i + 1]).then_inc(s_squares, 1)
            act.wait_ge(s_squares, TT + 1)
            act.wait_ge(s_eps, 1)
            act.activation(rms[:, 0:TT], ss[:, 0:TT], ACT.Sqrt, scale=1.0 / DM, bias=st[:, 0:1]).then_inc(s_rms, 1)
            act.activation(rms[0:SR, TT:], ss[0:SR, TT:], ACT.Sqrt, scale=1.0 / DM, bias=st[0:SR, 0:1]).then_inc(s_rms, 1)
            act.wait_ge(s_modT, 2)
            for n in range(0, 16, 2):
                ct, half = n % 8, n // 8
                act.wait_ge(s_xT, n + 1)
                act.activation(hT3[:, ct, half * 512:half * 512 + 512], bank(2 + n % 4), ACT.Identity,
                               scale=s1T[:, ct, 0:1], bias=shT[:, ct, 0:1]).then_inc(s_hT_act, 1)
            act.wait_ge(s_modTp, 1)
            for u in range(0, 27, 2):
                act.wait_ge(s_proj, u + 1)
                parts = unit_parts(u)
                for n, (d, s) in enumerate(parts):
                    ins = act.activation(d, s, ACT.Copy)
                ins.then_inc(s_kv_evac_act, 1)
                if u == 22:
                    act.wait_ge(s_dtabs, 1)
                    act.activation(dte, dte, ACT.Exp, scale=-1.0).then_inc(s_dtexp, 1)
                    act.wait_ge(s_dtexp, 1)
                    act.activation(dte, dte, ACT.Ln, bias=1.0).then_inc(s_dtexp, 1)
                    act.activation(gtmp, graw, ACT.Exp, scale=-1.0).then_inc(s_dtexp, 1)
                    act.wait_ge(s_heads_in, 48)
                    act.activation(abc, abc, ACT.Exp).then_inc(s_dtexp, 1)
            for n, (b, d) in enumerate(((4, KTs[:, 0:512]), (6, KTw[:, 0:512]))):
                act.wait_ge(s_keys_turned, 2 * n + 1)
                act.activation(d, bank(b), ACT.Copy).then_inc(s_keys_out_act, 1)
            for ct in range(9):
                if ct < 8:
                    act.wait_ge(s_xproj, ct + 1)
                    if ct >= 2:
                        act.wait_ge(s_conv, ct - 1)
                        act.wait_ge(s_tail, 2 * (ct - 1))
                    act.activation(raw[ct % 2][:, 3:515], bank(2 * (ct % 2)), ACT.Copy).then_inc(s_xev_act, 1)
                if ct >= 1:
                    act.wait_ge(s_conv, ct)
                    act.activation(U3[:, ct - 1, :], U3[:, ct - 1, :], ACT.Silu).then_inc(s_conv_silu, 1)
            for i in range(TT + 1):
                r = rows(i)
                act.wait_ge(s_chunk_ready, i + 1)
                if i == 0:
                    act.wait_ge(s_kv_stored, 16 * 12)
                    act.wait_ge(s_conv, 8)
                    act.wait_ge(s_mod_ok, 6)
                if i >= 2:
                    act.wait_ge(s_xw, i - 1)
                    act.wait_ge(s_skip, i - 1)
                    act.wait_ge(s_ssd_y, i - 1)
                act.activation(xtok[i % 2][0:r], bank(0)[0:r], ACT.Copy).then_inc(s_xtok, 1)
                n = 24 if i < TT else 16
                act.activation(ex[i % 2][0:r, 0:n], bank(4, 0, n)[0:r], ACT.Exp).then_inc(s_sums_exp, 1)
                if i >= 2:
                    act.wait_ge(s_chunk_done, i - 1)
                if i < TT:
                    act.activation(decf[i % 2], PS[:, 1024:2048], ACT.Exp).then_inc(s_dec, 1)
                else:
                    act.activation(T[0:SR, 512:1024], bank(2)[0:SR], ACT.Exp).then_inc(s_dec, 1)
            for n in range(0, 8, 2):
                act.wait_ge(s_natT, n + 1)
                act.activation(hTs[:, n, :], bank(n), ACT.Copy).then_inc(s_hTs_act, 1)
            act.wait_ge(s_dsum, 1)
            act.activation(st[:, 64:96], bank(4, 0, 32), ACT.Exp).then_inc(s_edec, 1)
            act.wait_ge(s_state_new, 8)
            act.wait_ge(s_conv_stored, 32)
            act.wait_ge(s_hstored, 16)
            def z_silu(u):
                s, i = u // 9, u % 9
                r = rows(i)
                act.wait_ge(s_z_out, u + 1)
                if s == 0 and i >= 2:
                    act.wait_ge(s_ysq, u - 1)
                if u == 17:
                    act.wait_ge(s_ysq, 9)
                d = zt[u % 2][0:r] if s == 0 else za[:, i, :] if i < TT else spare[0:r]
                act.activation(d, bank(z_bank(u))[0:r], ACT.Silu).then_inc(s_silu, 1)

            def z_square(u):
                if u < 9:
                    r = rows(u)
                    act.wait_ge(s_zmul, u + 1)
                    act.activation(zt[u % 2][0:r], Y3[0:r, u, :], ACT.Square, accum_out=ssq[0:r, 2 * u:2 * u + 1]).then_inc(s_ysq, 1)

            for p in range(NB // 2):
                for u in Z_AHEAD[p]:
                    z_silu(u)
                    z_square(u)
                for n in (0, 2, 4):
                    act.wait_ge(s_turned, 10 * p + n + 1)
                    if p:
                        act.wait_ge(s_smp_scores, p)
                    d = KTpair[:, n // 2, 0:512] if n < 4 else KTwpair[:, 0, :]
                    act.activation(d, bank(4), ACT.Copy).then_inc(s_turned_act, 1)
                for n, X in ((0, PPc), (2, PPw), (1, PPs)):
                    act.wait_ge(s_smp_max, 3 * p + (0, 2, 1).index(n) + 1)
                    act.activation(X, X, ACT.Exp, bias=snmax[:, n:n + 1], accum_out=ssum[:, n:n + 1]).then_inc(s_smp_exp, 1)
                    if n == 1:
                        z_silu(Z_AMID[p])
                        act.wait_ge(s_turned, 10 * p + 7)
                        if p:
                            act.wait_ge(s_smp_sum, p)
                        act.activation(PTs[:, 8:12, :].rearrange("p n r -> p (n r)"), bank(4), ACT.Copy).then_inc(s_turned_act, 1)
                z_square(Z_AMID[p])
                act.wait_ge(s_turned, 10 * p + 9)
                act.activation(PTs[:, 0:4, :].rearrange("p n r -> p (n r)"), bank(4), ACT.Copy).then_inc(s_turned_act, 1)
            for u in Z_AHEAD[NB // 2]:
                z_silu(u)
            act.wait_ge(s_ysq, 9)
            q = ssq.rearrange("p (i s) -> p i s", s=2)[:, :, 0:1]
            for a, b, r in ((0, TT, P), (TT, TT + 1, SR)):
                act.activation(q[0:r, a:b], q[0:r, a:b], ACT.Sqrt, scale=1.0 / SW, bias=eps2[0:r]).then_inc(s_yroot, 1)
            act.wait_ge(s_smp_sum, 4)
            act.wait_ge(s_orow, 4)
            act.wait_ge(s_ostored, 64)
            for n, (d, _, _) in enumerate(K2_PARTS + [(Kc2, 0, 0)]):
                act.wait_ge(s_doubled, n + 1)
                act.activation(d, bank(n % 8, 0, d.shape[1]), ACT.Copy).then_inc(s_leading, 1)
            for (what, u), again in zip(STEPS, AGAIN):
                tile = MIX[u] if what in OUTPUT else None
                r = rows(tile) if what in OUTPUT else None
                if what == "GATE":
                    if u:
                        act.wait_ge(s_zmul, 9 + u)
                    q = ssq[0:r, 2 * tile + 1:2 * tile + 2]
                    squares = za[:, tile, :] if u else res[1][0:r, 0:SW]
                    alink(act.activation(squares, Q3[0:r, tile, :], ACT.Square, accum_out=q))
                    act.activation(q, q, ACT.Sqrt, scale=1.0 / SW, bias=eps2[0:r]).then_inc(s_root, 1)
                if what == "ROOT" or (what == "GATE" and u > 1):
                    v = u if what == "ROOT" else u - 2
                    act.wait_ge(s_squared, v + 1)
                    f = fss[0:rows(MIX[v]), v:v + 1]
                    act.activation(f, f, ACT.Sqrt, scale=1.0 / DM, bias=eps2[0:rows(MIX[v])]).then_inc(s_froot, 1)
                if what == "SQUARE":
                    act.wait_ge(s_summed, 2 * u + 2)
                    f = fss[0:r, u:u + 1]
                    act.activation(xre[u % 2][0:r], res[u % 2][0:r], ACT.Square, accum_out=f).then_inc(s_squared, 1)
                if what == "S":
                    i, k, h, nh = UNITS[u]
                    a, n, step = keys(u)
                    S = PS[:, u % 2 * 1024:u % 2 * 1024 + 1024]
                    act.wait_ge(s_max, u + 1)
                    if k == "c":
                        act.activation(Pb[u % 4][:, 0:step], Pb[u % 4][:, 0:step], ACT.Exp).then_inc(s_exp, 1)
                    else:
                        if u >= 4:
                            act.wait_ge(s_fill, last_turn(u - 4))
                        for m in range(nh):
                            ins = act.activation(Pb[u % 4][:, m * step:m * step + n * P], S[:, m * step:m * step + n * P], ACT.Exp,
                                                 bias=sneg_m[u % 2][:, m:m + 1], accum_out=dsum[i % 2][:, " sw".index(k), h + m:h + m + 1])
                        ins.then_inc(s_exp, 1)
                if what == "COPY":
                    i, k = u // 2, "sw"[u % 2]
                    act.wait_ge(s_values, [g for g in range(len(TGROUPS)) if ends_branch(g) and g not in CGROUPS][u] + 1)
                    if u:
                        act.wait_ge(s_fill, FILLS["BACK", u - 1][0] + 1)
                    act.activation(OT, bank(6), ACT.Copy).then_inc(s_copied, 1)
                for n, F in enumerate(FILLS.get((what, u), [])):
                    if what == "QT":
                        act.wait_ge(s_fill, F + 1)
                        act.activation(QH[u % 2][:, GQ * n:GQ * n + GQ, :], bank(4 + F % 2).rearrange("p (h t) -> p h t", h=GQ), ACT.Copy,
                                       scale=HD ** -0.5).then_inc(s_qlead, 1)
                    if OWNER[F] == "act":
                        act.wait_ge(s_fill, F + 1)
                        if what == "T" and u >= 4:
                            act.wait_ge(s_values, u - 3)
                        for d, s in turn_parts(what, u, n):
                            ins = act.activation(d, s, ACT.Copy)
                        ins.then_inc(s_empty_act, 1)

        @block.vector
        def _(dve):
            def link(ins):
                after(dve, "dve", s_dve_chain, ins)

            nc.vector.memset(st[:, 0:1], EPS).then_inc(s_eps, 1)
            dve.wait_ge(s_cTp, 1)
            link(nc.vector.tensor_copy(vecT, bank(7, 72, 128)))
            nc.vector.tensor_copy(cT, bank(7, 0, 72)).then_inc(s_cT, 1)
            dve.wait_ge(s_rms, 2)
            link(nc.vector.reciprocal(rms[:, 0:TT], rms[:, 0:TT]))
            link(nc.vector.reciprocal(rms[0:SR, TT:], rms[0:SR, TT:]))
            for i in range(TT + 1):
                x = U[:, i * DM:(i + 1) * DM] if i < TT else Y[0:SR, 0:DM]
                nc.vector.tensor_scalar(x, x, rms[0:rows(i), i:i + 1], None, ALU.mult).then_inc(s_xn, 1)
            dve.wait_ge(s_bias_in, 16)

            def mod_bias(g):
                dve.wait_ge(s_mod, g + 1)
                cols, bias = T[0:9, g * 512:(g + 1) * 512], T[0:9, 3072 + g * 512:3584 + g * 512]
                if g >= 4:
                    cols = bias = gate_rows[:, (g - 4) * 512:(g - 3) * 512]
                nc.vector.tensor_tensor(cols, bank(g % 2)[0:9, :], bias,
                                        ALU.add).then_inc(s_mod_ok, 1)

            for g in range(4):
                mod_bias(g)
            dve.wait_ge(s_modTp, 1)
            nc.vector.tensor_copy(shT, bank(6, 0, 72).rearrange("p (c r) -> p c r", r=9)).then_inc(s_modT, 1)
            nc.vector.scalar_tensor_tensor(s1T, bank(6, 72, 144).rearrange("p (c r) -> p c r", r=9), 1.0,
                                           normT.unsqueeze(2).broadcast_to([P, 8, 9]), ALU.add, ALU.mult).then_inc(s_modT, 1)
            dve.wait_ge(s_modT, 2)
            for n in range(1, 16, 2):
                ct, half = n % 8, n // 8
                dve.wait_ge(s_xT, n + 1)
                nc.vector.tensor_scalar(hT3[:, ct, half * 512:half * 512 + 512], bank(2 + n % 4),
                                        s1T[:, ct, 0:1], shT[:, ct, 0:1], ALU.mult, ALU.add).then_inc(s_hT_dve, 1)
            dve.wait_ge(s_xsT, 1)
            hs = hT3[:, :, SEQ:].rearrange("p k (b t) -> p k b t", t=NT)
            link(nc.vector.tensor_tensor(hs, bank(7).rearrange("p (k b t) -> p k b t", k=8, t=NT),
                                         s1T[:, :, 1:9].unsqueeze(3).broadcast_to([P, 8, NB, NT]), ALU.mult))
            nc.vector.tensor_tensor(hs, hs, shT[:, :, 1:9].unsqueeze(3).broadcast_to([P, 8, NB, NT]),
                                    ALU.add).then_inc(s_hT_smp, 1)
            dve.wait_ge(s_pages_in, 48)
            pcol = const("pcol")
            nc.vector.scalar_tensor_tensor(idx[:, 0:2], pgt[:, 0:2], float(PAGE // CB), pcol[:, 1:2].broadcast_to([P, 2]),
                                           ALU.mult, ALU.add).then_inc(s_idx, 1)
            nc.vector.scalar_tensor_tensor(idx[:, 2:], pgt[:, 2:], float(PAGE), pcol[:, 0:1].broadcast_to([P, NB * NPG]),
                                           ALU.mult, ALU.add).then_inc(s_idx, 1)
            for ap in (graw, dtr):
                nc.vector.memset(ap, 0.0)
            nc.vector.memset(Vbd[:, :], 0.0)
            nc.vector.memset(hst[:, :], 0.0)
            nc.vector.tensor_copy(identb, ident)
            nc.vector.tensor_copy(causb, const("caus"))
            link(nc.vector.tensor_copy(edgeb, const("edge")))

            def rope(X, i0, i1, r, heads):
                X4 = X[0:r, i0:i1, :].rearrange("p i (h d) -> p i h d", d=HD)
                x1, x2 = X4[:, :, :, 0:HR], X4[:, :, :, HR:ROT]
                shp = [r, i1 - i0, heads, HR]
                n = (i1 - i0) * heads * HR
                cos, sin = (t[0:r, i0:i1, :].unsqueeze(2).broadcast_to(shp) for t in (cosT, sinT))
                tmp = [T[0:r, 2304 + 256 * k:2304 + 256 * k + n].rearrange("p (i h d) -> p i h d", h=heads, d=HR) for k in range(4)]
                nc.vector.tensor_tensor(tmp[0], x1, cos, ALU.mult)
                nc.vector.tensor_tensor(tmp[1], x2, sin, ALU.mult)
                nc.vector.tensor_tensor(tmp[2], x2, cos, ALU.mult)
                link(nc.vector.tensor_tensor(tmp[3], x1, sin, ALU.mult))
                nc.vector.tensor_tensor(x1, tmp[0], tmp[1], ALU.subtract)
                return nc.vector.tensor_tensor(x2, tmp[2], tmp[3], ALU.add)

            roped = [0]

            def rope_all(X, heads):
                for i0 in range(0, TT, 4):
                    link(rope(X, i0, i0 + 4, P, heads))
                rope(X, TT, TT + 1, SR, heads).then_inc(s_rope, 1)
                roped[0] += 1
                dve.wait_ge(s_rope, roped[0])

            dve.wait_ge(s_modTp, 1)
            for u in range(1, 27, 2):
                dve.wait_ge(s_proj, u + 1)
                for d, s in unit_parts(u):
                    ins = nc.vector.tensor_copy(d, s)
                ins.then_inc(s_kv_evac, 1)
                if u == 11:
                    dve.wait_ge(s_kv_evac_act, 5)
                    dve.wait_ge(s_kv_evac, 6)
                    rope_all(kvc3[:, :, 0:128], KVH)
                    rope_all(Ks3, KVH)
                if u == 19:
                    dve.wait_ge(s_kv_evac_act, 9)
                    dve.wait_ge(s_kv_evac, 10)
                    rope_all(Kw3, KVH)
                    dve.wait_ge(s_heads_in, 48)
                    link(nc.vector.tensor_tensor(dtv, dtr, dbias.unsqueeze(1).broadcast_to([P, 9, SH]), ALU.add))
                    nc.vector.scalar_tensor_tensor(dte, dtv, -1.0, dtv, ALU.mult, ALU.max).then_inc(s_dtabs, 1)
                if u == 25:
                    dve.wait_ge(s_dtexp, 4)
                    link(nc.vector.scalar_tensor_tensor(dtv, dtv, 0.0, dte, ALU.max, ALU.add))
                    link(nc.vector.tensor_tensor(dtA, dtv, abc.unsqueeze(1).broadcast_to([P, 9, SH]), ALU.mult))
                    link(nc.vector.tensor_scalar(dtA, dtA, -1.0, None, ALU.mult))
                    link(nc.vector.tensor_scalar(gtmp, gtmp, 1.0, None, ALU.add))
                    nc.vector.reciprocal(gtmp, gtmp).then_inc(s_dt, 1)
            for n, (b, d) in enumerate(((5, KTs[:, 512:]), (7, KTw[:, 512:]))):
                dve.wait_ge(s_keys_turned, 2 * n + 2)
                nc.vector.tensor_copy(d, bank(b)).then_inc(s_keys_out, 1)
            dve.wait_ge(s_small_T, 1)
            nc.vector.tensor_copy(KnT[:, :], bank(4, 0, 128)).then_inc(s_keys_out, 1)
            nc.vector.tensor_copy(KcT[:, 0:NCB], bank(4, 128, 160))
            nc.vector.tensor_copy(KcT[:, NCB:].rearrange("p (h c) -> p h c", h=GQ),
                                  bank(4, 160, 192).unsqueeze(1).broadcast_to([P, GQ, NCB])).then_inc(s_keys_out, 1)
            nc.vector.tensor_copy(KcTs[:, :], bank(5, 0, 256)).then_inc(s_keys_out, 1)
            nc.vector.tensor_copy(scT, bank(5, 256, 448).rearrange("p (c b t) -> p c b t", c=8, t=3)).then_inc(s_keys_out, 1)
            dve.wait_ge(s_cmp_values, 1)
            Vbd4 = Vbd[:, :].rearrange("p (k h d) -> p k h d", k=KVH, h=GQ)
            for h in range(GQ):
                q = slice(32 * h, 32 * h + 32)
                ins = nc.vector.tensor_copy(Vbd4[q, :, h, :], bank(6, 0, 128)[q].rearrange("p (k d) -> p k d", k=KVH))
            ins.then_inc(s_keys_out, 1)
            dve.wait_ge(s_kv_evac_act, 14)
            dve.wait_ge(s_kv_evac, 13)
            rope_all(Q3, AH)
            dve.wait_ge(s_blocksum, 12)
            for n in range(2):
                nc.vector.memset(raw[n][:, 0:3], 0.0)
            for ct in range(8):
                r, rs = raw[ct % 2], raw_s[ct % 2]
                dve.wait_ge(s_xproj, ct + 1)
                if ct >= 2:
                    dve.wait_ge(s_tail, 2 * (ct - 1))
                nc.vector.tensor_copy(r[:, 515:SEQ + 3], bank(2 * (ct % 2) + 1))
                nc.vector.tensor_copy(rs[:, :, 0:3], scT[:, ct])
                nc.vector.tensor_copy(rs[:, :, 3:], bank(4 + ct % 2, 0, SR).rearrange("p (b t) -> p b t", t=NT)).then_inc(s_xev_dve, 1)
                dve.wait_ge(s_xev_act, ct + 1)
                dve.wait_ge(s_xev_dve, ct + 1)
                o, os_ = U3[:, ct, 0:SEQ], U3[:, ct, SEQ:].rearrange("p (b t) -> p b t", t=NT)
                nc.vector.tensor_scalar(o, r[:, 0:SEQ], convw[:, 0, ct:ct + 1], convw[:, 4, ct:ct + 1], ALU.mult, ALU.add)
                link(nc.vector.tensor_scalar(os_, rs[:, :, 0:NT], convw[:, 0, ct:ct + 1], convw[:, 4, ct:ct + 1], ALU.mult, ALU.add))
                for k in range(1, CW):
                    w = convw[:, k, ct:ct + 1]
                    nc.vector.scalar_tensor_tensor(o, r[:, k:k + SEQ], w, o, ALU.mult, ALU.add)
                    ins = nc.vector.scalar_tensor_tensor(os_, rs[:, :, k:k + NT], w, os_, ALU.mult, ALU.add)
                    if k < CW - 1:
                        link(ins)
                ins.then_inc(s_conv, 1)
            dve.wait_ge(s_gate_bias_in, 16)
            for g in range(4, 6):
                mod_bias(g)
            dve.wait_ge(s_tailT, 1)
            dve.wait_ge(s_conv, 8)
            for h in range(2):
                nc.vector.tensor_copy(taps[0:27, h * 512:(h + 1) * 512], bank(6 + h)[0:27]).then_inc(s_taps, 1)
            def ssd_masks(i):
                r = rows(i)
                tri, D, n = (const("tri"), dec[i % 2], P) if i < TT else (const("tris"), decs, SR)
                dve.wait_ge(s_chunk_ready, i + 1)
                if i == 0:
                    dve.wait_ge(s_gate_out, 16)
                    dve.wait_ge(s_kv_stored, 16 * 12)
                    dve.wait_ge(s_tail, 16)
                if i >= 2:
                    dve.wait_ge(s_chunk_done, i - 1)
                nc.vector.tensor_copy(Btok[i % 2][0:r], bank(1, 0, 256)[0:r]).then_inc(s_Btok, 1)
                cb3 = CBm[i % 2][0:r, 0:2 * n].rearrange("p (g l) -> p g l", g=SG)
                link(nc.vector.tensor_tensor(cb3, bank(1, 256, 256 + 2 * n)[0:r].rearrange("p (g l) -> p g l", g=SG),
                                             tri[0:r].unsqueeze(1).broadcast_to([r, SG, n]), ALU.mult))
                dve.wait_ge(s_dec, i + 1)
                for g in range(SG):
                    ins = nc.vector.tensor_tensor(D[:, 4 * g:4 * g + 4], D[:, 4 * g:4 * g + 4],
                                                  cb3[:, g].unsqueeze(1).broadcast_to([r, 4, n]), ALU.mult)
                ins.then_inc(s_decay_cb, 1)

            ssd_masks(0)
            for i in range(TT + 1):
                r, e = rows(i), ex[i % 2]
                if i < TT:
                    ssd_masks(i + 1)
                if i == TT:
                    nc.vector.memset(T[:, 1024:2048], 0.0).then_inc(s_cm_zeroed, 1)
                    dve.wait_ge(s_cm_zeroed, 1)
                    for g in range(SG):
                        nc.vector.tensor_copy(CmT[g].rearrange("p (b c) -> p b c", c=NT * (NB + 1))[:, :, 0:NT],
                                              U3[:, 6 + g, SEQ:].rearrange("p (b t) -> p b t", t=NT)).then_inc(s_CmT, 1)
                    for n in range(1, 8, 2):
                        dve.wait_ge(s_natT, n + 1)
                        nc.vector.tensor_copy(hTs[:, n, :], bank(n)).then_inc(s_hTs_dve, 1)
                dve.wait_ge(s_chunk_done, i + 1)
                dve.wait_ge(s_skip, i + 1)
                y = heads(Y3[0:r, i, :], r)
                if i:
                    nc.vector.tensor_tensor(heads(yo, r), heads(bank(6), r), over_d(e[:, 8:16], r), ALU.mult)
                link(nc.vector.tensor_tensor(y, heads(bank(5), r), heads(sk[i % 2], r), ALU.add))
                if i:
                    ins = nc.vector.tensor_tensor(y, y, heads(yo, r), ALU.add)
                if i < TT:
                    link(nc.vector.tensor_tensor(heads(hst), heads(hst), over_d(e[:, 16:24]), ALU.mult))
                    ins = nc.vector.tensor_tensor(hst[:, :], hst[:, :], bank(7), ALU.add)
                ins.then_inc(s_ssd_y, 1)
                dve.wait_ge(s_ssd_y, i + 1)
            dve.wait_ge(s_hstT, 1)
            nc.vector.tensor_copy(yo, bank(0)).then_inc(s_hout, 1)
            for g in range(SG):
                nc.vector.tensor_tensor(Bblk[0:SR, g], Btok[0][0:SR, g * P:(g + 1) * P].unsqueeze(1).broadcast_to([SR, NB, P]),
                                        const("ind")[0:SR].unsqueeze(2).broadcast_to([SR, NB, P]), ALU.mult).then_inc(s_Bblk, 1)
            dve.wait_ge(s_edec, 1)
            for m in range(8):
                c, h = m // 2, m % 2
                dve.wait_ge(s_state_new, m + 1)
                part = nat[:, 4 * h:4 * h + 4, c, :]
                link(nc.vector.tensor_tensor(part, part, edec[:, c, 4 * h:4 * h + 4].unsqueeze(2).broadcast_to([P, 4, P]), ALU.mult))
                nc.vector.tensor_tensor(part, part, bank(m).rearrange("p (b n) -> p b n", b=4), ALU.add).then_inc(s_state_added, 1)
            dve.wait_ge(s_state_new, 8)
            dve.wait_ge(s_conv_stored, 32)
            dve.wait_ge(s_hstored, 16)
            nc.vector.memset(eps2, EPS)
            link(nc.vector.memset(QS, 0.0))
            dve.wait_ge(s_smp_q_turned, 1)
            for k in range(KVH):
                q = slice(64 * k, 64 * k + 64)
                nc.vector.tensor_scalar(QS[q, :, GQ * k:GQ * k + GQ, :], bank(7, 0, 256)[q].rearrange("p (g b t) -> p b g t", g=GQ, t=NT),
                                        HD ** -0.5, None, ALU.mult).then_inc(s_smp_q, 1)
            nneg = const("nneg").rearrange("p (n c) -> p n c", n=NB // 2)
            sneg = const("sneg").rearrange("p (n c) -> p n c", n=2)
            link(nc.vector.memset(drop, 0.0))

            def row_max(n, X):
                link(nc.vector.reduce_max(smax[:, n:n + 1], X, AX.X))
                nc.vector.tensor_scalar(snmax[:, n:n + 1], smax[:, n:n + 1], -1.0, None, ALU.mult).then_inc(s_smp_max, 1)

            def z_mul(u):
                if u < 9:
                    y = Y3[0:rows(u), u, :]
                    dve.wait_ge(s_silu, u + 1)
                    nc.vector.tensor_tensor(y, y, zt[u % 2][0:rows(u)], ALU.mult).then_inc(s_zmul, 1)

            for p in range(NB // 2):
                for u in Z_AHEAD[p]:
                    z_mul(u)
                for n in (1, 3, 5):
                    dve.wait_ge(s_turned, 10 * p + n + 1)
                    if p:
                        dve.wait_ge(s_smp_scores, p)
                    d = KTpair[:, n // 2, 512:] if n < 4 else KTwpair[:, 1, :]
                    nc.vector.tensor_copy(d, bank(5)).then_inc(s_turned_dve, 1)
                dve.wait_ge(s_smp_cscores, p + 1)
                if p:
                    dve.wait_ge(s_turned, 10 * p)
                link(nc.vector.tensor_tensor(PPc, bank(3, 128, 256), sneg[:, p % 2, :], ALU.add))
                nc.vector.tensor_tensor(PPw[:, 512:], bank(3, 64, 128), nneg[:, p, :], ALU.add)
                nc.vector.tensor_tensor(PPs[:, PAST:], bank(3, 0, 64), nneg[:, p, :], ALU.add)
                row_max(0, PPc)
                dve.wait_ge(s_smp_exp, 3 * p + 1)
                link(nc.vector.reciprocal(ssum[:, 0:1], ssum[:, 0:1]))
                nc.vector.tensor_scalar(PPc, PPc, ssum[:, 0:1], None, ALU.mult).then_inc(s_pc_norm, 1)
                dve.wait_ge(s_smp_scores, p + 1)
                nc.vector.tensor_copy(PPw[:, NT:512], bank(2, NT, 512))
                link(nc.vector.tensor_tensor(PPw[:, 0:NT], bank(2, 0, NT), const("wneg"), ALU.add))
                row_max(2, PPw)
                dve.wait_ge(s_group_sum, p + 1)
                link(nc.vector.tensor_reduce(imp, bank(3, 256, 384).rearrange("p (s k two) -> p k s two", s=4, two=2), AX.XY, ALU.add))
                link(nc.vector.tensor_reduce(least, imp[:, 1:15], AX.X, ALU.min))
                link(nc.vector.scalar_tensor_tensor(cand, imp[:, 1:15], least, const("idx")[:, 1:15], ALU.is_equal, ALU.mult))
                link(nc.vector.reduce_max(last, cand, AX.X))
                link(nc.vector.tensor_scalar(drop[:, 1:15], const("idx")[:, 1:15], last, NEG, ALU.is_equal, ALU.mult))
                nc.vector.tensor_tensor(PPs[:, 0:PAST].rearrange("p (k s) -> p k s", s=SB), PS[:, 0:PAST].rearrange("p (k s) -> p k s", s=SB),
                                        drop.unsqueeze(2).broadcast_to([P, PAST // SB, SB]), ALU.add).then_inc(s_smp_read, 1)
                dve.wait_ge(s_smp_read, p + 1)
                row_max(1, PPs)
                dve.wait_ge(s_turned, 10 * p + 8)
                nc.vector.tensor_copy(PTs[:, 12, :], bank(5, 0, P))
                nc.vector.tensor_copy(PTs[0:SR, 14, :], bank(5, P, 2 * P)[0:SR]).then_inc(s_turned_dve, 1)
                z_mul(Z_AMID[p])
                dve.wait_ge(s_turned, 10 * p + 10)
                nc.vector.tensor_copy(PTs[0:SR, 13, :], bank(3, 384, 512)[0:SR])
                nc.vector.tensor_copy(PTs[:, 4:8].rearrange("p n r -> p (n r)"), bank(5)).then_inc(s_turned_dve, 1)
                dve.wait_ge(s_smp_exp, 3 * p + 3)
                nc.vector.memset(ssum[:, 0:1], 1.0)
                link(nc.vector.reciprocal(ssum[:, 1:3], ssum[:, 1:3]))
                dve.wait_ge(s_smp_sum, p + 1)
                if p:
                    dve.wait_ge(s_ostored, 16 * p)
                for n in range(4):
                    q, k = slice(32 * n, 32 * n + 32), n % 2
                    ins = nc.vector.tensor_tensor(orow[q], bank(6, 0, 384)[q].rearrange("p (n k d) -> p n k d", n=NBR, k=KVH)[:, :, k, :],
                                                  ssum[q].unsqueeze(2).broadcast_to([32, NBR, HD]), ALU.mult)
                ins.then_inc(s_orow, 1)
                dve.wait_ge(s_orow, p + 1)
            dve.wait_ge(s_smp_in, 16 * NB)
            link(nc.vector.tensor_tensor(smp, smp, gtmp[0:SR, TT, :].rearrange("p (n h) -> p h n", n=NBR).unsqueeze(3).broadcast_to([SR, AH, NBR, HD]),
                                         ALU.mult))
            osm = heads(Q3[0:SR, TT, :], SR)
            link(nc.vector.tensor_tensor(osm, smp[:, :, 0, :], smp[:, :, 1, :], ALU.add))
            link(nc.vector.tensor_tensor(osm, osm, smp[:, :, 2, :], ALU.add))
            dve.wait_ge(s_silu, 18)
            nc.vector.tensor_tensor(Q3[0:SR, TT, :], Q3[0:SR, TT, :], spare[0:SR], ALU.mult).then_inc(s_smp_gated, 1)
            for n, (d, _, _) in enumerate(K2_PARTS + [(Kc2, 0, 0)]):
                dve.wait_ge(s_leading, n + 1)
                low = d[64:128]
                nc.vector.tensor_tensor(low, bank(n % 8, 0, d.shape[1])[64:128], low.bitcast(F32), ALU.subtract).then_inc(s_rest, 1)
            dve.wait_ge(s_smp_gated, 1)
            cm = const("cm").rearrange("p (i c) -> p i c", i=TT)
            for (what, u), again in zip(STEPS, AGAIN):
                tile = MIX[u] if what in OUTPUT else None
                r = rows(tile) if what in OUTPUT else None
                if what == "GATE" and u:
                    nc.vector.tensor_tensor(Q3[:, tile, :], Q3[:, tile, :], za[:, tile, :], ALU.mult).then_inc(s_zmul, 1)
                if what == "RES":
                    dve.wait_ge(s_out, 2 * u + again + 1)
                    if u + again == 0:
                        dve.wait_ge(s_gate_s_in, 32)
                        dve.wait_ge(s_gates_in, 32)
                    if u >= 2 and again == 0:
                        dve.wait_ge(ystored[u % 2], 16 * (u // 2))
                    if again == 0:
                        dve.wait_ge(xagain[u % 2], 16 * (u // 2 + 1))
                    c = slice(512 * again, 512 * again + 512)
                    x = res[u % 2][0:r, c]
                    nc.vector.tensor_tensor(x, bank(7)[0:r], gate_p[:, c] if u else gate_s[again], ALU.mult).then_inc(s_gated, 1)
                    dve.wait_ge(s_gated, 2 * u + again + 1)
                    nc.vector.tensor_tensor(x, x, xre[u % 2][0:r, c], ALU.add).then_inc(s_summed, 1)
                if what == "SCALE":
                    dve.wait_ge(s_root, u + 1)
                    if u == 0:
                        dve.wait_ge(s_yroot, 2)
                    q = ssq[0:r, 2 * tile:2 * tile + 2]
                    link(nc.vector.reciprocal(q, q))
                    for s, M in enumerate((Y3, Q3)):
                        nc.vector.tensor_scalar(M[0:r, tile, :], M[0:r, tile, :], q[:, s:s + 1], None, ALU.mult).then_inc(s_scaled, 1)
                if what == "FINAL":
                    dve.wait_ge(s_froot, u + 1)
                    x = res[u % 2][0:r]
                    link(nc.vector.reciprocal(fss[0:r, u:u + 1], fss[0:r, u:u + 1]))
                    nc.vector.scalar_tensor_tensor(x, x, fss[0:r, u:u + 1], fin_g[0:r], ALU.mult, ALU.mult).then_inc(s_final, 1)
                if what == "S":
                    i, k, h, nh = UNITS[u]
                    a, n, step = keys(u)
                    S = PS[:, u % 2 * 1024:u % 2 * 1024 + 1024]
                    dve.wait_ge(s_scores, u + 1)
                    if k == "c":
                        C, S = Pb[u % 4][:, 0:step].rearrange("p (h c) -> p h c", h=AH), S[:, 0:step].rearrange("p (h c) -> p h c", h=AH)
                        if u >= 4:
                            dve.wait_ge(s_fill, last_turn(u - 4))
                        link(nc.vector.tensor_scalar(cbias, cm[:, i, :], -1.0, -NEG, ALU.add, ALU.mult))
                        link(nc.vector.tensor_tensor(C, S, cbias.unsqueeze(1).broadcast_to([P, AH, NCB]), ALU.add))
                        link(nc.vector.tensor_reduce(cmax, C, AX.X, ALU.max))
                        nc.vector.tensor_tensor(C, C, cmax.unsqueeze(2).broadcast_to([P, AH, NCB]), ALU.subtract).then_inc(s_max, 1)
                    else:
                        if u >= 2:
                            dve.wait_ge(s_exp, u - 1)
                        nc.vector.tensor_reduce(sneg_m[u % 2][:, 0:nh], S.rearrange("p (h s) -> p h s", h=nh)[:, :, 0:n * P], AX.X, ALU.max,
                                                negate=True).then_inc(s_max, 1)
                if what == "T" and u in CGROUPS:
                    c = BUNDLES[TGROUPS[u][0]][0]
                    i = UNITS[c][0]
                    C = Pb[c % 4][:, 0:256].rearrange("p (h c) -> p h c", h=AH)
                    dve.wait_ge(s_exp, c + 1)
                    link(nc.vector.tensor_tensor(C, C, cm[:, i, :].unsqueeze(1).broadcast_to([P, AH, NCB]), ALU.mult))
                    nc.vector.tensor_reduce(dsum[i % 2][:, 0, :], C, AX.X, ALU.add).then_inc(s_cmasked, 1)
                for n, F in enumerate(FILLS.get((what, u), [])):
                    if what == "QT":
                        dve.wait_ge(s_qlead, 2 * u + n + 1)
                        h = slice(GQ * n, GQ * n + GQ)
                        nc.vector.scalar_tensor_tensor(QL[u % 2][:, h, :], bank(4 + F % 2).rearrange("p (h t) -> p h t", h=GQ), HD ** -0.5,
                                                       QH[u % 2][:, h, :].bitcast(F32), ALU.mult, ALU.subtract).then_inc(s_empty_dve, 1)
                    elif OWNER[F] == "dve" and what != "BACK":
                        dve.wait_ge(s_fill, F + 1)
                        if what == "T" and u >= 4:
                            dve.wait_ge(s_values, u - 3)
                        for d, s in turn_parts(what, u, n):
                            ins = nc.vector.tensor_copy(d, s)
                        ins.then_inc(s_empty_dve, 1)
                if what in ("SUM", "BACK"):
                    i, n = (u, 0) if what == "SUM" else (u // 2, 1 + u % 2)
                    d = dsum[i % 2][:, n, :]
                    link(nc.vector.tensor_scalar(wgt, d, 1e-30, None, ALU.max))
                    link(nc.vector.reciprocal(wgt, wgt))
                    link(nc.vector.tensor_tensor(wgt, wgt, gtmp[:, i, n * AH:(n + 1) * AH], ALU.mult))
                    o = Q3[:, i, :]
                    if what == "SUM":
                        dve.wait_ge(s_values, CGROUPS[i] + 1)
                        nc.vector.tensor_tensor(heads(o), heads(bank(6)), over_d(wgt), ALU.mult).then_inc(s_csum, 1)
                        dve.wait_ge(s_csum, i + 1)
                    else:
                        F = FILLS[what, u][0]
                        dve.wait_ge(s_fill, F + 1)
                        back = bank(4 + F % 2).rearrange("p (g k d) -> p k g d", g=GQ, k=KVH)
                        w = wgt.rearrange("p (k g) -> p k g", k=KVH).unsqueeze(3).broadcast_to([P, KVH, GQ, HD])
                        nc.vector.tensor_tensor(spare.rearrange("p (k g d) -> p k g d", k=KVH, g=GQ), back, w, ALU.mult).then_inc(s_empty_dve, 1)
                        dve.wait_ge(s_empty_dve, EMPTIED[F])
                        link(nc.vector.tensor_tensor(o, o, spare, ALU.add))

        @block.tensor
        def _(pe):
            pe.wait_ge(s_csil, 1)
            pe.wait_ge(s_consts_in, 16)
            pe.wait_ge(s_vec_in, 5 * 16)
            nc.tensor.transpose(bank(7, 72, 128), Y[0:56, 4096:4224], ident[0:56, 0:56])
            for c in range(KT8):
                ins = nc.tensor.transpose(bank(7, c * 9, c * 9 + 9), Y[0:9, 2048 + c * P:2048 + (c + 1) * P], ident[0:9, 0:9])
            ins.then_inc(s_cTp, 1)
            pe.wait_ge(s_cT, 1)

            def mod_group(g):
                at = g if g < 4 else G_GATE + g - 4
                arrived(pe, at)
                if g >= 2:
                    pe.wait_ge(s_mod_ok, g - 1)
                for k in range(KT8):
                    ins = nc.tensor.matmul(bank(g % 2)[0:9, :], cT[:, k * 9:k * 9 + 9], Wk[at % 2][:, k, :],
                                           start=(k == 0), stop=(k == KT8 - 1))
                    if k == KT8 - 1:
                        ins.then_inc(s_mod, 1)

            for g in range(4):
                mod_group(g)
            pe.wait_ge(s_mod_ok, 4)
            for c in range(16):
                ins = nc.tensor.transpose(bank(6, c * 9, c * 9 + 9), T[0:9, c * P:(c + 1) * P], ident[0:9, 0:9])
            ins.then_inc(s_modTp, 1)
            pe.wait_ge(s_xn, TT + 1)
            for n in range(16):
                ct, half = n % 8, n // 8
                if n >= 4:
                    pe.wait_ge((s_hT_act, s_hT_dve)[n % 2], (n - 4) // 2 + 1)
                for j in range(4):
                    i = 4 * half + j
                    ins = nc.tensor.transpose(bank(2 + n % 4, j * P, j * P + P), U[:, i * DM + ct * P:i * DM + ct * P + P], ident)
                ins.then_inc(s_xT, 1)
            for ct in range(8):
                ins = nc.tensor.transpose(bank(7, ct * SR, ct * SR + SR), Y[0:SR, ct * P:(ct + 1) * P], ident[0:SR, 0:SR])
            ins.then_inc(s_xsT, 1)

            pe.wait_ge(s_hT_act, 8)
            pe.wait_ge(s_hT_dve, 8)
            pe.wait_ge(s_hT_smp, 1)
            pe.wait_ge(s_mod_ok, 4)
            UCOLS = (512, 288, 512)
            for u in range(27):
                g, i = u // 9, u % 9
                if i == 0:
                    arrived(pe, G_KV + g)
                if u >= 4:
                    pe.wait_ge((s_kv_evac_act, s_kv_evac)[u % 2], (u - 4) // 2 + 1)
                for k in range(KT8):
                    ins = nc.tensor.matmul(bank(u % 4, 0, UCOLS[g])[0:rows(i)], hT3[:, k, i * P:i * P + rows(i)],
                                           Wk[(G_KV + g) % 2][:, k, 0:UCOLS[g]], start=(k == 0), stop=(k == KT8 - 1))
                ins.then_inc(s_proj, 1)
            pe.wait_ge(s_rope, 3)
            for n, K3 in enumerate((Ks3, Kw3)):
                for i in range(TT):
                    ins = nc.tensor.transpose(bank(4 + 2 * n + i // 4, i % 4 * P, i % 4 * P + P), K3[:, i, :], ident)
                    if i % 4 == 3:
                        ins.then_inc(s_keys_turned, 1)
            pe.wait_ge(s_keys_out_act, 2)
            pe.wait_ge(s_keys_out, 2)
            pe.wait_ge(s_kv_evac, 13)
            for n, K3 in enumerate((Ks3, Kw3)):
                nc.tensor.transpose(bank(4, n * SR, (n + 1) * SR), K3[0:SR, TT, :], ident[0:SR, 0:SR])
            for i in range(TT):
                for a in range(2):
                    nc.tensor.matmul(bank(4, 128 + a * 32 + 4 * i, 132 + a * 32 + 4 * i), kvc3[:, i, a * P:(a + 1) * P], const("blk"),
                                     start=True, stop=True)
            pe.wait_ge(s_blocksum, 12)
            for h in range(2):
                nc.tensor.transpose(bank(5, h * P, (h + 1) * P), cmpm3[:, h, 0:P], ident)
            pe.wait_ge(s_sconv_in, 16)
            for ct in range(8):
                ins = nc.tensor.transpose(bank(5, 256 + ct * 24, 280 + ct * 24), sconv[:, ct * P:(ct + 1) * P], ident[0:24, 0:24])
            ins.then_inc(s_small_T, 1)
            pe.wait_ge(s_keys_out, 6)
            nc.tensor.matmul(bank(6, 0, P), KcT[:, NCB:], ident, start=True, stop=True).then_inc(s_cmp_values, 1)
            pe.wait_ge(s_kv_evac_act, 14)
            for ct in range(8):
                if ct % 4 == 0:
                    arrived(pe, G_X + ct // 4)
                if ct >= 2:
                    pe.wait_ge(s_xev_act, ct - 1)
                    pe.wait_ge(s_xev_dve, ct - 1)
                w = Wk[(G_X + ct // 4) % 2]
                for b, a, n in ((2 * (ct % 2), 0, 512), (2 * (ct % 2) + 1, 512, 512), (4 + ct % 2, SEQ, SR)):
                    for k in range(KT8):
                        ins = nc.tensor.matmul(bank(b, 0, n), w[:, k, ct % 4 * P:ct % 4 * P + P], hT3[:, k, a:a + n],
                                               start=(k == 0), stop=(k == KT8 - 1))
                ins.then_inc(s_xproj, 1)
            pe.wait_ge(s_xev_act, 7)
            pe.wait_ge(s_xev_dve, 7)
            for g in range(4, 6):
                mod_group(g)
            pe.wait_ge(s_tail, 16)
            pe.wait_ge(s_keys_out, 7)
            for ct in range(8):
                ins = nc.tensor.transpose(bank(6 + ct // 4, ct % 4 * P, ct % 4 * P + P)[0:27], tail[:, ct, :], ident)
            ins.then_inc(s_tailT, 1)

            def ssd_A(i):
                r = rows(i)
                t = slice(i * P, i * P + r)
                if i == 0:
                    pe.wait_ge(s_conv_silu, 8)
                    pe.wait_ge(s_mod_ok, 6)
                    pe.wait_ge(s_taps, 2)
                    pe.wait_ge(s_keys_out, 7)
                    pe.wait_ge(s_dt, 1)
                else:
                    pe.wait_ge(s_xtok, i)
                    pe.wait_ge(s_decay_cb, i)
                    pe.wait_ge(s_sums_exp, i)
                    pe.wait_ge(s_dec, i)
                for c in range(6):
                    nc.tensor.transpose(bank(c // 4, c % 4 * P, c % 4 * P + P)[0:r], U3[:, c, t], ident)
                for g in range(SG):
                    nc.tensor.matmul(bank(1, 256 + g * r, 256 + (g + 1) * r)[0:r], U3[:, 4 + g, t], U3[:, 6 + g, t],
                                     start=True, stop=True)
                lo, tr = (const("low"), const("tri")) if i < TT else (const("lows"), const("tris"))
                for n, m in enumerate((lo, tr, const("ones"))[0:3 if i < TT else 2]):
                    nc.tensor.matmul(bank(4, 8 * n, 8 * n + 8)[0:r], m[0:r], dtA[0:r, i, :], start=True, stop=True)
                pe.wait_ge(s_segl, i + 1)
                for h in range(SH):
                    s = segl[:, h, :] if i < TT else segls[:, h, :]
                    o = bank(2 + h // 4, h % 4 * P, h % 4 * P + P) if i < TT else bank(2, h * SR, (h + 1) * SR)[0:SR]
                    ins = nc.tensor.matmul(o, s, tr[0:r], start=True, stop=True)
                ins.then_inc(s_chunk_ready, 1)

            def ssd_B(i):
                r = rows(i)
                if i:
                    pe.wait_ge(s_ssd_y, i)
                if 0 < i < TT:
                    for g in range(SG):
                        nc.tensor.matmul(bank(6, g * 256, (g + 1) * 256), U3[:, 6 + g, i * P:(i + 1) * P],
                                         hst[:, g * 256:(g + 1) * 256], start=True, stop=True)
                if i == TT:
                    pe.wait_ge(s_hTs_act, 4)
                    pe.wait_ge(s_hTs_dve, 4)
                    pe.wait_ge(s_CmT, 2)
                    for g in range(SG):
                        for b in range(NB):
                            nc.tensor.matmul(bank(6, g * 256, (g + 1) * 256)[0:SR], CmT[g][:, b * SR:(b + 1) * SR],
                                             hTs[:, b, g * 256:(g + 1) * 256], start=(b == 0), stop=(b == NB - 1))
                pe.wait_ge(s_decay_cb, i + 1)
                pe.wait_ge(s_xw, i + 1)
                n = i % 2
                D = dec[n] if i < TT else decs
                for h in range(SH):
                    ins = nc.tensor.matmul(bank(5, h * HD, (h + 1) * HD)[0:r], D[:, h, :], xdt[n][0:r, h * HD:(h + 1) * HD],
                                           start=True, stop=True)
                pe.wait_ge(s_Btok, i + 1)
                if i < TT:
                    for g in range(SG):
                        ins = nc.tensor.matmul(bank(7, g * 256, (g + 1) * 256), Btok[n][:, g * P:(g + 1) * P],
                                               xw[n][:, g * 256:(g + 1) * 256], start=True, stop=True)
                ins.then_inc(s_chunk_done, 1)

            ssd_A(0)
            for i in range(TT):
                ssd_A(i + 1)
                ssd_B(i)
            pe.wait_ge(s_nat_in, 16)
            pe.wait_ge(s_xtok, 9)
            pe.wait_ge(s_sums_exp, 9)
            pe.wait_ge(s_dec, 9)
            pe.wait_ge(s_decay_cb, 9)
            pe.wait_ge(s_ssd_y, 8)
            for b in range(NB):
                for c in range(4):
                    ins = nc.tensor.transpose(bank(b, c * P, (c + 1) * P), nat[:, b, c, :], ident)
                ins.then_inc(s_natT, 1)
            ssd_B(TT)
            for c in range(4):
                ins = nc.tensor.transpose(bank(0, c * P, (c + 1) * P), hst[:, c * P:(c + 1) * P], ident)
            ins.then_inc(s_hstT, 1)
            pe.wait_ge(s_dtrep, 1)
            for c in range(4):
                ins = nc.tensor.matmul(bank(4, c * 8, c * 8 + 8), kvrep[:, c * P:(c + 1) * P], const("ind")[0:SR], start=True, stop=True)
            ins.then_inc(s_dsum, 1)
            pe.wait_ge(s_Bblk, 2)
            pe.wait_ge(s_below, 2)
            pe.wait_ge(s_hout, 1)
            pe.wait_ge(s_ssd_y, 9)
            pe.wait_ge(s_edec, 1)
            for m in range(8):
                c, h = m // 2, m % 2
                nc.tensor.matmul(bank(m), xw[0][:, c * P:(c + 1) * P],
                                 Bblk[:, c // 2, 4 * h:4 * h + 4, :].rearrange("p b n -> p (b n)"), start=True, stop=True).then_inc(s_state_new, 1)

            pe.wait_ge(s_rope, 4)
            pe.wait_ge(s_state_added, 8)
            for g in range(GQ):
                ins = nc.tensor.transpose(bank(7, g * SR, (g + 1) * SR), Q3[0:SR, TT, g * P:(g + 1) * P], ident[0:SR, 0:SR])
            ins.then_inc(s_smp_q_turned, 1)

            def turn(G, parts):
                if G >= 2:
                    pe.wait_ge((s_turned_act, s_turned_dve)[G % 2], (G - 2) // 2 + 1)
                for a, src in parts:
                    n = src.shape[1]
                    ins = nc.tensor.transpose(bank(4 + G % 2, a, a + P)[0:n], src, ident)
                ins.then_inc(s_turned, 1)

            def z_unit(u):
                s, i = u // 9, u % 9
                if i == 0:
                    arrived(pe, G_Z + s)
                if u:
                    pe.wait_ge(s_silu, u - (u % 4 in (1, 2)))
                for k in range(KT8):
                    ins = nc.tensor.matmul(bank(z_bank(u))[0:rows(i)], hT3[:, k, i * P:i * P + rows(i)], Wk[(G_Z + s) % 2][:, k, :],
                                           start=(k == 0), stop=(k == KT8 - 1))
                ins.then_inc(s_z_out, 1)

            pe.wait_ge(s_smp_q, 2)
            for p in range(NB // 2):
                for u in Z_AHEAD[p]:
                    z_unit(u)
                pe.wait_ge(s_pages, 288 * (p + 1))
                for n in range(6):
                    src = pgs[:, n // 2, 4 * (n % 2):4 * (n % 2) + 4] if n < 4 else pgw[:, n - 4]
                    turn(10 * p + n, [(j * P, src[:, j, 0:P]) for j in range(4)])
                pe.wait_ge(s_turned_act, 5 * p + 3)
                pe.wait_ge(s_turned_dve, 5 * p + 3)
                if p:
                    pe.wait_ge(s_smp_read, p)
                pe.wait_ge(s_silu, 4 * p + 2)
                queries = [QS[:, 2 * p + b].rearrange("p h t -> p (h t)") for b in range(2)]
                for b in range(2):
                    for o, rhs in ((bank(3, 128, 256), KcTs[:, p // 2 * P:(p // 2 + 1) * P]), (bank(3, 0, 64), KnT[:, 0:SR]),
                                   (bank(3, 64, 128), KnT[:, SR:])):
                        ins = nc.tensor.matmul(o[64 * b:64 * b + 64], queries[b], rhs, start=True, stop=True)
                ins.then_inc(s_smp_cscores, 1)
                for b in range(2):
                    q, lhsT = slice(64 * b, 64 * b + 64), queries[b]
                    for o, rhs in ((bank(2), KTwpair[:, b, :]),
                                   (bank(0), KTpair[:, b, 0:512]), (bank(1), KTpair[:, b, 512:])):
                        ins = nc.tensor.matmul(o[q], lhsT, rhs, start=True, stop=True)
                ins.then_inc(s_smp_scores, 1)
                pe.wait_ge(s_pc_norm, p + 1)
                nc.tensor.matmul(bank(3, 256, 384), const("gsum"), PPc, start=True, stop=True).then_inc(s_group_sum, 1)
                z_unit(Z_AMID[p])
                pe.wait_ge(s_smp_exp, 3 * p + 2)
                turn(10 * p + 6, [(j * P, PPw[:, j * P:(j + 1) * P]) for j in range(4)])
                turn(10 * p + 7, [(0, PPc), (P, PPw[:, 512:])])
                pe.wait_ge(s_turned_act, 5 * p + 4)
                pe.wait_ge(s_turned_dve, 5 * p + 4)
                if p:
                    pe.wait_ge(s_orow, p)
                nc.tensor.matmul(bank(6, 0, P), PTs[:, 12, :], cmpm3[:, p // 2, P:], start=True, stop=True)
                for o, t0, vals, nt, tn, Vn in ((bank(6, 2 * P, 3 * P), 8, pgw, WIN // P, 14, Vw3), (bank(6, P, 2 * P), 0, pgs, NPG, 13, Vs3)):
                    if t0 == 0:
                        pe.wait_ge(s_smp_exp, 3 * p + 3)
                        for n in range(2):
                            if n == 1:
                                nc.tensor.transpose(bank(3, 384, 512)[0:SR], PPs[:, PAST:], ident)
                            turn(10 * p + 8 + n, [(j * P, PPs[:, (4 * n + j) * P:(4 * n + j + 1) * P]) for j in range(4)])
                        pe.wait_ge(s_turned_act, 5 * p + 5)
                        pe.wait_ge(s_turned_dve, 5 * p + 5)
                    for b in range(2):
                        q = slice(64 * b, 64 * b + 64)
                        for t in range(nt):
                            nc.tensor.matmul(o[q], PTs[:, t0 + t, q], vals[:, b, t, P:], start=(t == 0), stop=False)
                        ins = nc.tensor.matmul(o[q], PTs[0:SR, tn, q], Vn[0:SR, TT, :], start=False, stop=True)
                ins.then_inc(s_smp_sum, 1)
            for u in Z_AHEAD[NB // 2]:
                z_unit(u)

            pe.wait_ge(s_orow, 4)
            pe.wait_ge(s_silu, 18)
            for n, (_, kv, K) in enumerate(K2_PARTS):
                nc.tensor.matmul(bank(n), const("dup")[:, kv * P:(kv + 1) * P], K, start=True, stop=True).then_inc(s_doubled, 1)
            pe.wait_ge(s_rest, 1)
            for kv in range(KVH):
                ins = nc.tensor.matmul(bank(0, kv * NCB, (kv + 1) * NCB), const("dup")[:, kv * P:(kv + 1) * P], KcT[:, 0:NCB], start=True, stop=True)
            ins.then_inc(s_doubled, 1)
            pe.wait_ge(s_rest, 6)

            def emptied(F):
                if F >= 0:
                    pe.wait_ge({"act": s_empty_act, "dve": s_empty_dve}[OWNER[F]], EMPTIED[F])

            for (what, u), again in zip(STEPS, AGAIN):
                if what in ("GATE", "SCALE", "RES", "SQUARE", "ROOT", "FINAL", "SUM", "COPY"):
                    continue
                tile = MIX[u] if what in OUTPUT else None
                r = rows(tile) if what in OUTPUT else None
                if what == "TURN":
                    pe.wait_ge(s_scaled, 2 * u + 2)
                    for n, F in enumerate(FILLS[what, u]):
                        emptied(F - 2)
                        for c in range(4):
                            ins = nc.tensor.transpose(bank(4 + F % 2, c * r, (c + 1) * r), (Y3, Q3)[n][0:r, tile, c * P:(c + 1) * P],
                                                      ident[0:r, 0:r])
                        ins.then_inc(s_fill, 1)
                    continue
                if what == "OUT":
                    half, n = again // 4, again % 4
                    if again == 0:
                        pe.wait_ge(s_wo_scaled, KT8) if u == 0 else None
                        for F in FILLS["TURN", u]:
                            emptied(F)
                    if n == 0 and u + half:
                        pe.wait_ge(s_gated, 2 * u + half)
                    for k in range(2 * n, 2 * n + 2):
                        ins = nc.tensor.matmul(bank(7)[0:r], mixT(tile, k // 4)[:, k % 4 * r:(k % 4 + 1) * r], wo[:, k, half * 512:(half + 1) * 512],
                                               start=(k == 0), stop=(k == KT8 - 1))
                    if n == 3:
                        ins.then_inc(s_out, 1)
                    continue
                if what == "QT":
                    for kv, F in enumerate(FILLS[what, u]):
                        emptied(F - 2)
                        for g in range(GQ):
                            q, to = Q3[:, u, g * P + kv * HD:g * P + (kv + 1) * HD], bank(4 + F % 2, g * P, (g + 1) * P)
                            nc.tensor.transpose(to[0:64], q, ident)
                            ins = nc.tensor.matmul(to[64:128], q, ident, start=True, stop=True)
                        ins.then_inc(s_fill, 1)
                elif what == "S":
                    i, k, h, nh = UNITS[u]
                    a, n, step = keys(u)
                    if u == 0:
                        pe.wait_ge(s_rest, len(K2_PARTS) + 1)
                    if k == "c":
                        emptied(FILLS["QT", i][1])
                    if u >= 2:
                        pe.wait_ge(s_exp, u - 1)
                    base = u % 2 * 1024
                    if k == "c":
                        for hh in range(AH):
                            for n, q in enumerate((QH, QL)):
                                ins = nc.tensor.matmul(PS[:, base + hh * NCB:base + (hh + 1) * NCB], q[i % 2][:, hh, :],
                                                       Kc2[:, hh // GQ * NCB:(hh // GQ + 1) * NCB], start=(n == 0), stop=(n == 1))
                    else:
                        for hh in range(h, h + nh):
                            K = K2[k, hh // GQ]
                            for t in range(0, n, 4):
                                m = min(4, n - t)
                                edge = k == "w" and t == 0 and i >= WIN // P
                                last = t + m == n
                                for x, q in enumerate((QH, QL)):
                                    ins = nc.tensor.matmul(PS[:, base + t * P:base + (t + m) * P], q[i % 2][:, hh, :],
                                                           K[:, (a + t) * P:(a + t + m) * P], start=(x == 0), stop=x == 1 and not (edge or last))
                                if edge:
                                    ins = nc.tensor.matmul(PS[:, base:base + P], identb, edgeb, start=False, stop=not last)
                                if last:
                                    ins = nc.tensor.matmul(PS[:, base + (n - 1) * P:base + n * P], identb, causb, start=False, stop=True)
                            base += step
                    ins.then_inc(s_scores, 1)
                elif what == "T":
                    F = FILLS[what, u][0]
                    m, bl = TGROUPS[u]
                    pe.wait_ge(s_exp, BUNDLES[m][-1] + 1)
                    if u in CGROUPS:
                        pe.wait_ge(s_cmasked, CGROUPS.index(u) + 1)
                    emptied(F - 2)
                    for n, (unit, c) in enumerate(x for b in bl for x in b[3]):
                        ins = nc.tensor.transpose(bank(4 + F % 2, n * P, (n + 1) * P), Pb[unit % 4][:, c:c + P], ident)
                    ins.then_inc(s_fill, 1)
                elif what == "V":
                    m, bl = TGROUPS[u]
                    i, k = UNITS[BUNDLES[m][0]][0:2]
                    a, n, _ = keys(BUNDLES[m][0])
                    emptied(FILLS["T", u][0])
                    if k == "c" and i:
                        pe.wait_ge(s_copied, 2 * i)
                    if k == "s" and u - 1 in CGROUPS:
                        pe.wait_ge(s_csum, i + 1)
                    if k == "w" and ends_branch(u - 1):
                        pe.wait_ge(s_copied, 2 * i + 1)
                    if k == "c":
                        for kk in range(KVH):
                            ins = nc.tensor.matmul(bank(6, kk * 256, (kk + 1) * 256), PT[u % 4][:, kk * P:(kk + 1) * P],
                                                   Vbd[:, kk * 256:(kk + 1) * 256], start=True, stop=True)
                    else:
                        V3, at = Vs3 if k == "s" else Vw3, 0
                        for kv, t, h0, where_h in bl:
                            w, c = len(where_h) * P, h0 % GQ * P
                            ins = nc.tensor.matmul(bank(6, c, c + w)[64 * kv:64 * kv + 64], V3[:, a + t, kv * HD:(kv + 1) * HD],
                                                   PT[u % 4][:, at:at + w], start=(t == 0), stop=(t == n - 1))
                            at += w
                    ins.then_inc(s_values, 1)
                elif what == "BACK":
                    F = FILLS[what, u][0]
                    pe.wait_ge(s_copied, u + 1)
                    emptied(F - 2)
                    for g in range(GQ):
                        ins = nc.tensor.transpose(bank(4 + F % 2, g * P, (g + 1) * P), OT[:, g * P:(g + 1) * P], ident)
                    ins.then_inc(s_fill, 1)


        @block.sync
        def _(sp):
            sp.dma_start(Y[0:1, 1024:2048], A["c_prompt"]).then_inc(s_c_in, 16)
            sp.dma_start(Y[1:9, 1024:2048], A["c_sample"]).then_inc(s_c_in, 16)
            vec = Y[:, 4096:4224]
            for r, n, src in ((0, 8, A["norm_g"]), (8, 4, A["ssd_norm_g"]), (12, 4, A["att_norm_g"]),
                              (16, 32, A["conv_w"].rearrange("l k c -> l (k c)")), (48, 8, A["conv_b"])):
                sp.dma_start(vec[r:r + n, :], src[0].rearrange("(c p) -> c p", p=P)).then_inc(s_vec_in, 16)
            sp.dma_start(consts[:, :], A["table"]).then_inc(s_consts_in, 16)
            for i in range(TT):
                sp.dma_start(U[:, i * DM:(i + 1) * DM], A["x_prompt"][0][i * P:(i + 1) * P, :]).then_inc(xin[i], 16)
            sp.dma_start(Y[0:SR, 0:DM], A["x_sample"].rearrange("b t c -> (b t) c")).then_inc(xin[TT], 16)
            sp.dma_start(T[0:9, 3072:5120], A["b_ada"][0, 0:2 * DM].partition_broadcast(9)).then_inc(s_bias_in, 16)
            USED = {g: (s_mod, g + 1) for g in range(4)} | {G_GATE: (s_mod, 5), G_GATE + 1: (s_mod, 6)}
            USED |= {g: (s_proj, 9 * (g - G_KV + 1)) for g in (G_KV, G_KW, G_Q)}
            USED |= {g: (s_xproj, 4 * (g - G_X + 1)) for g in (G_X, G_X + 1)}
            for g in range(len(GROUPS)):
                if g >= 2:
                    sp.wait_ge(*USED[g - 2])
                if g == G_Z:
                    sp.wait_ge(s_chunk_done, TT + 1)
                    sp.wait_ge(s_ssd_y, TT)
                if g == G_Z + 1:
                    sp.wait_ge(s_states_stored, 32)
                for a, b, src in GROUPS[g]:
                    sp.dma_start(Wk[g % 2][:, :, a:b], src.rearrange("(k p) c -> p k c", p=P)).then_inc(wload[g % 2], 16)
                if g == G_KW:
                    sp.wait_ge(s_hT_smp, 1)
                    sp.dma_start(gate_rows, A["b_ada"][0, 2 * DM:].partition_broadcast(9)).then_inc(s_gate_bias_in, 16)
                    sp.dma_start(sconv, A["state_conv"][0].rearrange("b t c -> (b t) c")).then_inc(s_sconv_in, 16)
                if g == G_GATE + 1:
                    sp.wait_ge(s_mod_ok, 6)
                    sp.dma_start(gate_dram, gate_rows).then_inc(s_gate_out, 16)
            for p in range(NB // 2):
                sp.wait_ge(s_orow, p + 1)
                sp.dma_start(out_dram[2 * p:2 * p + 2].rearrange("b r c -> (b r) c"), orow.rearrange("p n d -> p (n d)")).then_inc(s_ostored, 16)
            sp.wait_ge(s_ostored, 64)
            sp.wait_ge(s_smp_sum, 4)
            for b in range(NB):
                sp.dma_start(smp[b * NT:(b + 1) * NT], out_dram[b].rearrange("(h t) (n d) -> t h n d", t=NT, n=NBR)).then_inc(s_smp_in, 16)
            w_out_rows = A["w_out"][0].rearrange("(k p) c -> p k c", p=P)
            sp.dma_start(wo[:, 2:], w_out_rows[:, 2:]).then_inc(s_wo_in, 16)
            sp.wait_ge(s_smp_gated, 1)
            sp.dma_start(wo[:, 0:2], w_out_rows[:, 0:2]).then_inc(s_wo_first_in, 16)
            sp.wait_ge(s_silu, 18)
            sp.wait_ge(s_gate_out, 16)
            x_rows = [A["x_prompt"][0][i * P:(i + 1) * P, :] for i in range(TT)] + [A["x_sample"].rearrange("b t c -> (b t) c")]
            y_rows = [O["y_prompt"][0][i * P:(i + 1) * P, :] for i in range(TT)] + [O["y_sample"].rearrange("b t c -> (b t) c")]
            for n in range(2):
                sp.dma_start(xre[n][0:rows(MIX[n])], x_rows[MIX[n]]).then_inc(xagain[n], 16)
            for c in range(2):
                sp.dma_start(gate_s[c], gate_dram[1:9, c * 512:(c + 1) * 512].unsqueeze(1).broadcast_to([NB, NT, 512])).then_inc(s_gate_s_in, 16)
            sp.dma_start(gate_p, gate_dram[0].partition_broadcast(P)).then_inc(s_gates_in, 16)
            sp.dma_start(fin_g, A["final_g"].partition_broadcast(P)).then_inc(s_gates_in, 16)
            for n, tile in enumerate(MIX):
                sp.wait_ge(s_squared, n + 1)
                if n + 2 <= TT:
                    sp.dma_start(xre[n % 2], x_rows[MIX[n + 2]]).then_inc(xagain[n % 2], 16)
                sp.wait_ge(s_final, n + 1)
                store(sp, y_rows[tile], res[n % 2][0:rows(tile)], ystored[n % 2])
            for signal, count in stores.values():
                sp.wait_ge(signal, count)


_IN = ['x_prompt', 'x_sample', 'cache_cmp_kv', 'cache_slc_kv', 'state_win_kv', 'state_conv', 'state_ssm',
       'page_table', 'c_prompt', 'c_sample', 'w_ada', 'b_ada', 'norm_g', 'w_in', 'conv_w', 'conv_b',
       'dt_bias', 'a_log', 'd_skip', 'ssd_norm_g', 'att_norm_g', 'w_out', 'final_g']
_OUT = [("y_prompt", (1, SEQ, DM)), ("y_sample", (NB, NT, DM)),
        ("new_cmp_prompt", (1, 1, SEQ, 2, KVH, HD)), ("new_slc_prompt", (1, 1, SEQ, 2, KVH, HD)),
        ("new_win_prompt", (1, 1, WIN, 2, KVH, HD)), ("new_conv_prompt", (1, 1, CW - 1, CCH)),
        ("new_ssm_prompt", (1, 1, SH, HD, DS)),
        ("new_cmp_sample", (1, NB, NT, 2, KVH, HD)), ("new_slc_sample", (1, NB, NT, 2, KVH, HD)),
        ("new_win_sample", (1, NB, WIN, 2, KVH, HD)), ("new_conv_sample", (1, NB, CW - 1, CCH)),
        ("new_ssm_sample", (1, NB, SH, HD, DS))]


def kernel(**inputs):
    import concourse.bacc as bacc
    from concourse.bass_utils import run_bass_kernel_spmd

    nc = bacc.Bacc("TRN2", target_bir_lowering=False, num_devices=1)
    where, table = constants()
    arrays = {"in_" + n: np.ascontiguousarray(inputs[n]) for n in _IN}
    arrays["in_table"] = table
    A = {n[3:]: nc.dram_tensor(n, a.shape, mybir.dt.from_np(a.dtype), kind="ExternalInput").ap()
         for n, a in arrays.items()}
    O = {n: nc.dram_tensor("out_" + n, shape, F32, kind="ExternalOutput").ap() for n, shape in _OUT}
    gate_dram = nc.dram_tensor("gate_rows", (9, DM), F32).ap()
    out_dram = nc.dram_tensor("sample_heads", (NB, AH * NT, NBR * HD), F32).ap()
    build_layer(nc, A, O, where, table.shape[1], gate_dram, out_dram)
    r = run_bass_kernel_spmd(nc, [arrays], core_ids=[0])
    return tuple(r.results[0]["out_" + n] for n, _ in _OUT)
```
